# Optimizing a Trainium2 kernel written in Bass

```python
import jax, jax.numpy as jnp
from jax import lax
import numpy as np

D_MODEL = 1024
BATCH = 1
SEQ = 128
DEPTH = 2
DEC_BATCH = 1
DEC_SEQ = 512
PAST_LEN = 128

GRID_W = 64
MLA_HEADS = 8
Q_LORA = 384
KV_LORA = 256
QK_NOPE = 64
QK_ROPE = 32
V_HEAD = 64
MLA_W = MLA_HEADS * V_HEAD
SOFTMAX_SCALE = (QK_NOPE + QK_ROPE) ** -0.5
ROPE_BASE = 10000.0
Q_BLOCK = 128
CONV_W = 256
CONV_K = 31
GMLP_W = 256
GMLP_GROUPS = 4
GMLP_CHUNK = 128
POOL_W = 256
POOL_WINDOWS = (2, 4, 8, 16)
POOL_GROUPS = 4
N_BRANCH = 4
D_FF = 2816
FFN_K = 3
NORM_EPS = 1e-6
OFF_KV = Q_LORA
OFF_CONV = OFF_KV + KV_LORA + QK_ROPE
OFF_GMLP = OFF_CONV + 2 * CONV_W
OFF_POOL = OFF_GMLP + 2 * GMLP_W
OFF_GATE = OFF_POOL + POOL_W
D_IN = OFF_GATE + N_BRANCH * D_MODEL

kernel_name = "hybrid_diffusion_parallel_mla_conv_gmlp_pool_step"

def rmsnorm(x, g):
    xf = x.astype(jnp.float32)
    y = xf * lax.rsqrt(jnp.mean(xf * xf, axis=-1, keepdims=True) + NORM_EPS)
    return (y * g.astype(jnp.float32)).astype(x.dtype)

def layernorm(x, g, b):
    xf = x.astype(jnp.float32)
    mu = jnp.mean(xf, axis=-1, keepdims=True)
    var = jnp.mean(jnp.square(xf - mu), axis=-1, keepdims=True)
    y = (xf - mu) * lax.rsqrt(var + NORM_EPS)
    return (y * g.astype(jnp.float32) + b.astype(jnp.float32)).astype(x.dtype)

def depthwise_conv(x, w, b):
    C = x.shape[-1]
    y = lax.conv_general_dilated(x, w[:, None, :].astype(x.dtype), window_strides=(1,), padding='SAME',
                                 dimension_numbers=('NWC', 'WIO', 'NWC'), feature_group_count=C)
    return y + b

def grid_positions(L):
    rows = L // GRID_W
    row = jnp.repeat(jnp.arange(rows), GRID_W)
    col = jnp.tile(jnp.arange(GRID_W), rows)
    return row, col

def rope_1d(x, pos):
    half = x.shape[-1] // 2
    inv = ROPE_BASE ** (-jnp.arange(half, dtype=jnp.float32) / half)
    ang = pos.astype(jnp.float32)[:, None] * inv[None, :]
    cos = jnp.cos(ang)[None, :, None, :].astype(x.dtype)
    sin = jnp.sin(ang)[None, :, None, :].astype(x.dtype)
    x1, x2 = x[..., :half], x[..., half:]
    return jnp.concatenate([x1 * cos - x2 * sin, x1 * sin + x2 * cos], axis=-1)

def axial_rope(x, row, col):
    r = x.shape[-1] // 2
    return jnp.concatenate([rope_1d(x[..., :r], row), rope_1d(x[..., r:], col)], axis=-1)

def kv_expand(c_kv, w_kv_b):
    B, L, _ = c_kv.shape
    kv = (c_kv @ w_kv_b).reshape(B, L, MLA_HEADS, QK_NOPE + V_HEAD)
    return kv[..., :QK_NOPE], kv[..., QK_NOPE:]

def blocked_attention(q_nope, q_pe_parts, k_nope, k_pe_parts, v):
    B, L, H, _ = q_nope.shape
    nb = L // Q_BLOCK

    def to_blocks(t):
        return jnp.moveaxis(t.reshape((B, nb, Q_BLOCK) + t.shape[2:]), 1, 0)

    def one_block(qs):
        qn, qpes = qs
        s_pe = jnp.concatenate([jnp.einsum('bqhr,bkr->bhqk', qp, kp) for qp, kp in zip(qpes, k_pe_parts)], axis=-1)
        s = jnp.einsum('bqhd,bkhd->bhqk', qn, k_nope) + s_pe
        p = jax.nn.softmax(s.astype(jnp.float32), axis=-1).astype(v.dtype)
        return jnp.einsum('bhqk,bkhd->bqhd', p, v)

    out = lax.map(one_block, (to_blocks(q_nope), tuple(to_blocks(t) for t in q_pe_parts)))
    return jnp.moveaxis(out, 0, 1).reshape(B, L, H, v.shape[-1])

def centred_mean_minus_self(x, w):
    L = x.shape[1]
    lo = w // 2
    hi = w - lo - 1
    xf = x.astype(jnp.float32)
    cs = jnp.concatenate([jnp.zeros_like(xf[:, :1]), jnp.cumsum(xf, axis=1)], axis=1)
    t = jnp.arange(L)
    end = jnp.minimum(t + hi + 1, L)
    start = jnp.maximum(t - lo, 0)
    cnt = (end - start).astype(jnp.float32)[None, :, None]
    mean = (jnp.take(cs, end, axis=1) - jnp.take(cs, start, axis=1)) / cnt
    return (mean - xf).astype(x.dtype)

def token_mixing(h, lp, row, col, ctx):
    B, L, _ = h.shape
    proj = h @ lp['w_in']
    q_a = proj[..., :OFF_KV]
    kv_a = proj[..., OFF_KV:OFF_CONV]
    conv_in = proj[..., OFF_CONV:OFF_GMLP]
    gmlp_in = proj[..., OFF_GMLP:OFF_POOL]
    pool_in = proj[..., OFF_POOL:OFF_GATE]
    gate_logits = proj[..., OFF_GATE:]

    q = (rmsnorm(q_a, lp['q_norm_g']) @ lp['w_q_b']).reshape(B, L, MLA_HEADS, QK_NOPE + QK_ROPE) * SOFTMAX_SCALE
    q_nope, q_pe = q[..., :QK_NOPE], q[..., QK_NOPE:]
    c_kv = rmsnorm(kv_a[..., :KV_LORA], lp['kv_norm_g'])
    k_pe = kv_a[..., KV_LORA:]
    kn, vv = kv_expand(c_kv, lp['w_kv_b'])
    if ctx is None:
        attn = blocked_attention(q_nope, (q_pe,), kn, (k_pe,), vv)
    else:
        ctx_ckv, ctx_kpe = ctx
        kn_c, v_c = kv_expand(ctx_ckv, lp['w_kv_b'])
        q_pe_rot = axial_rope(q_pe, row, col)
        k_pe_rot = axial_rope(k_pe[:, :, None, :], row, col)[:, :, 0, :]
        attn = blocked_attention(q_nope, (q_pe_rot, q_pe), jnp.concatenate([kn, kn_c], axis=1),
                                 (k_pe_rot, ctx_kpe), jnp.concatenate([vv, v_c], axis=1))
    branch_a = attn.reshape(B, L, MLA_W) @ lp['w_o_mla']

    a = conv_in[..., :CONV_W] * jax.nn.sigmoid(conv_in[..., CONV_W:])
    a = depthwise_conv(a, lp['conv_dw'], lp['conv_dw_b'])
    a = jax.nn.silu(layernorm(a, lp['conv_ln_g'], lp['conv_ln_b']))
    branch_b = a @ lp['w_conv_out']

    uv = jax.nn.gelu(gmlp_in, approximate=False)
    u, v = uv[..., :GMLP_W], uv[..., GMLP_W:]
    v = layernorm(v, lp['gmlp_ln_g'], lp['gmlp_ln_b'])
    vc = v.reshape(B, L // GMLP_CHUNK, GMLP_CHUNK, GMLP_GROUPS, GMLP_W // GMLP_GROUPS)
    sv = jnp.einsum('gpq,bnqgc->bnpgc', lp['gmlp_ws'], vc) + lp['gmlp_bs'].T[:, :, None]
    branch_c = (u * sv.reshape(B, L, GMLP_W)) @ lp['w_gmlp_out']

    groups = jnp.split(pool_in, POOL_GROUPS, axis=-1)
    pooled = jnp.stack([centred_mean_minus_self(g, w) for g, w in zip(groups, POOL_WINDOWS)], axis=2)
    pmix = jnp.einsum('blgc,gcd->blgd', pooled, lp['pool_w']).reshape(B, L, POOL_W) * lp['pool_scale']
    branch_d = pmix @ lp['w_pool_out']

    gates = jax.nn.sigmoid(gate_logits + lp['b_gate']).reshape(B, L, N_BRANCH, D_MODEL)
    merged = (gates[:, :, 0] * branch_a + gates[:, :, 1] * branch_b
              + gates[:, :, 2] * branch_c + gates[:, :, 3] * branch_d)
    return merged @ lp['w_out'], c_kv, k_pe

def conv_ffn(h, lp):
    up = depthwise_conv(h @ lp['ffn_up'], lp['ffn_dw'], lp['ffn_dw_b'])
    gate, val = up[..., :D_FF], up[..., D_FF:]
    return (jax.nn.silu(gate) * val) @ lp['ffn_down']

def trunk_layer(x, mod, lp, row, col, ctx):
    sh1, sc1, g1, sh2, sc2, g2 = jnp.split(mod[:, None, :], 6, axis=-1)
    h = rmsnorm(x, lp['pre_mix_g']) * (1.0 + sc1) + sh1
    mix, c_kv, k_pe = token_mixing(h, lp, row, col, ctx)
    x = x + g1 * rmsnorm(mix, lp['post_mix_g'])
    h = rmsnorm(x, lp['pre_ffn_g']) * (1.0 + sc2) + sh2
    x = x + g2 * rmsnorm(conv_ffn(h, lp), lp['post_ffn_g'])
    return x, c_kv, k_pe

def setup_inputs(seed: int = 0) -> dict:
    key = jax.random.key(seed)
    ks = iter(jax.random.split(key, 48))

    def nrm(shape, scale):
        return jax.random.normal(next(ks), shape, jnp.float32) * scale

    def gain(shape):
        return 1.0 + nrm(shape, 0.05)

    L = DEPTH
    return {
        'x_prompt': nrm((BATCH, SEQ, D_MODEL), 1.0),
        'x_sample': nrm((DEC_BATCH, DEC_SEQ, D_MODEL), 1.0),
        'cache_ckv': nrm((DEC_BATCH, DEPTH, PAST_LEN, KV_LORA), 1.0),
        'cache_kpe': nrm((DEC_BATCH, DEPTH, PAST_LEN, QK_ROPE), 1.0),
        'c': nrm((DEC_BATCH, D_MODEL), 1.0),
        'c_ctx': nrm((D_MODEL,), 1.0),
        'ada_w': nrm((L, D_MODEL, 6 * D_MODEL), D_MODEL ** -0.5),
        'ada_b': nrm((L, 6 * D_MODEL), 0.02),
        'pre_mix_g': gain((L, D_MODEL)),
        'post_mix_g': gain((L, D_MODEL)),
        'pre_ffn_g': gain((L, D_MODEL)),
        'post_ffn_g': gain((L, D_MODEL)),
        'w_in': nrm((L, D_MODEL, D_IN), D_MODEL ** -0.5),
        'b_gate': nrm((L, N_BRANCH * D_MODEL), 0.1),
        'q_norm_g': gain((L, Q_LORA)),
        'w_q_b': nrm((L, Q_LORA, MLA_HEADS * (QK_NOPE + QK_ROPE)), Q_LORA ** -0.5),
        'kv_norm_g': gain((L, KV_LORA)),
        'w_kv_b': nrm((L, KV_LORA, MLA_HEADS * (QK_NOPE + V_HEAD)), KV_LORA ** -0.5),
        'w_o_mla': nrm((L, MLA_W, D_MODEL), MLA_W ** -0.5),
        'conv_dw': nrm((L, CONV_K, CONV_W), CONV_K ** -0.5),
        'conv_dw_b': nrm((L, CONV_W), 0.02),
        'conv_ln_g': gain((L, CONV_W)),
        'conv_ln_b': nrm((L, CONV_W), 0.02),
        'w_conv_out': nrm((L, CONV_W, D_MODEL), CONV_W ** -0.5),
        'gmlp_ln_g': gain((L, GMLP_W)),
        'gmlp_ln_b': nrm((L, GMLP_W), 0.02),
        'gmlp_ws': nrm((L, GMLP_GROUPS, GMLP_CHUNK, GMLP_CHUNK), GMLP_CHUNK ** -0.5),
        'gmlp_bs': 1.0 + nrm((L, GMLP_GROUPS, GMLP_CHUNK), 0.1),
        'w_gmlp_out': nrm((L, GMLP_W, D_MODEL), GMLP_W ** -0.5),
        'pool_w': nrm((L, POOL_GROUPS, POOL_W // POOL_GROUPS, POOL_W // POOL_GROUPS), (POOL_W // POOL_GROUPS) ** -0.5),
        'pool_scale': 1.0 + nrm((L, POOL_W), 0.1),
        'w_pool_out': nrm((L, POOL_W, D_MODEL), POOL_W ** -0.5),
        'w_out': nrm((L, D_MODEL, D_MODEL), D_MODEL ** -0.5),
        'ffn_up': nrm((L, D_MODEL, 2 * D_FF), D_MODEL ** -0.5),
        'ffn_dw': nrm((L, FFN_K, 2 * D_FF), FFN_K ** -0.5),
        'ffn_dw_b': nrm((L, 2 * D_FF), 0.02),
        'ffn_down': nrm((L, D_FF, D_MODEL), D_FF ** -0.5),
    }

def reference(x_prompt, x_sample, cache_ckv, cache_kpe, c, c_ctx, ada_w, ada_b, pre_mix_g, post_mix_g,
              pre_ffn_g, post_ffn_g, w_in, b_gate, q_norm_g, w_q_b, kv_norm_g, w_kv_b, w_o_mla,
              conv_dw, conv_dw_b, conv_ln_g, conv_ln_b, w_conv_out, gmlp_ln_g, gmlp_ln_b, gmlp_ws,
              gmlp_bs, w_gmlp_out, pool_w, pool_scale, w_pool_out, w_out, ffn_up, ffn_dw, ffn_dw_b,
              ffn_down):
    weights = dict(pre_mix_g=pre_mix_g, post_mix_g=post_mix_g, pre_ffn_g=pre_ffn_g, post_ffn_g=post_ffn_g,
                   w_in=w_in, b_gate=b_gate, q_norm_g=q_norm_g, w_q_b=w_q_b, kv_norm_g=kv_norm_g,
                   w_kv_b=w_kv_b, w_o_mla=w_o_mla, conv_dw=conv_dw, conv_dw_b=conv_dw_b,
                   conv_ln_g=conv_ln_g, conv_ln_b=conv_ln_b, w_conv_out=w_conv_out, gmlp_ln_g=gmlp_ln_g,
                   gmlp_ln_b=gmlp_ln_b, gmlp_ws=gmlp_ws, gmlp_bs=gmlp_bs, w_gmlp_out=w_gmlp_out,
                   pool_w=pool_w, pool_scale=pool_scale, w_pool_out=w_pool_out, w_out=w_out,
                   ffn_up=ffn_up, ffn_dw=ffn_dw, ffn_dw_b=ffn_dw_b, ffn_down=ffn_down)
    row, col = grid_positions(x_sample.shape[1])
    xp = x_prompt
    xs = x_sample
    ckv_list = []
    kpe_list = []
    for l in range(DEPTH):
        lp = {k: v[l] for k, v in weights.items()}
        mod_ctx = jax.nn.silu(c_ctx)[None, :] @ ada_w[l] + ada_b[l]
        xp, ckv_l, kpe_l = trunk_layer(xp, mod_ctx, lp, None, None, None)
        ckv_list.append(ckv_l)
        kpe_list.append(kpe_l)
        mod_lat = jax.nn.silu(c) @ ada_w[l] + ada_b[l]
        xs, _, _ = trunk_layer(xs, mod_lat, lp, row, col, (cache_ckv[:, l], cache_kpe[:, l]))
    new_ckv = jnp.stack(ckv_list, axis=1)
    new_kpe = jnp.stack(kpe_list, axis=1)
    return (xp, xs, new_ckv, new_kpe)


_drawn_inputs = setup_inputs


def setup_inputs(seed=0):
    import zlib

    import numpy as np

    out = dict(_drawn_inputs(seed))
    spreads = {}
    factors = {'cache_ckv': 4.583,
     'cache_kpe': 7.887,
     'q_norm_g': 8.0,
     'conv_dw_b': 7.594,
     'conv_ln_g': 4.021,
     'conv_ln_b': 8.0,
     'gmlp_ln_g': 3.12,
     'gmlp_ln_b': 7.442,
     'ffn_dw_b': 4.329}
    for name, (base, spread) in spreads.items():
        noise = np.random.default_rng([zlib.crc32(name.encode()), seed]).standard_normal(out[name].shape)
        drawn = base * np.exp(spread * noise) if base else spread * noise
        out[name] = __import__('jax').numpy.asarray(drawn.astype(out[name].dtype))
    for name, factor in factors.items():
        out[name] = (out[name] * factor).astype(out[name].dtype)
    return out
```

```python
from contextlib import ExitStack

import numpy as np

import concourse.bass as bass
from concourse import mybir
from concourse.alu_op_type import AluOpType as ALU

F32 = mybir.dt.float32
F32R = mybir.dt.float32r
I32 = mybir.dt.int32
ACT = mybir.ActivationFunctionType
AX = mybir.AxisListType

P = 128
DEPTH = 2
D_MODEL = 1024
DC = D_MODEL // P
SEQ, DEC_SEQ, PAST = 128, 512, 128
GRID_W = 64
HEADS, QK_NOPE, QK_ROPE, V_HEAD = 8, 64, 32, 64
QK = QK_NOPE + QK_ROPE
SOFTMAX_SCALE = QK ** -0.5
ROPE_BASE = 10000.0
Q_LORA, KV_LORA = 384, 256
QC, KVC = Q_LORA // P, KV_LORA // P
CONV_W, CONV_K = 256, 31
GMLP_W = POOL_W = 256
HALO = CONV_K // 2
D_FF = 2816
FFC = D_FF // P
EPS = 1e-6
OFF_KV = Q_LORA
OFF_KPE = OFF_KV + KV_LORA
OFF_CONV = OFF_KPE + QK_ROPE
OFF_GMLP = OFF_CONV + 2 * CONV_W
OFF_POOL = OFF_GMLP + 2 * GMLP_W
OFF_GATE = OFF_POOL + POOL_W

SAMPLE0 = SEQ + 2
TOK = SAMPLE0 + DEC_SEQ + 2
HALF = TOK // 2
REGIONS = ((0, SEQ, 0), (SAMPLE0, DEC_SEQ, 1))
NBLK = 5
BLOCK_COL = [0] + [SAMPLE0 + P * b for b in range(4)]
KEYS = DEC_SEQ + PAST
NKEY = KEYS + SEQ

SLOTS = 4
TILES = 4
WBLK = TILES * P
ADA_BLOCKS = 24 * DC // TILES
P1_TILES = 16
P1_BLOCKS = P1_TILES * DC // TILES
OUT_BLOCKS = DC * DC // TILES
UP_BLOCKS = 2 * FFC * DC // TILES
DOWN_BLOCKS = 2 * FFC
MERGE_SIZES = (4, 4, 4, 4, 4, 2, 4, 4, 4, 4, 2, 2)
MERGE_TILES = sum(MERGE_SIZES)
RAW_ORDER = (("ada1", ADA_BLOCKS), ("p1", P1_BLOCKS), ("merge", DC * len(MERGE_SIZES)), ("out", OUT_BLOCKS),
             ("ada2", ADA_BLOCKS), ("up", UP_BLOCKS), ("down", DOWN_BLOCKS))
RAW0, SPLIT0 = {}, {}
RAW_LAYER = SPLIT_LAYER = 0
for _name, _n in RAW_ORDER:
    assert _n % SLOTS == 0
    RAW0[_name], SPLIT0[_name] = RAW_LAYER, SPLIT_LAYER
    RAW_LAYER += _n // SLOTS
    SPLIT_LAYER += 0 if _name.startswith("ada") else _n // SLOTS
LIN0, LIN_BLOCKS = {}, 0
for _name, _n in RAW_ORDER:
    if _name != "merge":
        LIN0[_name] = LIN_BLOCKS
        LIN_BLOCKS += _n

N_PAIRS = HEADS // 2
SET_ORDER = (("gap1", (2, 2, 1, 1)), ("p1", (5, 5, 5, 5)), ("mix", (2, 2, 1, 1)), ("expand", (2, 2, 0, 0)),
             ("pair", (7 * 3, 7 * 3, 10 * 3, 2 * 3)), ("ln", (1, 1, 0, 0)), ("lastpair", (5, 5, 10, 2)), ("lnback", (0, 0, 1, 1)),
             ("merge", (2 * DC,) * 4), ("out", (2,) * 4), ("gap2", (2, 2, 1, 1)), ("up", (FFC // 2,) * 4), ("down", (2,) * 4))
SET0 = {}
SET_LAYER = (0, 0, 0, 0)
for _name, _uses in SET_ORDER:
    SET0[_name] = SET_LAYER
    SET_LAYER = tuple(a + b for a, b in zip(SET_LAYER, _uses))

PAIR_USES = (7, 7, 10, 2)
P1_SET = (0, 1, 2, 3, 0, 1, 2, 3, 2, 3, 2, 3, 0, 2, 3, 1)
MERGE_PLAN = ((0, 0, None), (1, 0, None), (2, 0, (0, 4)), (3, 0, (4, 2)),
              (0, 1, None), (1, 1, None), (2, 1, (6, 2)), (3, 1, (8, 2)))
GATE_LAST_SLOT = (1, 3, 3, 1)
BRANCH_LAST_SLOT = (0, 1, 2, 3)
SQ_GAP1, SQ_P1, SQ_OUT, SQ_GAP2, SQ_DOWN, SQ_LAYER = 0, 8, 13, 21, 29, 37
NSUM = 6

PARAMS = (("pre_mix_g", DC), ("post_mix_g", DC), ("pre_ffn_g", DC), ("post_ffn_g", DC), ("q_norm_g", QC), ("kv_norm_g", KVC),
          ("b_gate", 4 * DC), ("conv_dw", 2 * CONV_K), ("conv_dw_b", 2), ("conv_ln_g", 2), ("conv_ln_b", 2), ("pool_scale", 2),
          ("ffn_dw", 3 * 2 * FFC), ("ffn_dw_b", 2 * FFC), ("ada_b", 48))
PCOL, NPARAM = {}, 0
for _name, _n in PARAMS:
    PCOL[_name] = NPARAM
    NPARAM += _n
TABLES = 2 * GMLP_W + 2 * P + 2 * P + 4 * P
POOL_WINDOWS = (2, 4, 8, 16)
EDGE = 8
CPAD = HALO + SEQ + HALO + DEC_SEQ + HALO
CLEN = SEQ + HALO + DEC_SEQ
PPAD = EDGE + SEQ + EDGE + DEC_SEQ + EDGE


def trunk_kernel(nc, x_in, cond_in, w_lin, w_merge, w_pair, params_in, tables_in, ctx_ckv, ctx_kpe, const_in,
                 y_out, ckv_out, kpe_out):
    with ExitStack() as ctx:
        end = [16512]

        def sb(name, words, dt=F32, at=None, shape=None):
            offset = end[0] if at is None else at
            if at is None:
                end[0] += (words * 4 + 31) // 32 * 32
            return nc.alloc_sbuf_tensor_at(name, [P] + (shape or [words]), dt, offset=offset)

        x = sb("x", DC * TOK, shape=[DC, TOK])
        h_hi = sb("h_hi", DC * TOK, F32R, shape=[DC, TOK])
        h_lo = sb("h_lo", DC * TOK, F32R, shape=[DC, TOK])
        w_raw = sb("w_raw", SLOTS * WBLK, shape=[SLOTS, WBLK])
        w_hi = sb("w_hi", SLOTS * WBLK, F32R, shape=[SLOTS, WBLK])
        w_lo = sb("w_lo", SLOTS * WBLK, F32R, shape=[SLOTS, WBLK])
        const = sb("const", 2 * P + DEC_SEQ + 4 * EDGE + 2)
        ident = const[:, 0:P]
        ones = const[:, P:2 * P]
        rope = const[:, 2 * P:2 * P + DEC_SEQ]
        edge = const[:, 2 * P + DEC_SEQ:2 * P + DEC_SEQ + 4 * EDGE].rearrange("p (c s e) -> p c s e", c=2, s=2)
        inv_window = const[:, 2 * P + DEC_SEQ + 4 * EDGE:]
        par = sb("par", NPARAM)
        half_gate = sb("half_gate", 4 * DC)
        cond = sb("cond", 2 * DC, shape=[DC, 2])
        cond_t = sb("cond_t", 2 * DC, shape=[DC, 2])
        mod = sb("mod", 48, shape=[24, 2])
        mod_a = sb("mod_a", 2 * DC, shape=[DC, 2])
        mod_b = sb("mod_b", 2 * DC, shape=[DC, 2])
        mod_g = sb("mod_g", 2 * DC, shape=[DC, 2])
        small = sb("small", 96)
        var_e, rstd, nw_a, nw_b = (small[:, 8 * i:8 * i + NBLK] for i in range(4))
        neg_max, exp_sum, inv_sum = (small[:, 32 + 2 * i:34 + 2 * i] for i in range(3))
        bn = small[:, 48:48 + 6 * NBLK].rearrange("p (b n) -> p b n", b=NBLK)
        mean_var = small[:, 80:80 + 2 * NBLK].rearrange("p (b n) -> p b n", b=NBLK)
        u0 = end[0]
        U_WORDS = (nc.sbuf_usable_end - u0) // 4

        def u(name, start, words, dt=F32, shape=None):
            assert start % 8 == 0 and start + words <= U_WORDS, (name, start + words, U_WORDS)
            return sb(name, words, dt, u0 + 4 * start, shape)

        yb = u("yb", 0, DC * TOK, shape=[DC, TOK])
        qa = u("qa", 0, QC * TOK, shape=[QC, TOK])
        ckv = u("ckv", 1936, KVC * NKEY, shape=[KVC, NKEY])
        v_pair = u("v_pair", 3472, NKEY, shape=[6, P])
        q_raw = u("q_raw", 4240, 2 * TOK, shape=[2, TOK])
        q_rot = u("q_rot", 5528, 2 * DEC_SEQ, shape=[2, DEC_SEQ])
        k_t = u("k_t", 6552, 2 * NKEY, shape=[2, NKEY])
        probs = u("probs", 8088, 2 * KEYS, shape=[2, KEYS])
        probs_t = u("probs_t", 9368, 5 * DEC_SEQ, shape=[5, DEC_SEQ])
        probs_tp = u("probs_tp", 11928, SEQ)
        diag_kv = u("diag_kv", 12056, NBLK * P, shape=[NBLK, P])
        kv_raw = u("kv_raw", 9368, KVC * TOK, shape=[KVC, TOK])
        kpe_raw = u("kpe_raw", 10656, TOK)
        pool_x = u("pool_x", 8088, PPAD)
        sum_a = u("sum_a", 4240, PPAD)
        sum_b = u("sum_b", 4904, PPAD)
        sq_sum_kv = u("sq_sum_kv", 5568, TOK)
        br_hi = u("br_hi", 0, 10 * TOK, F32R, shape=[10, TOK])
        br_lo = u("br_lo", 10 * TOK, 10 * TOK, F32R, shape=[10, TOK])
        A_END = 20 * TOK
        br = u("br", A_END, 10 * TOK, shape=[10, TOK])
        conv_x = u("conv_x", A_END + 6440, 2 * 688, shape=[2, 688])
        conv_tok = u("conv_tok", A_END + 6440, NBLK * 256, shape=[NBLK, 256])
        conv_acc = u("conv_acc", A_END + 6440 + 1376, 2 * 656, shape=[2, 656])
        tables = u("tables", A_END + 9128, 1024)
        tok_major = u("tok_major", A_END + 2 * TOK, NBLK * 256, shape=[NBLK, 256])
        mg_hi = u("mg_hi", A_END, DC * TOK, F32R, shape=[DC, TOK])
        mg_lo = u("mg_lo", A_END + DC * TOK, DC * TOK, F32R, shape=[DC, TOK])
        E0 = A_END + 2 * DC * TOK
        sq = u("sq", E0, 2 * TOK, shape=[2, TOK])
        sq_sum = u("sq_sum", E0 + 2 * TOK, TOK)
        conv_tmp = u("conv_tmp", E0, 2 * 656, shape=[2, 656])
        hx = u("hx", E0 + 1936, 2 * TOK, shape=[2, TOK])
        diag = u("diag", E0 + 3224, NBLK * P, shape=[NBLK, P])
        gate_t = u("gate_t", E0, 4 * TOK, shape=[4, TOK])
        macc = u("macc", E0 + 4 * TOK, TOK)
        mtmp = u("mtmp", E0 + 3224, TOK)
        ws_t = u("ws_t", E0 + 3872, 4 * P)
        pw = u("pw", E0 + 4512, 10 * P)
        act = u("act", DC * TOK, FFC * TOK, shape=[FFC, TOK])
        F0 = (DC + FFC) * TOK
        up_x = u("up_x", F0, 4 * 648, shape=[4, 648])
        up_y = u("up_y", E0 + 1936, 4 * TOK, shape=[4, TOK])
        up_t = u("up_t", E0 + 4512, 2 * TOK, shape=[2, TOK])
        a_hi = u("a_hi", F0, 2 * TOK, F32R, shape=[2, TOK])
        a_lo = u("a_lo", F0 + 2 * TOK, 2 * TOK, F32R, shape=[2, TOK])

        ps = ctx.enter_context(nc.psum_tensor("ps", [P, 8, 512], F32))

        def pset(s):
            return ps[:, 2 * s:2 * s + 2, :]

        def halves(s, lo=0, hi=P):
            return ps[lo:hi, 2 * s:2 * s + 2, 0:HALF]

        def line(s, n, lo=0, hi=P):
            return pset(s).rearrange("p a b -> p (a b)")[lo:hi, 0:n]

        def region(s, g, lo=0, hi=P):
            return ps[lo:hi, 2 * s + g, 0:(SEQ, DEC_SEQ)[g]]

        def two(ap):
            return ap.rearrange("p (a b) -> p a b", a=2)

        def sem(name):
            return ctx.enter_context(nc.semaphore(name))

        const_in_place = sem("const_in_place")
        x_loaded = sem("x_loaded")
        raw_loaded = [sem(f"raw_loaded{s}") for s in range(SLOTS)]
        raw_empty = [sem(f"raw_empty{s}") for s in range(SLOTS)]
        w_split = [sem(f"w_split{s}") for s in range(SLOTS)]
        w_used = [sem(f"w_used{s}") for s in range(SLOTS)]
        set_full = [sem(f"set_full{s}") for s in range(4)]
        set_empty = [sem(f"set_empty{s}") for s in range(4)]
        layer_free = sem("layer_free")
        par_loaded = sem("par_loaded")
        ctx_loaded = sem("ctx_loaded")
        pw_loaded = sem("pw_loaded")
        pw_used = sem("pw_used")
        halo_zero = sem("halo_zero")
        cond_tanh = sem("cond_tanh")
        cond_ready = sem("cond_ready")
        sum_ready = sem("sum_ready")
        diag_ready = sem("diag_ready")
        x_new = sem("x_new")
        sq_ready = sem("sq_ready")
        sq_used = sem("sq_used")
        t_ready = sem("t_ready")
        hi_ready = sem("hi_ready")
        h_ready = sem("h_ready")
        p1_copied = sem("p1_copied")
        gmlp_in = sem("gmlp_in")
        gmlp_norm = sem("gmlp_norm")
        pool_x_free = sem("pool_x_free")
        pool_ready = sem("pool_ready")
        conv_in = sem("conv_in")
        conv_done = sem("conv_done")
        conv_norm = sem("conv_norm")
        conv_pre = sem("conv_pre")
        conv_silu = sem("conv_silu")
        qkv_ready = sem("qkv_ready")
        qkv_out = sem("qkv_out")
        q_part = sem("q_part")
        q_ready = sem("q_ready")
        k_ready = sem("k_ready")
        k2_ready = sem("k2_ready")
        v_ready = sem("v_ready")
        max_ready = sem("max_ready")
        exp_ready = sem("exp_ready")
        probs_ready = sem("probs_ready")
        pt_ready = sem("pt_ready")
        attn_ready = sem("attn_ready")
        br_part = sem("br_part")
        br_ready = sem("br_ready")
        gate_ready = sem("gate_ready")
        merge_sum = sem("merge_sum")
        mg_part = sem("mg_part")
        mg_ready = sem("mg_ready")
        up_copied = sem("up_copied")
        up_conv = sem("up_conv")
        up_tanh = sem("up_tanh")
        act_ready = sem("act_ready")
        a_part = sem("a_part")
        a_ready = sem("a_ready")
        pool_steps = sem("pool_steps")
        y_stored = sem("y_stored")

        def raw_round(L, phase, k):
            return L * RAW_LAYER + (RAW0[phase] + k)

        def split_round(L, phase, k):
            return L * SPLIT_LAYER + (SPLIT0[phase] + k)

        def set_use(L, phase, s, k):
            return L * SET_LAYER[s] + (SET0[phase][s] + k)

        block = ctx.enter_context(nc.Block())

        @block.sync
        def _(sp):
            sp.dma_start(const[:, :], const_in).then_inc(const_in_place, 16)
            sp.dma_start(cond[:, :, :], cond_in).then_inc(const_in_place, 16)
            for c in range(DC):
                sp.dma_start(x[:, c, :], x_in[c]).then_inc(x_loaded, 16)

            def load_linear(L, phase, first_round, rounds):
                with sp.Fori(0, rounds) as r:
                    for s in range(SLOTS):
                        sp.wait_ge(raw_empty[s], raw_round(L, phase, first_round + 1) + r)
                        src = w_lin[bass.ds(L * LIN_BLOCKS + r * SLOTS + (LIN0[phase] + first_round * SLOTS + s), 1)]
                        sp.dma_start(w_raw[:, s, :], src.rearrange("a p n -> (a p) n")).then_inc(raw_loaded[s], 16)

            with sp.Fori(0, DEPTH) as L:
                load_linear(L, "ada1", 0, 2)
                sp.wait_ge(layer_free, L + 1)
                sp.dma_start(par[:, :], params_in[bass.ds(L, 1)].rearrange("a p n -> (a p) n")).then_inc(par_loaded, 16)
                sp.dma_start(tables[:, :], tables_in[bass.ds(L, 1), :, 0:1024].rearrange("a p n -> (a p) n")).then_inc(par_loaded, 16)
                sp.dma_start(ws_t[:, :], tables_in[bass.ds(L, 1), :, 1024:1536].rearrange("a p n -> (a p) n")).then_inc(par_loaded, 16)
                load_linear(L, "ada1", 2, ADA_BLOCKS // SLOTS - 2)
                load_linear(L, "p1", 0, 1)
                sp.wait_ge(h_ready, L * 2 * DC + DC)
                sp.dma_start(ckv[:, :, DEC_SEQ:KEYS], ctx_ckv[bass.ds(L, 1)].rearrange("a p c n -> (a p) c n")).then_inc(ctx_loaded, 16)
                for hd in range(2):
                    sp.dma_start(k_t[QK_NOPE:QK, hd, DEC_SEQ:KEYS], ctx_kpe[bass.ds(L, 1)].rearrange("a p n -> (a p) n")).then_inc(ctx_loaded, 16)
                load_linear(L, "p1", 1, P1_BLOCKS // SLOTS - 1)
                for p in range(N_PAIRS):
                    sp.wait_ge(pw_used, L * N_PAIRS + (p + 1))
                    sp.dma_start(pw[:, :], w_pair[bass.ds(L * N_PAIRS + p, 1)].rearrange("a p n -> (a p) n")).then_inc(pw_loaded, 16)
                with sp.Fori(0, DC) as d:
                    at = 0
                    for b, n in enumerate(MERGE_SIZES):
                        s, k = b % SLOTS, b // SLOTS
                        sp.wait_ge(raw_empty[s], raw_round(L, "merge", k + 1) + d * (len(MERGE_SIZES) // SLOTS))
                        src = w_merge[bass.ds(L * DC + d, 1), :, at * P:(at + n) * P]
                        sp.dma_start(w_raw[:, s, 0:n * P], src.rearrange("a p n -> (a p) n")).then_inc(raw_loaded[s], 16)
                        at += n
                load_linear(L, "out", 0, OUT_BLOCKS // SLOTS)
                load_linear(L, "ada2", 0, ADA_BLOCKS // SLOTS)
                load_linear(L, "up", 0, UP_BLOCKS // SLOTS)
                load_linear(L, "down", 0, DOWN_BLOCKS // SLOTS)
            for c in range(DC):
                sp.wait_ge(x_new, 2 * DC * DEPTH + c + 1)
                sp.dma_start(y_out[c], x[:, c, :]).then_inc(y_stored, 16)
            sp.wait_ge(y_stored, 16 * DC)

        @block.gpsimd
        def _(pool):
            for s in range(SLOTS):
                pool.sem_inc(raw_empty[s], 1)
            pool.sem_inc(layer_free, 1)
            pool.sem_inc(pw_used, 1)

            def split(L, phase, r, nth, s, n):
                pool.wait_ge(raw_loaded[s], (raw_round(L, phase, nth + 1) + r) * 16)
                pool.wait_ge(w_used[s], split_round(L, phase, nth + 1) + r)
                pool.sem_inc(pool_steps, 1)
                raw = w_raw[:, s, 0:n * P]
                pool.tensor_scalar(w_hi[:, s, 0:n * P], raw, 1.0, None, ALU.mult)
                pool.drain()
                pool.tensor_tensor(w_lo[:, s, 0:n * P], raw, w_hi[:, s, 0:n * P], ALU.subtract).then_inc(w_split[s], 1)
                pool.wait_ge(w_split[s], split_round(L, phase, nth + 1) + r)
                pool.sem_inc(raw_empty[s], 1)

            def split_linear(L, phase, rounds):
                with pool.Fori(0, rounds) as r:
                    for s in range(SLOTS):
                        split(L, phase, r, 0, s, TILES)

            for s in range(SLOTS):
                pool.sem_inc(w_used[s], 1)
            with pool.Fori(0, DEPTH) as L:
                pool.wait_ge(layer_free, L + 1)
                pool.sem_inc(pool_steps, 1)
                pool.memset(conv_x[:, :, :], 0.0).then_inc(halo_zero, 1)
                split_linear(L, "p1", P1_BLOCKS // SLOTS)
                pool.wait_ge(conv_in, 2 * (L + 1))
                pool.sem_inc(pool_steps, 1)
                tap = par[:, PCOL["conv_dw"]:PCOL["conv_dw"] + 2 * CONV_K].rearrange("p (c k) -> p c k", c=2)
                for k in range(CONV_K):
                    for c in range(2):
                        dst = conv_tmp if k else conv_acc
                        pool.tensor_scalar(dst[:, c, 0:CLEN], conv_x[:, c, k:k + CLEN], tap[:, c, k:k + 1],
                                           0.0 if k else par[:, PCOL["conv_dw_b"] + c:PCOL["conv_dw_b"] + c + 1], ALU.mult, ALU.add)
                    pool.drain()
                    if k:
                        for c in range(2):
                            pool.tensor_tensor(conv_acc[:, c, 0:CLEN], conv_acc[:, c, 0:CLEN], conv_tmp[:, c, 0:CLEN], ALU.add)
                        pool.drain()
                pool.sem_inc(conv_done, 1)
                with pool.Fori(0, DC) as d:
                    for b, n in enumerate(MERGE_SIZES):
                        split(L, "merge", d * (len(MERGE_SIZES) // SLOTS), b // SLOTS, b % SLOTS, n)
                split_linear(L, "out", OUT_BLOCKS // SLOTS)
                split_linear(L, "up", UP_BLOCKS // SLOTS)
                split_linear(L, "down", DOWN_BLOCKS // SLOTS)

        @block.tensor
        def _(pe):
            def begin(L, phase, s, k):
                pe.wait_ge(set_empty[s], set_use(L, phase, s, k + 1))

            def product(L, phase, r, s, blocks, rhs, k_wait=None):
                total = sum(n for _, _, n in blocks)
                k = 0
                for b, (slot, nth, n) in enumerate(blocks):
                    pe.wait_ge(w_split[slot], split_round(L, phase, nth + 1) + r)
                    for t in range(n):
                        if k_wait is not None:
                            k_wait(k)
                        hi, lo = rhs(k)
                        whi, wlo = w_hi[:, slot, t * P:(t + 1) * P], w_lo[:, slot, t * P:(t + 1) * P]
                        for i, (w, a) in enumerate(((whi, hi), (whi, lo), (wlo, hi))):
                            for j in range(2):
                                last = pe.matmul(ps[:, 2 * s + j, 0:HALF], w, a[:, j * HALF:(j + 1) * HALF],
                                                 start=(k == 0 and i == 0), stop=(k == total - 1 and i == 2))
                        k += 1
                    last.then_inc(set_full[s] if b == len(blocks) - 1 else w_used[slot], 1)

            def h_part(k):
                return h_hi[:, k, :], h_lo[:, k, :]

            def two_blocks(j):
                return [((2 * j) % SLOTS, 2 * j // SLOTS, TILES), ((2 * j + 1) % SLOTS, (2 * j + 1) // SLOTS, TILES)]

            def sum_over_partitions(L, phase, s, k, n, src=sq_sum):
                begin(L, phase, s, k)
                pe.wait_ge(sum_ready, n)
                for b in range(NBLK):
                    last = pe.matmul(ps[:, 2 * s, b:b + 1], src[:, BLOCK_COL[b]:BLOCK_COL[b] + P], ones[:, 0:1],
                                     start=True, stop=True)
                last.then_inc(set_full[s], 1)

            def spread(L, phase, s, k, n, src=diag):
                begin(L, phase, s, k)
                pe.wait_ge(diag_ready, n)
                pe.matmul(ps[:, 2 * s, 0:P], ones, src[:, 0, :], start=True, stop=True)
                pe.matmul(ps[:, 2 * s + 1, :], ones, src[:, 1:NBLK, :].rearrange("p a b -> p (a b)"),
                          start=True, stop=True).then_inc(set_full[s], 1)

            def ada(L, phase, first, rounds, ct0, last_round=False):
                def one(r):
                    for s in range(SLOTS):
                        pe.wait_ge(raw_loaded[s], (raw_round(L, phase, first + 1) + r) * 16)
                        for t in range(TILES):
                            k = (s % 2) * TILES + t
                            col = r * 4 + (2 * (2 * first - ct0) + 2 * (s // 2))
                            out = ps[:, 0, col:col + 2] if isinstance(col, int) else ps[:, 0, bass.ds(col, 2)]
                            last = pe.matmul(out, w_raw[:, s, t * P:(t + 1) * P], cond[:, k, :], start=(k == 0), stop=(k == DC - 1))
                        last.then_inc(set_full[0] if last_round and s == SLOTS - 1 else raw_empty[s], 1)
                if rounds == 1:
                    one(0)
                else:
                    with pe.Fori(0, rounds) as r:
                        one(r)

            def gap(L, phase, ada_phase, n):
                begin(L, phase, 0, 0)
                ada(L, ada_phase, 0, 1, 0)
                sum_over_partitions(L, phase, 1, 0, n + 1)
                ada(L, ada_phase, 1, 1, 0)
                spread(L, phase, 2, 0, n + 1)
                ada(L, ada_phase, 2, 5, 0)
                sum_over_partitions(L, phase, 3, 0, n + 2)
                ada(L, ada_phase, 7, 1, 0, last_round=True)
                spread(L, phase, 1, 1, n + 2)
                begin(L, phase, 0, 1)
                ada(L, ada_phase, 8, 1, 16)
                ada(L, ada_phase, 9, 2, 16)
                ada(L, ada_phase, 11, 1, 16, last_round=True)

            pe.wait_ge(const_in_place, 32)
            pe.wait_ge(cond_ready, 1)
            with pe.Fori(0, DEPTH) as L:
                gap(L, "gap1", "ada1", L * NSUM)

                uses = [0, 0, 0, 0]

                def p1_tile(t, wait_h=False):
                    s = P1_SET[t]
                    begin(L, "p1", s, uses[s])
                    product(L, "p1", t // 2, s, [((2 * t) % SLOTS, 0, TILES), ((2 * t + 1) % SLOTS, 0, TILES)], h_part,
                            (lambda k: pe.wait_ge(h_ready, L * 2 * DC + k + 1)) if wait_h else None)
                    uses[s] += 1

                for t in range(8):
                    p1_tile(t, t == 0)
                sum_over_partitions(L, "p1", 0, uses[0], L * NSUM + 3)
                sum_over_partitions(L, "p1", 1, uses[1], L * NSUM + 4, sq_sum_kv)
                uses[0] += 1
                uses[1] += 1
                p1_tile(8)
                p1_tile(9)
                spread(L, "p1", 0, uses[0], L * NSUM + 3)
                uses[0] += 1
                spread(L, "p1", 1, uses[1], L * NSUM + 4, diag_kv)
                uses[1] += 1
                for t in range(10, 16):
                    p1_tile(t)
                assert tuple(uses) == (5, 5, 5, 5), uses

                pe.wait_ge(gmlp_in, 2 * (L + 1))
                for b in range(NBLK):
                    s, bank = (0, b // 2) if b < 4 else (1, 0)
                    if b in (0, 4):
                        begin(L, "mix", s, 0)
                    for c in range(2):
                        last = pe.transpose(ps[:, 2 * s + bank, (b % 2) * 256 + c * P:(b % 2) * 256 + (c + 1) * P],
                                            br[:, c, BLOCK_COL[b]:BLOCK_COL[b] + P], ident)
                    if b >= 3:
                        last.then_inc(set_full[s], 1)
                pe.wait_ge(gmlp_norm, L + 1)
                for c in range(2):
                    begin(L, "mix", 2 + c, 0)
                    for b in range(NBLK):
                        for g in range(2):
                            out = ps[64 * g:64 * g + 64, 2 * (2 + c) + min(b, 1), max(b - 1, 0) * P:max(b - 1, 0) * P + P]
                            last = pe.matmul(out, tok_major[:, b, c * P + 64 * g:c * P + 64 * g + 64],
                                             ws_t[:, (2 * c + g) * P:(2 * c + g + 1) * P], start=True, stop=True)
                    last.then_inc(set_full[2 + c], 1)
                for c in range(2):
                    begin(L, "mix", c, 1)
                    pe.wait_ge(pool_ready, L * 2 + (c + 1))
                    w = tables[:, 768 + c * P:768 + (c + 1) * P]
                    for j in range(2):
                        last = pe.matmul(ps[:, 2 * c + j, 0:HALF], w, br[:, 8 + c, j * HALF:(j + 1) * HALF], start=True, stop=True)
                    last.then_inc(set_full[c], 1)

                pe.wait_ge(qkv_ready, L + 1)
                pe.wait_ge(ctx_loaded, (L + 1) * 48)

                def expand_qk(phase, p, use, k0, k1):
                    pe.wait_ge(pw_loaded, (L * N_PAIRS + p + 1) * 16)
                    for hd in range(2):
                        pe.wait_ge(set_empty[hd], use(hd, (k0, k1)[hd]) + 1)
                        for g, (c0, n, _) in enumerate(REGIONS):
                            for k in range(QC):
                                last = pe.matmul(ps[:, 2 * hd + g, 0:n], pw[:, (3 * hd + k) * P:(3 * hd + k + 1) * P],
                                                 qa[:, k, c0:c0 + n], start=(k == 0), stop=(k == QC - 1))
                        last.then_inc(set_full[hd], 1)
                    pe.wait_ge(set_empty[0], use(0, k0 + 1) + 1)
                    for bank, (c0, n) in enumerate(((0, 512), (512, NKEY - 512))):
                        for k in range(KVC):
                            last = pe.matmul(ps[:, bank, 0:n], pw[:, (6 + k) * P:(7 + k) * P], ckv[:, k, c0:c0 + n],
                                             start=(k == 0), stop=(k == KVC - 1))
                    last.then_inc(set_full[0], 1)

                def expand_v(use, k1):
                    pe.wait_ge(set_empty[1], use(1, k1) + 1)
                    for b in range(6):
                        for k in range(KVC):
                            last = pe.matmul(ps[:, 2 + b // 4, (b % 4) * P:(b % 4 + 1) * P], ckv[:, k, b * P:(b + 1) * P],
                                             pw[:, (8 + k) * P:(9 + k) * P], start=(k == 0), stop=(k == KVC - 1))
                    last.then_inc(set_full[1], 1)

                def scores(p, i, use):
                    hd, j, s = i // 5, i % 5, i % 2
                    pe.wait_ge(set_empty[s], use(s, i // 2) + 1)
                    if j == 0:
                        pe.wait_ge(q_ready, (L * N_PAIRS + p) * 2 + (hd + 1))
                        pe.wait_ge((k_ready, k2_ready)[hd], L * N_PAIRS + p + 1)
                    if j < 4:
                        pe.matmul(ps[:, 2 * s, :], q_rot[0:QK, hd, j * P:(j + 1) * P], k_t[0:QK, hd, 0:DEC_SEQ],
                                  start=True, stop=True)
                        last = pe.matmul(ps[:, 2 * s + 1, 0:PAST], q_raw[0:QK, hd, SAMPLE0 + j * P:SAMPLE0 + (j + 1) * P],
                                         k_t[0:QK, hd, DEC_SEQ:KEYS], start=True, stop=True)
                    else:
                        last = pe.matmul(ps[:, 2 * s, 0:SEQ], q_raw[0:QK, hd, 0:SEQ], k_t[0:QK, hd, KEYS:NKEY],
                                         start=True, stop=True)
                    last.then_inc(set_full[s], 1)

                def transposes(p, i, use):
                    pe.wait_ge(set_empty[2], use(2, i) + 1)
                    pe.wait_ge(probs_ready, (L * N_PAIRS + p) * 10 + (i + 1))
                    for b in range(5 if i % 5 < 4 else 1):
                        last = pe.transpose(ps[:, 4 + b // 4, (b % 4) * P:(b % 4 + 1) * P], probs[:, i % 2, b * P:(b + 1) * P], ident)
                    last.then_inc(set_full[2], 1)

                def weighted(p, hd, use):
                    pe.wait_ge(set_empty[3], use(3, hd) + 1)
                    pe.wait_ge(pt_ready, (L * N_PAIRS + p) * 10 + 5 * (hd + 1))
                    if hd == 0:
                        pe.wait_ge(v_ready, L * N_PAIRS + p + 1)
                    vs = slice(hd * V_HEAD, (hd + 1) * V_HEAD)
                    for b in range(5):
                        pe.matmul(ps[0:V_HEAD, 7, :], v_pair[:, b, vs], probs_t[:, b, :], start=(b == 0), stop=(b == 4))
                    pe.matmul(ps[0:V_HEAD, 6, 0:SEQ], v_pair[:, 5, vs], probs_tp[:, :], start=True, stop=True).then_inc(set_full[3], 1)

                def pair(p, use, expand_next):
                    scores(p, 0, use)
                    scores(p, 1, use)
                    for i in range(10):
                        transposes(p, i, use)
                        if i + 2 < 10:
                            scores(p, i + 2, use)
                        if i == 4:
                            weighted(p, 0, use)
                    if expand_next:
                        expand_qk("pair", p + 1, use, 5, 5)
                    weighted(p, 1, use)
                    if expand_next:
                        expand_v(use, 6)

                def first_use(s, k):
                    return set_use(L, "expand", s, k)

                expand_qk("expand", 0, first_use, 0, 0)
                expand_v(first_use, 1)
                with pe.Fori(0, N_PAIRS - 1) as p:
                    pair(p, lambda s, k: set_use(L, "pair", s, k) + p * PAIR_USES[s], True)
                pe.wait_ge(conv_done, L + 1)
                for b in range(NBLK):
                    s, bank = (0, b // 2) if b < 4 else (1, 0)
                    if b in (0, 4):
                        begin(L, "ln", s, 0)
                    at = 0 if b == 0 else SEQ + HALO + (b - 1) * P
                    for c in range(2):
                        last = pe.transpose(ps[:, 2 * s + bank, (b % 2) * 256 + c * P:(b % 2) * 256 + (c + 1) * P],
                                            conv_acc[:, c, at:at + P], ident)
                    if b >= 3:
                        last.then_inc(set_full[s], 1)
                pair(N_PAIRS - 1, lambda s, k: set_use(L, "lastpair", s, k), False)
                pe.wait_ge(conv_norm, L + 1)
                for c in range(2):
                    begin(L, "lnback", 2 + c, 0)
                    for b in range(NBLK):
                        last = pe.transpose(ps[:, 2 * (2 + c) + min(b, 1), max(b - 1, 0) * P:max(b - 1, 0) * P + P],
                                            conv_tok[:, b, c * P:(c + 1) * P], ident)
                    last.then_inc(set_full[2 + c], 1)

                with pe.Fori(0, DC) as d:
                    b0 = 0
                    for s, half, src in MERGE_PLAN:
                        n_blocks = 2 if src is None else 1
                        blocks = [((b0 + i) % SLOTS, (b0 + i) // SLOTS, MERGE_SIZES[b0 + i]) for i in range(n_blocks)]
                        b0 += n_blocks
                        pe.wait_ge(set_empty[s], set_use(L, "merge", s, half + 1) + d * 2)
                        if src is None:
                            rhs = h_part
                        else:
                            first, n = src
                            pe.wait_ge(br_ready, L * 10 + (first + n))
                            rhs = lambda k, first=first: (br_hi[:, first + k, :], br_lo[:, first + k, :])
                        product(L, "merge", d * 3, s, blocks, rhs)

                with pe.Fori(0, 2) as i:
                    for j in range(4):
                        pe.wait_ge(set_empty[j], set_use(L, "out", j, 1) + i)
                        if j == 0:
                            pe.wait_ge(mg_ready, (L + 1) * DC)
                        product(L, "out", i * 2, j, two_blocks(j), lambda k: (mg_hi[:, k, :], mg_lo[:, k, :]))

                gap(L, "gap2", "ada2", L * NSUM + 4)

                with pe.Fori(0, FFC // 2) as i:
                    for j in range(4):
                        pe.wait_ge(set_empty[j], set_use(L, "up", j, 1) + i)
                        if j == 0:
                            pe.wait_ge(h_ready, (L + 1) * 2 * DC)
                        product(L, "up", i * 2, j, two_blocks(j), h_part)

                def down_chunk(pass_, chunk, nth, slot, par_, start, stop):
                    pe.wait_ge(w_split[slot], split_round(L, "down", 1) + nth)
                    pe.wait_ge(a_ready, L * (2 * FFC) + chunk + 1)
                    for s in range(4):
                        if start:
                            begin(L, "down", s, pass_)
                        hi, lo = a_hi[:, par_, :], a_lo[:, par_, :]
                        whi, wlo = w_hi[:, slot, s * P:(s + 1) * P], w_lo[:, slot, s * P:(s + 1) * P]
                        for i, (w, a) in enumerate(((whi, hi), (whi, lo), (wlo, hi))):
                            for j in range(2):
                                last = pe.matmul(ps[:, 2 * s + j, 0:HALF], w, a[:, j * HALF:(j + 1) * HALF],
                                                 start=(start and i == 0), stop=(stop and i == 2))
                        if stop:
                            last.then_inc(set_full[s], 1)
                    if not stop:
                        last.then_inc(w_used[slot], 1)

                for q in range(2):
                    c0 = q * FFC
                    for k in (0, 1):
                        down_chunk(q, c0 + k, (c0 + k) // SLOTS, (c0 + k) % SLOTS, k % 2, k == 0, False)
                    with pe.Fori(0, (FFC - 6) // SLOTS) as i:
                        for k in range(2, 6):
                            down_chunk(q, i * SLOTS + (c0 + k), i + (c0 + k) // SLOTS, (c0 + k) % SLOTS, k % 2, False, False)
                    for k in range(FFC - 4, FFC):
                        down_chunk(q, c0 + k, (c0 + k) // SLOTS, (c0 + k) % SLOTS, k % 2, False, k == FFC - 1)

            sum_over_partitions(DEPTH, "gap1", 1, 0, DEPTH * NSUM + 1)
            spread(DEPTH, "gap1", 2, 0, DEPTH * NSUM + 1)

        @block.scalar
        def _(ac):
            def full(L, phase, s, k):
                ac.wait_ge(set_full[s], set_use(L, phase, s, k + 1))

            def square(dst, src, L, n, first, i=0):
                ac.wait_ge(sq_used, L * SQ_LAYER + (n + (1 if first else 0)) + i)
                ac.activation(dst, src, ACT.Square).then_inc(sq_ready, 1)

            def release_after_square(s, L, n, i=0):
                ac.wait_ge(sq_ready, L * SQ_LAYER + (n + 1) + i)
                ac.sem_inc(set_empty[s], 1)

            def chunk(t, k):
                return t[:, bass.ds(k, 1), :].rearrange("p a b -> p (a b)")

            def gap(L, sq0, n):
                for c in range(DC):
                    ac.wait_ge(x_new, n * DC + (c + 1))
                    square(sq[:, c % 2, :], x[:, c, :], L, sq0 + c, c == 0)
                for c in range(DC):
                    ac.wait_ge(t_ready, n * DC + (c + 1))
                    for c0, m, g in REGIONS:
                        last = ac.activation(h_hi[:, c, c0:c0 + m], hx[:, c % 2, c0:c0 + m], ACT.Identity, bias=mod_b[:, c, g:g + 1])
                    last.then_inc(hi_ready, 1)

            for s in range(4):
                ac.sem_inc(set_empty[s], 1)
            ac.wait_ge(const_in_place, 32)
            ac.activation(cond_t[:, :, :], cond[:, :, :], ACT.Tanh, scale=0.5).then_inc(cond_tanh, 1)
            with ac.Fori(0, DEPTH) as L:
                gap(L, SQ_GAP1, L * 2)

                uses = [0, 0, 0, 0]

                def tile_done(t):
                    s = P1_SET[t]
                    full(L, "p1", s, uses[s])
                    ac.sem_inc(w_used[(2 * t + 1) % SLOTS], 1)
                    uses[s] += 1
                    return s

                for t in range(QC + KVC):
                    s = tile_done(t)
                    dst = qa[:, t, :] if t < QC else kv_raw[:, t - QC, :]
                    ac.activation(two(dst), halves(s), ACT.Copy).then_inc(p1_copied, 1)
                    square(two(sq[:, t % 2, :]), halves(s), L, SQ_P1 + t, t == 0)
                    release_after_square(s, L, SQ_P1 + t)

                def copied(s):
                    ac.wait_ge(set_empty[s], set_use(L, "p1", s, uses[s] + 1))
                    ac.sem_inc(p1_copied, 1)

                s = tile_done(5)
                ac.activation(two(kpe_raw[64:P, :]), halves(s, 64, P), ACT.Copy).then_inc(set_empty[s], 1)
                copied(s)
                for c in range(2):
                    s = tile_done(6 + c)
                    ac.activation(two(br[:, c, :]), halves(s), ACT.Gelu).then_inc(set_empty[s], 1)
                    ac.wait_ge(set_empty[s], set_use(L, "p1", s, uses[s] + 1))
                    ac.sem_inc(gmlp_in, 1)
                uses[0] += 2
                uses[1] += 2
                for c in range(2):
                    s = tile_done(8 + c)
                    ac.activation(two(br[:, 6 + c, :]), halves(s), ACT.Gelu).then_inc(set_empty[s], 1)
                for c in range(2):
                    s = tile_done(10 + 3 * c)
                    ac.activation(two(br[:, 2 + c, :]), halves(s), ACT.Tanh, scale=0.5).then_inc(set_empty[s], 1)
                    s = tile_done(11 + 3 * c)
                    ac.activation(two(br[:, 4 + c, :]), halves(s), ACT.Copy).then_inc(set_empty[s], 1)
                    copied(s)
                    s = tile_done(12 + 3 * c)
                    ac.wait_ge(pool_x_free, L * 3 + (c + 1))
                    p0, in_first = 2 * EDGE + SEQ, HALF - SAMPLE0
                    ac.activation(pool_x[:, EDGE:EDGE + SEQ], ps[:, 2 * s, 0:SEQ], ACT.Copy)
                    ac.activation(pool_x[:, p0:p0 + in_first], ps[:, 2 * s, SAMPLE0:HALF], ACT.Copy)
                    ac.activation(pool_x[:, p0 + in_first:p0 + DEC_SEQ], ps[:, 2 * s + 1, 0:DEC_SEQ - in_first], ACT.Copy)\
                        .then_inc(set_empty[s], 1)
                    copied(s)
                assert uses == [5, 5, 5, 5], uses

                ac.wait_ge(qkv_ready, L + 1)
                ac.dma_start(ckv_out[bass.ds(L, 1)].rearrange("a p c n -> (a p) c n"), ckv[:, :, KEYS:NKEY]).then_inc(qkv_out, 16)
                ac.dma_start(kpe_out[bass.ds(L, 1)].rearrange("a p n -> (a p) n"), k_t[QK_NOPE:QK, 0, KEYS:NKEY]).then_inc(qkv_out, 16)
                for c in range(2):
                    full(L, "mix", c, 1)
                    ac.activation(two(br[:, 8 + c, :]), halves(c), ACT.Copy, scale=par[:, PCOL["pool_scale"] + c:PCOL["pool_scale"] + c + 1])\
                        .then_inc(set_empty[c], 1)

                def expand(p, use, k):
                    n = L * N_PAIRS + p
                    for hd in range(2):
                        ac.wait_ge(set_full[hd], use(hd, k) + 1)
                        ac.activation(q_raw[:, hd, 0:SEQ], region(hd, 0), ACT.Copy, scale=SOFTMAX_SCALE)
                        ac.activation(q_raw[:, hd, SAMPLE0:SAMPLE0 + DEC_SEQ], region(hd, 1), ACT.Copy, scale=SOFTMAX_SCALE)
                        ac.activation(q_rot[0:QK_NOPE, hd, :], region(hd, 1, 0, QK_NOPE), ACT.Copy, scale=SOFTMAX_SCALE).then_inc(q_part, 1)
                        ac.wait_ge(q_part, n * 2 + (hd + 1))
                        ac.sem_inc(set_empty[hd], 1)
                    ac.wait_ge(set_full[0], use(0, k + 1) + 1)
                    ac.activation(k_t[0:QK_NOPE, 0, :], line(0, NKEY, 0, QK_NOPE), ACT.Copy).then_inc(k_ready, 1)
                    ac.wait_ge(set_full[1], use(1, k + 1) + 1)
                    ac.activation(v_pair[:, :, :].rearrange("p a b -> p (a b)"), line(1, NKEY), ACT.Copy).then_inc(v_ready, 1)
                    ac.wait_ge(v_ready, n + 1)
                    ac.sem_inc(set_empty[1], 1)
                    ac.sem_inc(pw_used, 1)

                def exp_item(p, i, use):
                    n, s, keys = (L * N_PAIRS + p) * 10 + (i + 1), i % 2, KEYS if i % 5 < 4 else SEQ
                    ac.wait_ge(max_ready, n)
                    ac.activation(probs[:, s, 0:keys], line(s, keys), ACT.Exp, bias=neg_max[:, s:s + 1],
                                  accum_out=exp_sum[:, s:s + 1]).then_inc(exp_ready, 1)
                    ac.wait_ge(exp_ready, n)
                    ac.sem_inc(set_empty[s], 1)

                def copy_item(p, i, use):
                    j = i % 5
                    ac.wait_ge(set_full[2], use(2, i) + 1)
                    if i == 0:
                        ac.wait_ge(attn_ready, (L * N_PAIRS + p) * 2 + 1)
                    if i == 5:
                        ac.wait_ge(set_full[3], use(3, 0) + 1)
                    if j < 4:
                        ac.activation(probs_t[:, :, j * P:(j + 1) * P], line(2, KEYS).rearrange("p (a b) -> p a b", a=5),
                                      ACT.Copy).then_inc(pt_ready, 1)
                    else:
                        ac.activation(probs_tp[:, :], line(2, SEQ), ACT.Copy).then_inc(pt_ready, 1)
                    ac.wait_ge(pt_ready, (L * N_PAIRS + p) * 10 + (i + 1))
                    ac.sem_inc(set_empty[2], 1)

                def pair(p, use, expand_next):
                    for i in range(11):
                        if i < 10:
                            exp_item(p, i, use)
                        if i >= 1:
                            copy_item(p, i - 1, use)
                    if expand_next:
                        expand(p + 1, use, 5)

                expand(0, lambda s, k: set_use(L, "expand", s, k), 0)
                with ac.Fori(0, N_PAIRS - 1) as p:
                    pair(p, lambda s, k: set_use(L, "pair", s, k) + p * PAIR_USES[s], True)
                pair(N_PAIRS - 1, lambda s, k: set_use(L, "lastpair", s, k), False)

                for c in range(2):
                    full(L, "lnback", 2 + c, 0)
                    for c0, m, g in REGIONS:
                        last = ac.activation(br[:, 4 + c, c0:c0 + m], region(2 + c, g), ACT.Identity,
                                             scale=par[:, PCOL["conv_ln_g"] + c:PCOL["conv_ln_g"] + c + 1],
                                             bias=par[:, PCOL["conv_ln_b"] + c:PCOL["conv_ln_b"] + c + 1])
                    last.then_inc(set_empty[2 + c], 1)
                    ac.wait_ge(set_empty[2 + c], set_use(L, "lnback", 2 + c, 2))
                    for c0, m, g in REGIONS:
                        last = ac.activation(hx[:, c, c0:c0 + m], br[:, 4 + c, c0:c0 + m], ACT.Tanh, scale=0.5)
                    last.then_inc(conv_pre, 1)

                ac.wait_ge(attn_ready, (L + 1) * HEADS + 1)
                ac.wait_ge(qkv_out, (L + 1) * 32)
                for c in range(10):
                    if c == 4:
                        ac.wait_ge(conv_silu, (L + 1) * 2)
                    ac.activation(br_hi[:, c, :], br[:, c, :], ACT.Copy).then_inc(br_part, 1)

                ac.wait_ge(br_ready, (L + 1) * 10)
                with ac.Fori(0, DC) as d:
                    for b, (s, k) in enumerate((s, k) for s, k, src in MERGE_PLAN if src is None):
                        ac.wait_ge(set_full[s], set_use(L, "merge", s, k + 1) + d * 2)
                        ac.sem_inc(w_used[GATE_LAST_SLOT[b]], 1)
                        if b == 0:
                            ac.wait_ge(merge_sum, (L * DC + d) + 1)
                        ac.activation(two(gate_t[:, b, :]), halves(s), ACT.Tanh, scale=0.5, bias=half_gate[:, bass.ds(d + b * DC, 1)])\
                            .then_inc(gate_ready, 1)
                        ac.wait_ge(gate_ready, (L * DC + d) * 4 + (b + 1))
                        ac.sem_inc(set_empty[s], 1)
                    ac.wait_ge(merge_sum, (L * DC + d) + 2)
                    ac.activation(chunk(mg_hi, d), macc[:, :], ACT.Copy, scale=0.5).then_inc(mg_part, 1)

                ac.wait_ge(mg_ready, (L + 1) * DC)
                with ac.Fori(0, 2) as i:
                    for j in range(4):
                        ac.wait_ge(set_full[j], set_use(L, "out", j, 1) + i)
                        ac.sem_inc(w_used[(2 * j + 1) % SLOTS], 1)
                        ac.activation(two(chunk(yb, i * 4 + j)), halves(j), ACT.Copy)
                        square(two(sq[:, j % 2, :]), halves(j), L, SQ_OUT + j, False, i * 4)
                        release_after_square(j, L, SQ_OUT + j, i * 4)

                gap(L, SQ_GAP2, L * 2 + 1)

                with ac.Fori(0, FFC // 2) as i:
                    for j in range(4):
                        q = j // 2
                        ac.wait_ge(set_full[j], set_use(L, "up", j, 1) + i)
                        ac.sem_inc(w_used[(2 * j + 1) % SLOTS], 1)
                        if j % 2 == 0:
                            ac.wait_ge(up_conv, L * FFC + i * 2 + (q + 1))
                        ac.activation(two(up_x[:, j, 2:2 + TOK]), halves(j), ACT.Copy).then_inc(up_copied, 1)
                        ac.wait_ge(up_copied, (L * FFC + i * 2) * 2 + (j + 1))
                        ac.sem_inc(set_empty[j], 1)
                        if j % 2 == 1:
                            ac.wait_ge(up_conv, L * FFC + i * 2 + (q + 3))
                            ac.activation(up_t[:, q, :], up_y[:, 2 * q, :], ACT.Tanh, scale=0.5).then_inc(up_tanh, 1)

                ac.wait_ge(act_ready, (L + 1) * FFC)

                def hi_part(n, k, i=0):
                    if n >= 2:
                        ac.wait_ge(w_used[(n - 2) % SLOTS], split_round(L, "down", (n - 2) // SLOTS + 2) + i)
                    src = act[:, k, :] if isinstance(k, int) else chunk(act, k)
                    ac.activation(a_hi[:, n % 2, :], src, ACT.Copy).then_inc(a_part, 1)

                def outputs(q):
                    for s in range(4):
                        full(L, "down", s, q)
                        if s == 3:
                            ac.sem_inc(w_used[((q + 1) * FFC - 1) % SLOTS], 1)
                        ac.activation(two(yb[:, 4 * q + s, :]), halves(s), ACT.Copy)
                        square(two(sq[:, s % 2, :]), halves(s), L, SQ_DOWN + 4 * q + s, q == 0 and s == 0)
                        release_after_square(s, L, SQ_DOWN + 4 * q + s)

                for q in range(2):
                    n0 = q * FFC
                    hi_part(n0, 0)
                    if q == 1:
                        outputs(0)
                    hi_part(n0 + 1, 1)
                    with ac.Fori(0, (FFC - 2) // SLOTS) as i:
                        for k in range(2, 2 + SLOTS):
                            hi_part(n0 + k, i * SLOTS + k, i)
                outputs(1)
                ac.sem_inc(layer_free, 1)

        @block.vector
        def _(dv):
            def full(L, phase, s, k):
                dv.wait_ge(set_full[s], set_use(L, phase, s, k + 1))

            def chunk(t, k):
                return t[:, bass.ds(k, 1), :].rearrange("p a b -> p (a b)")

            def add_square(sums, b, L, n, i=0):
                dv.wait_ge(sq_ready, L * SQ_LAYER + (n + 1) + i)
                dv.tensor_tensor(sums[:, :], sums[:, :], sq[:, b, :], ALU.add).then_inc(sq_used, 1)
                dv.drain()

            def inverse_root(src, scale):
                dv.tensor_scalar(var_e, src, scale, EPS, ALU.mult, ALU.add)
                dv.drain()
                dv.tensor_scalar(rstd.bitcast(I32), var_e.bitcast(I32), -0.5, 1597463007.0, ALU.mult, ALU.add)
                dv.drain()
                for _ in range(3):
                    dv.tensor_tensor(nw_a, rstd, rstd, ALU.mult)
                    dv.drain()
                    dv.scalar_tensor_tensor(out=nw_b, in0=nw_a, scalar=-0.5, in1=var_e, op0=ALU.mult, op1=ALU.mult)
                    dv.drain()
                    dv.scalar_tensor_tensor(out=rstd, in0=nw_b, scalar=1.5, in1=rstd, op0=ALU.add, op1=ALU.mult)
                    dv.drain()

            def diagonals(dst):
                dv.tensor_tensor(dst[:, :, :], ident[:, None, :].broadcast_to([P, NBLK, P]),
                                 rstd[:, :, None].broadcast_to([P, NBLK, P]), ALU.mult).then_inc(diag_ready, 1)

            def rms(L, phase, s, k, width, dst):
                full(L, phase, s, k)
                inverse_root(ps[:, 2 * s, 0:NBLK], 1.0 / width)
                dv.sem_inc(set_empty[s], 1)
                diagonals(dst)

            def update_x(L, squares, n):
                full(L, "gap1" if n is None else n, 2, 0)
                for c in range(DC + 2):
                    if c < DC:
                        for c0, m, g in REGIONS:
                            dv.scalar_tensor_tensor(out=yb[:, c, c0:c0 + m], in0=yb[:, c, c0:c0 + m], scalar=mod_g[:, c, g:g + 1],
                                                    in1=region(2, g), op0=ALU.mult, op1=ALU.mult)
                    if 1 <= c <= DC:
                        for c0, m, g in REGIONS:
                            last = dv.tensor_tensor(x[:, c - 1, c0:c0 + m], x[:, c - 1, c0:c0 + m], yb[:, c - 1, c0:c0 + m], ALU.add)
                        last.then_inc(x_new, 1)
                    dv.drain()
                    if c == DC:
                        dv.sem_inc(set_empty[2], 1)
                    if squares is not None and c >= 2:
                        add_square(sq_sum, c % 2, L, squares + c - 2)

            def gap(L, phase, n, sq0, ada0, pre_g, post_g):
                rms(L, phase, 1, 0, D_MODEL, diag)
                dv.memset(sq_sum[:, :], 0.0)
                dv.drain()
                update_x(L, sq0, phase)
                dv.sem_inc(sum_ready, 1)
                rms(L, phase, 3, 0, D_MODEL, diag)
                if phase == "gap1":
                    dv.wait_ge(par_loaded, (L + 1) * 48)
                    dv.tensor_scalar(half_gate[:, :], par[:, PCOL["b_gate"]:PCOL["b_gate"] + 4 * DC], 0.5, None, ALU.mult)
                full(L, phase, 0, 0)
                dv.sem_inc(raw_empty[SLOTS - 1], 1)
                bias = par[:, PCOL["ada_b"] + ada0:PCOL["ada_b"] + ada0 + 24, None]
                dv.tensor_tensor(mod[:, 0:16, :], ps[:, 0, 0:32].rearrange("p (a b) -> p a b", b=2), bias[:, 0:16].broadcast_to([P, 16, 2]), ALU.add)
                dv.drain()
                dv.sem_inc(set_empty[0], 1)
                g = par[:, PCOL[pre_g]:PCOL[pre_g] + DC, None].broadcast_to([P, DC, 2])
                dv.scalar_tensor_tensor(out=mod_a[:, :, :], in0=mod[:, DC:2 * DC, :], scalar=1.0, in1=g, op0=ALU.add, op1=ALU.mult)
                dv.tensor_copy(mod_b[:, :, :], mod[:, 0:DC, :])
                dv.drain()
                full(L, phase, 1, 1)
                for c in range(DC + 1):
                    if c < DC:
                        for c0, m, g in REGIONS:
                            last = dv.scalar_tensor_tensor(out=hx[:, c % 2, c0:c0 + m], in0=x[:, c, c0:c0 + m], scalar=mod_a[:, c, g:g + 1],
                                                           in1=region(1, g), op0=ALU.mult, op1=ALU.mult)
                        last.then_inc(t_ready, 1)
                    if c >= 1:
                        dv.wait_ge(hi_ready, n * DC + c)
                        for c0, m, g in REGIONS:
                            last = dv.scalar_tensor_tensor(out=h_lo[:, c - 1, c0:c0 + m], in0=hx[:, (c - 1) % 2, c0:c0 + m],
                                                           scalar=mod_b[:, c - 1, g:g + 1], in1=h_hi[:, c - 1, c0:c0 + m],
                                                           op0=ALU.add, op1=ALU.subtract)
                        last.then_inc(h_ready, 1)
                    dv.drain()
                dv.sem_inc(set_empty[1], 1)
                full(L, phase, 0, 1)
                dv.sem_inc(raw_empty[SLOTS - 1], 1)
                dv.tensor_tensor(mod[:, 16:24, :], ps[:, 0, 0:16].rearrange("p (a b) -> p a b", b=2), bias[:, 16:24].broadcast_to([P, DC, 2]), ALU.add)
                dv.drain()
                dv.sem_inc(set_empty[0], 1)
                g = par[:, PCOL[post_g]:PCOL[post_g] + DC, None].broadcast_to([P, DC, 2])
                dv.tensor_tensor(mod_g[:, :, :], mod[:, 16:24, :], g, ALU.mult)
                dv.drain()

            def layernorm(L, phase, dst):
                def src(b):
                    return ps[:, b // 2, (b % 2) * 256:(b % 2) * 256 + 256]
                for b in range(NBLK):
                    if b in (0, 4):
                        full(L, phase, b // 4, 0)
                    dv.bn_stats(bn[:, b, :], src(b))
                dv.drain()
                for b in range(NBLK):
                    dv.bn_aggr(mean_var[:, b, :], bn[:, b, :])
                dv.drain()
                inverse_root(mean_var[:, :, 1], 1.0)
                for b in range(NBLK):
                    dv.tensor_scalar(dst[:, b, :], src(b), mean_var[:, b, 0:1], rstd[:, b:b + 1], ALU.subtract, ALU.mult)
                dv.drain()
                dv.sem_inc(set_empty[0], 1)
                dv.sem_inc(set_empty[1], 1)

            def rotate(dst, pe_rows, swapped_rows):
                dv.scalar_tensor_tensor(out=hx[64:96, 0, 0:DEC_SEQ], in0=pe_rows, scalar=1.0, in1=rope[64:96, :], op0=ALU.mult, op1=ALU.mult)
                dv.scalar_tensor_tensor(out=hx[64:96, 1, 0:DEC_SEQ], in0=swapped_rows, scalar=1.0, in1=rope[96:P, :], op0=ALU.mult, op1=ALU.mult)
                dv.drain()
                return dv.tensor_tensor(dst, hx[64:96, 0, 0:DEC_SEQ], hx[64:96, 1, 0:DEC_SEQ], ALU.add)

            dv.sem_inc(sq_used, 1)
            dv.sem_inc(attn_ready, 1)
            dv.sem_inc(merge_sum, 1)
            dv.sem_inc(up_conv, 2)
            dv.memset(mod_g[:, :, :], 0.0)
            dv.memset(yb[:, :, :], 0.0)
            for c in (SEQ, TOK - 2):
                dv.memset(h_hi[:, :, c:c + 2].bitcast(F32), 0.0)
                dv.memset(h_lo[:, :, c:c + 2].bitcast(F32), 0.0)
            dv.memset(sq_sum[:, :], 0.0).then_inc(sum_ready, 1)
            dv.wait_ge(cond_tanh, 1)
            dv.tensor_scalar(cond_t[:, :, :], cond_t[:, :, :], 0.5, 0.5, ALU.mult, ALU.add)
            dv.drain()
            dv.tensor_tensor(cond[:, :, :], cond[:, :, :], cond_t[:, :, :], ALU.mult).then_inc(cond_ready, 1)
            dv.wait_ge(x_loaded, 16 * DC)

            with dv.Fori(0, DEPTH) as L:
                gap(L, "gap1", L * 2, SQ_GAP1, 0, "pre_mix_g", "post_mix_g")

                dv.memset(sq_sum[:, :], 0.0)
                dv.memset(sq_sum_kv[:, :], 0.0)
                dv.memset(pool_x[:, :], 0.0)
                dv.drain()
                dv.sem_inc(pool_x_free, 1)
                for c in range(QC):
                    add_square(sq_sum, c % 2, L, SQ_P1 + c)
                dv.sem_inc(sum_ready, 1)
                for c in range(KVC):
                    add_square(sq_sum_kv, (QC + c) % 2, L, SQ_P1 + QC + c)
                dv.sem_inc(sum_ready, 1)
                dv.wait_ge(p1_copied, L * 10 + 6)
                rotate(k_t[64:96, 0, 0:DEC_SEQ], kpe_raw[64:96, SAMPLE0:SAMPLE0 + DEC_SEQ], kpe_raw[96:P, SAMPLE0:SAMPLE0 + DEC_SEQ])
                for hd in range(2):
                    dv.tensor_copy(k_t[64:96, hd, KEYS:NKEY], kpe_raw[64:96, 0:SEQ])
                dv.drain()
                dv.tensor_copy(k_t[64:96, 1, 0:DEC_SEQ], k_t[64:96, 0, 0:DEC_SEQ])
                rms(L, "p1", 0, 2, Q_LORA, diag)
                dv.drain()
                rms(L, "p1", 1, 2, KV_LORA, diag_kv)
                full(L, "p1", 0, 3)
                for c in range(QC):
                    for c0, m, g in REGIONS:
                        dv.scalar_tensor_tensor(out=qa[:, c, c0:c0 + m], in0=qa[:, c, c0:c0 + m], scalar=par[:, PCOL["q_norm_g"] + c:PCOL["q_norm_g"] + c + 1],
                                                in1=region(0, g), op0=ALU.mult, op1=ALU.mult)
                dv.drain()
                dv.sem_inc(set_empty[0], 1)
                full(L, "p1", 1, 3)
                for c in range(KVC):
                    for c0, m, g in REGIONS:
                        to = 0 if g else KEYS
                        dv.scalar_tensor_tensor(out=ckv[:, c, to:to + m], in0=kv_raw[:, c, c0:c0 + m], scalar=par[:, PCOL["kv_norm_g"] + c:PCOL["kv_norm_g"] + c + 1],
                                                in1=region(1, g), op0=ALU.mult, op1=ALU.mult)
                dv.drain()
                dv.sem_inc(set_empty[1], 1)
                dv.sem_inc(qkv_ready, 1)

                dv.wait_ge(halo_zero, L + 1)
                for c in range(2):
                    dv.wait_ge(p1_copied, L * 10 + (7 + 2 * c))
                    dv.tensor_scalar(br[:, 2 + c, :], br[:, 2 + c, :], 0.5, 0.5, ALU.mult, ALU.add)
                    dv.drain()
                    for c0, m, g in REGIONS:
                        to = HALO + (SEQ + HALO) * g
                        last = dv.tensor_tensor(conv_x[:, c, to:to + m], br[:, 2 + c, c0:c0 + m], br[:, 4 + c, c0:c0 + m], ALU.mult)
                    last.then_inc(conv_in, 1)
                    dv.wait_ge(p1_copied, L * 10 + (8 + 2 * c))
                    n = PPAD
                    dv.tensor_tensor(sum_a[:, 1:n], pool_x[:, 0:n - 1], pool_x[:, 1:n], ALU.add)
                    dv.drain()
                    dv.tensor_tensor(sum_b[:, 2:n - 1], sum_a[:, 1:n - 2], sum_a[:, 3:n], ALU.add)
                    dv.drain()
                    if c == 1:
                        dv.tensor_tensor(sum_a[:, 4:n - 3], sum_b[:, 2:n - 5], sum_b[:, 6:n - 1], ALU.add)
                        dv.drain()
                        dv.tensor_tensor(sum_b[:, 8:n - 7], sum_a[:, 4:n - 11], sum_a[:, 12:n - 3], ALU.add)
                        dv.drain()
                    dv.tensor_copy(sum_a[64:P, 8:n - 8], sum_b[64:P, 8:n - 8])
                    dv.drain()
                    for g, m in enumerate((SEQ, DEC_SEQ)):
                        p0 = EDGE + (SEQ + EDGE) * g
                        for side in range(2):
                            at = p0 + side * (m - EDGE)
                            dv.tensor_tensor(sum_a[:, at:at + EDGE], sum_a[:, at:at + EDGE], edge[:, c, side, :], ALU.mult)
                    dv.drain()
                    for c0, m, g in REGIONS:
                        p0 = EDGE + (SEQ + EDGE) * g
                        dv.scalar_tensor_tensor(out=br[:, 8 + c, c0:c0 + m], in0=sum_a[:, p0:p0 + m], scalar=inv_window[:, c:c + 1],
                                                in1=pool_x[:, p0:p0 + m], op0=ALU.mult, op1=ALU.subtract)
                        dv.memset(br[:, 8 + c, c0 + m:c0 + m + 2], 0.0)
                    dv.drain()
                    dv.sem_inc(pool_ready, 1)
                    dv.sem_inc(pool_x_free, 1)

                layernorm(L, "mix", tok_major)
                for i, op in enumerate((ALU.mult, ALU.add)):
                    t = tables[:, None, i * GMLP_W:(i + 1) * GMLP_W].broadcast_to([P, NBLK, GMLP_W])
                    last = dv.tensor_tensor(tok_major[:, :, :], tok_major[:, :, :], t, op)
                    dv.drain()
                dv.sem_inc(gmlp_norm, 1)
                for c in range(2):
                    full(L, "mix", 2 + c, 0)
                    t = tables[:, 512 + c * P:512 + (c + 1) * P]
                    dv.tensor_tensor(hx[:, c, 0:SEQ], region(2 + c, 0), t, ALU.add)
                    dv.tensor_tensor(hx[:, c, SAMPLE0:SAMPLE0 + DEC_SEQ].rearrange("p (a b) -> p a b", a=4),
                                     region(2 + c, 1).rearrange("p (a b) -> p a b", a=4), t[:, None, :].broadcast_to([P, 4, P]), ALU.add)
                    dv.drain()
                    dv.sem_inc(set_empty[2 + c], 1)
                    for c0, m, g in REGIONS:
                        dv.tensor_tensor(br[:, 6 + c, c0:c0 + m], br[:, 6 + c, c0:c0 + m], hx[:, c, c0:c0 + m], ALU.mult)
                for c in (SEQ, TOK - 2):
                    dv.memset(br[:, 0:4, c:c + 2], 0.0)
                dv.drain()

                def expand(p, use, k):
                    n = L * N_PAIRS + p
                    for hd in range(2):
                        dv.wait_ge(q_part, n * 2 + (hd + 1))
                        sample = slice(SAMPLE0, SAMPLE0 + DEC_SEQ)
                        rotate(q_rot[64:96, hd, :], q_raw[64:96, hd, sample], q_raw[96:P, hd, sample])
                        dv.drain()
                        dv.sem_inc(q_ready, 1)
                    dv.wait_ge(set_full[0], use(0, k + 1) + 1)
                    dv.tensor_copy(k_t[0:QK_NOPE, 1, :], line(0, NKEY, 64, P)).then_inc(k2_ready, 1)
                    dv.wait_ge(k2_ready, n + 1)
                    dv.wait_ge(k_ready, n + 1)
                    dv.sem_inc(set_empty[0], 1)

                def max_item(p, i, use):
                    s, keys = i % 2, KEYS if i % 5 < 4 else SEQ
                    dv.wait_ge(set_full[s], use(s, i // 2) + 1)
                    dv.tensor_reduce(neg_max[:, s:s + 1], line(s, keys), AX.X, ALU.max, negate=True).then_inc(max_ready, 1)

                def normalise_item(p, i):
                    s, keys = i % 2, KEYS if i % 5 < 4 else SEQ
                    dv.wait_ge(exp_ready, (L * N_PAIRS + p) * 10 + (i + 1))
                    dv.reciprocal(inv_sum[:, s:s + 1], exp_sum[:, s:s + 1])
                    dv.drain()
                    dv.tensor_scalar(probs[:, s, 0:keys], probs[:, s, 0:keys], inv_sum[:, s:s + 1], None, ALU.mult).then_inc(probs_ready, 1)

                def head_out(p, hd, use):
                    dv.wait_ge(set_full[3], use(3, hd) + 1)
                    rows = slice(64 * hd, 64 * hd + 64)
                    for c0, m, g in REGIONS:
                        dst = br[rows, p, c0:c0 + m] if isinstance(p, int) else br[rows, bass.ds(p, 1), c0:c0 + m].rearrange("p a b -> p (a b)")
                        dv.tensor_copy(dst, region(3, g, 0, V_HEAD))
                    dv.drain()
                    dv.sem_inc(set_empty[3], 1)
                    dv.sem_inc(attn_ready, 1)

                def pair(p, use, expand_next):
                    max_item(p, 0, use)
                    for i in range(10):
                        if i + 1 < 10:
                            max_item(p, i + 1, use)
                        normalise_item(p, i)
                        if i == 5:
                            head_out(p, 0, use)
                    if expand_next:
                        expand(p + 1, use, 5)
                    head_out(p, 1, use)

                expand(0, lambda s, k: set_use(L, "expand", s, k), 0)
                with dv.Fori(0, N_PAIRS - 1) as p:
                    pair(p, lambda s, k: set_use(L, "pair", s, k) + p * PAIR_USES[s], True)
                layernorm(L, "ln", conv_tok)
                dv.sem_inc(conv_norm, 1)
                pair(N_PAIRS - 1, lambda s, k: set_use(L, "lastpair", s, k), False)

                for c in range(2):
                    dv.wait_ge(conv_pre, L * 2 + (c + 1))
                    for c0, m, g in REGIONS:
                        dv.tensor_scalar(hx[:, c, c0:c0 + m], hx[:, c, c0:c0 + m], 0.5, 0.5, ALU.mult, ALU.add)
                    dv.drain()
                    for c0, m, g in REGIONS:
                        last = dv.tensor_tensor(br[:, 4 + c, c0:c0 + m], br[:, 4 + c, c0:c0 + m], hx[:, c, c0:c0 + m], ALU.mult)
                    last.then_inc(conv_silu, 1)
                dv.drain()
                for c in range(10):
                    dv.wait_ge(br_part, L * 10 + (c + 1))
                    dv.tensor_tensor(br_lo[:, c, :], br[:, c, :], br_hi[:, c, :], ALU.subtract).then_inc(br_ready, 1)

                with dv.Fori(0, DC) as d:
                    for b, (s, k) in enumerate((s, k) for s, k, src in MERGE_PLAN if src is not None):
                        dv.wait_ge(set_full[s], set_use(L, "merge", s, k + 1) + d * 2)
                        dv.sem_inc(w_used[BRANCH_LAST_SLOT[b]], 1)
                        dv.wait_ge(gate_ready, (L * DC + d) * 4 + (b + 1))
                        dst = macc if b == 0 else mtmp
                        dv.scalar_tensor_tensor(out=two(dst[:, :]), in0=two(gate_t[:, b, :]), scalar=1.0, in1=halves(s),
                                                op0=ALU.add, op1=ALU.mult).then_inc(set_empty[s], 1)
                        dv.drain()
                        if b:
                            last = dv.tensor_tensor(macc[:, :], macc[:, :], mtmp[:, :], ALU.add)
                            if b == 3:
                                last.then_inc(merge_sum, 1)
                            dv.drain()
                    dv.wait_ge(mg_part, L * DC + d + 1)
                    dv.scalar_tensor_tensor(out=chunk(mg_lo, d), in0=macc[:, :], scalar=0.5, in1=chunk(mg_hi, d),
                                            op0=ALU.mult, op1=ALU.subtract).then_inc(mg_ready, 1)
                    dv.drain()

                dv.memset(sq_sum[:, :], 0.0)
                dv.drain()
                with dv.Fori(0, 2) as i:
                    for j in range(4):
                        add_square(sq_sum, j % 2, L, SQ_OUT + j, i * 4)
                dv.sem_inc(sum_ready, 1)

                gap(L, "gap2", L * 2 + 1, SQ_GAP2, 24, "pre_ffn_g", "post_ffn_g")

                for j in range(4):
                    dv.memset(up_x[:, j, 0:2], 0.0)
                    dv.memset(up_x[:, j, 2 + TOK:4 + TOK], 0.0)
                dv.drain()
                with dv.Fori(0, FFC // 2) as i:
                    for q in range(2):
                        def col(name, v, tap=0):
                            return par[:, bass.ds(i * 4 + (PCOL[name] + tap * 2 * FFC + 2 * q + v), 1)]
                        dv.wait_ge(up_copied, (L * FFC + i * 2) * 2 + (2 * q + 2))
                        for v in range(2):
                            j = 2 * q + v
                            dv.tensor_scalar(up_y[:, j, :], up_x[:, j, 2:2 + TOK], col("ffn_dw", v, 1), col("ffn_dw_b", v), ALU.mult, ALU.add)
                        for tap in (0, 2):
                            dv.drain()
                            for v in range(2):
                                j = 2 * q + v
                                last = dv.scalar_tensor_tensor(out=up_y[:, j, :], in0=up_x[:, j, 1 + tap:1 + tap + TOK], scalar=col("ffn_dw", v, tap),
                                                               in1=up_y[:, j, :], op0=ALU.mult, op1=ALU.add)
                        last.then_inc(up_conv, 1)
                        dv.drain()
                        dv.wait_ge(up_tanh, L * FFC + i * 2 + (q + 1))
                        dv.scalar_tensor_tensor(out=up_t[:, q, :], in0=up_t[:, q, :], scalar=1.0, in1=up_y[:, 2 * q, :], op0=ALU.add, op1=ALU.mult)
                        dv.drain()
                        dv.scalar_tensor_tensor(out=chunk(act, i * 2 + q), in0=up_t[:, q, :], scalar=0.5, in1=up_y[:, 2 * q + 1, :],
                                                op0=ALU.mult, op1=ALU.mult).then_inc(act_ready, 1)

                dv.memset(sq_sum[:, :], 0.0)
                dv.drain()

                def lo_part(n, k, i=0):
                    dv.wait_ge(a_part, L * 2 * FFC + (n + 1) + i * SLOTS)
                    src = act[:, k, :] if isinstance(k, int) else chunk(act, k)
                    dv.tensor_tensor(a_lo[:, n % 2, :], src, a_hi[:, n % 2, :], ALU.subtract).then_inc(a_ready, 1)

                for q in range(2):
                    n0 = q * FFC
                    lo_part(n0, 0)
                    if q == 1:
                        for s in range(4):
                            add_square(sq_sum, s % 2, L, SQ_DOWN + s)
                    lo_part(n0 + 1, 1)
                    with dv.Fori(0, (FFC - 2) // SLOTS) as i:
                        for k in range(2, 2 + SLOTS):
                            lo_part(n0 + k, i * SLOTS + k, i)
                for s in range(4):
                    add_square(sq_sum, s % 2, L, SQ_DOWN + 4 + s)
                dv.sem_inc(sum_ready, 1)

            rms(DEPTH, "gap1", 1, 0, D_MODEL, diag)
            update_x(DEPTH, None, "gap1")


def _tiles(w, cols):
    n_l, k, _ = w.shape
    t = np.stack([w[:, :, c:c + P] for c in cols], 1)
    return t.reshape(n_l, len(cols), k // P, P, P).transpose(0, 1, 3, 2, 4)


def _blocks(t):
    n_l, n, _, k, _ = t.shape
    return t.reshape(n_l, n, P, k // TILES, WBLK).transpose(0, 1, 3, 2, 4).reshape(n_l, -1, P, WBLK)


def _columns(v):
    return v.reshape(v.shape[0], -1, P).transpose(0, 2, 1)


_SWAP = np.concatenate([np.arange(8, 16), np.arange(0, 8), np.arange(24, 32), np.arange(16, 24)])


def _const():
    c = np.zeros((P, 2 * P + DEC_SEQ + 4 * EDGE + 2), np.float32)
    c[:, 0:P] = np.eye(P)
    c[:, P:2 * P] = 1.0
    t = np.arange(DEC_SEQ)
    half = QK_ROPE // 4
    inv = (np.float32(ROPE_BASE) ** (-np.arange(half, dtype=np.float32) / np.float32(half))).astype(np.float32)
    for i in range(QK_ROPE):
        pos = (t // GRID_W if i < QK_ROPE // 2 else t % GRID_W).astype(np.float32)
        ang = pos * inv[i % half]
        c[64 + i, 2 * P:2 * P + DEC_SEQ] = np.cos(ang)
        c[96 + i, 2 * P:2 * P + DEC_SEQ] = np.sin(ang) * (-1.0 if (i // half) % 2 == 0 else 1.0)
    for p in range(P):
        for k in range(2):
            w = POOL_WINDOWS[2 * k + p // 64]
            lo, hi = w // 2, w - w // 2 - 1
            for e in range(EDGE):
                base = 2 * P + DEC_SEQ + 2 * k * EDGE
                c[p, base + e] = w / (min(e, lo) + hi + 1)
                c[p, base + EDGE + e] = w / (lo + min(EDGE - 1 - e, hi) + 1)
            c[p, 2 * P + DEC_SEQ + 4 * EDGE + k] = 1.0 / w
    return c


def kernel(**inputs):
    import concourse.bacc as _bacc
    from concourse import mybir as _mybir
    from concourse.bass_utils import run_bass_kernel_spmd as _run

    a = {k: np.asarray(v) for k, v in inputs.items()}
    f = np.float32
    ld = DEPTH
    x_in = np.zeros((DC, P, TOK), f)
    x_in[:, :, 0:SEQ] = a["x_prompt"][0].T.reshape(DC, P, SEQ)
    x_in[:, :, SAMPLE0:SAMPLE0 + DEC_SEQ] = a["x_sample"][0].T.reshape(DC, P, DEC_SEQ)
    cond_in = np.stack([a["c_ctx"].reshape(DC, P).T, a["c"][0].reshape(DC, P).T], 2)

    w_in = a["w_in"]
    kpe = w_in[:, :, OFF_KPE:OFF_CONV]
    zeros = np.zeros((ld, D_MODEL, 64), f)
    kpe_tile = np.concatenate([zeros, kpe, kpe[:, :, _SWAP]], 2)
    def t(*cols):
        return _tiles(w_in, cols)
    v0, u0, x1, x2, pl = OFF_GMLP + GMLP_W, OFF_GMLP, OFF_CONV, OFF_CONV + CONV_W, OFF_POOL
    p1 = np.concatenate([t(0, P, 2 * P, OFF_KV, OFF_KV + P), _tiles(kpe_tile, [0]), t(v0, v0 + P, u0, u0 + P),
                         t(x2, x1, pl, x2 + P, x1 + P, pl + P)], 1)
    ada = _tiles(a["ada_w"], range(0, 6 * D_MODEL, P))
    up = _tiles(a["ffn_up"], [o + c * P for c in range(FFC) for o in (0, D_FF)])
    down = a["ffn_down"].reshape(ld, FFC, P, 2, 4 * P).transpose(0, 3, 1, 2, 4).reshape(ld, 2 * FFC, P, WBLK)
    w_lin = np.concatenate([_blocks(ada[:, 0:24]), _blocks(p1), _blocks(_tiles(a["w_out"], range(0, D_MODEL, P))),
                            _blocks(ada[:, 24:48]), _blocks(up), down], 1).reshape(ld * LIN_BLOCKS, P, WBLK)
    gates = [_tiles(w_in, [OFF_GATE + b * D_MODEL + d * P for d in range(DC)]) for b in range(4)]
    outs = [_tiles(a[n], range(0, D_MODEL, P)) for n in ("w_o_mla", "w_conv_out", "w_gmlp_out", "w_pool_out")]
    w_merge = np.concatenate([gates[0], gates[1], outs[0], outs[1], gates[2], gates[3], outs[2], outs[3]], 3)
    w_merge = w_merge.reshape(ld * DC, P, MERGE_TILES * P)
    wq = a["w_q_b"].reshape(ld, QC, P, HEADS, QK)
    wq = np.concatenate([wq, wq[..., QK_NOPE:][..., _SWAP]], 4).transpose(0, 3, 2, 1, 4)
    wq = wq.reshape(ld, N_PAIRS, 2, P, QC * P).transpose(0, 1, 3, 2, 4).reshape(ld, N_PAIRS, P, 2 * QC * P)
    wkv = a["w_kv_b"].reshape(ld, KVC, P, N_PAIRS, 2, 2, 64).transpose(0, 3, 2, 5, 1, 4, 6)
    w_pair = np.concatenate([wq, wkv.reshape(ld, N_PAIRS, P, 4 * P)], 3).reshape(ld * N_PAIRS, P, 10 * P)

    def taps(w, order):
        return w.reshape(ld, w.shape[1], -1, P).transpose(order).reshape(ld, P, -1)

    def interleaved(v):
        return v.reshape(ld, v.shape[1], 2, FFC, P).transpose(0, 4, 1, 3, 2).reshape(ld, P, -1)

    parts = {n: _columns(a[n]) for n in ("pre_mix_g", "post_mix_g", "pre_ffn_g", "post_ffn_g", "q_norm_g", "kv_norm_g", "b_gate",
                                         "conv_dw_b", "conv_ln_g", "conv_ln_b", "pool_scale", "ada_b")}
    parts["conv_dw"] = taps(a["conv_dw"], (0, 3, 2, 1))
    parts["ffn_dw"] = interleaved(a["ffn_dw"])
    parts["ffn_dw_b"] = interleaved(a["ffn_dw_b"][:, None, :])
    params_in = np.concatenate([parts[n] for n, _ in PARAMS], 2)

    rows = np.broadcast_to(np.concatenate([a["gmlp_ln_g"], a["gmlp_ln_b"]], 1)[:, None, :], (ld, P, 2 * GMLP_W))
    bs = np.repeat(a["gmlp_bs"], 64, axis=1).reshape(ld, 2, P, P).transpose(0, 2, 1, 3).reshape(ld, P, 2 * P)
    pool_w = np.zeros((ld, P, 2, P), f)
    for g in range(4):
        o = 64 * (g % 2)
        pool_w[:, o:o + 64, g // 2, o:o + 64] = a["pool_w"][:, g]
    ws = a["gmlp_ws"].transpose(0, 3, 1, 2).reshape(ld, P, 4 * P)
    tables_in = np.concatenate([rows, bs, pool_w.reshape(ld, P, 2 * P), ws], 2)
    ctx_ckv = a["cache_ckv"][0].reshape(ld, PAST, KVC, P).transpose(0, 3, 2, 1)
    ctx_kpe = a["cache_kpe"][0].transpose(0, 2, 1)

    nc = _bacc.Bacc("TRN2", target_bir_lowering=False, num_devices=1)
    arrays, args = {}, []
    for name, v in (("x", x_in), ("cond", cond_in), ("w_lin", w_lin), ("w_merge", w_merge), ("w_pair", w_pair), ("params", params_in),
                    ("tables", tables_in), ("ctx_ckv", ctx_ckv), ("ctx_kpe", ctx_kpe), ("const", _const())):
        v = np.ascontiguousarray(v)
        arrays[f"in_{name}_dram"] = v
        args.append(nc.dram_tensor(f"in_{name}_dram", v.shape, _mybir.dt.from_np(v.dtype), kind="ExternalInput").ap())
    for name, shape in (("y", (DC, P, TOK)), ("ckv", (ld, P, KVC, SEQ)), ("kpe", (ld, QK_ROPE, SEQ))):
        args.append(nc.dram_tensor(f"out_{name}_dram", shape, F32, kind="ExternalOutput").ap())
    trunk_kernel(nc, *args)
    r = _run(nc, [arrays], core_ids=[0]).results[0]
    y = r["out_y_dram"].reshape(D_MODEL, TOK)
    y_prompt = np.ascontiguousarray(y[:, 0:SEQ].T)[None]
    y_sample = np.ascontiguousarray(y[:, SAMPLE0:SAMPLE0 + DEC_SEQ].T)[None]
    new_ckv = np.ascontiguousarray(r["out_ckv_dram"].transpose(0, 3, 2, 1).reshape(ld, SEQ, KV_LORA))[None]
    new_kpe = np.ascontiguousarray(r["out_kpe_dram"].transpose(0, 2, 1))[None]
    return y_prompt, y_sample, new_ckv, new_kpe
```

```python
from contextlib import ExitStack

import numpy as np

import concourse.bass as bass
from concourse import mybir
from concourse.alu_op_type import AluOpType as ALU

F32 = mybir.dt.float32
F32R = mybir.dt.float32r
I32 = mybir.dt.int32
ACT = mybir.ActivationFunctionType
AX = mybir.AxisListType

P = 128
DEPTH = 2
D_MODEL = 1024
DC = D_MODEL // P
SEQ, DEC_SEQ, PAST = 128, 512, 128
GRID_W = 64
HEADS, QK_NOPE, QK_ROPE, V_HEAD = 8, 64, 32, 64
QK = QK_NOPE + QK_ROPE
SOFTMAX_SCALE = QK ** -0.5
ROPE_BASE = 10000.0
Q_LORA, KV_LORA = 384, 256
QC, KVC = Q_LORA // P, KV_LORA // P
CONV_W, CONV_K = 256, 31
GMLP_W = POOL_W = 256
HALO = CONV_K // 2
D_FF = 2816
FFC = D_FF // P
EPS = 1e-6
OFF_KV = Q_LORA
OFF_KPE = OFF_KV + KV_LORA
OFF_CONV = OFF_KPE + QK_ROPE
OFF_GMLP = OFF_CONV + 2 * CONV_W
OFF_POOL = OFF_GMLP + 2 * GMLP_W
OFF_GATE = OFF_POOL + POOL_W

SAMPLE0 = SEQ + 2
TOK = SAMPLE0 + DEC_SEQ + 2
HALF = TOK // 2
REGIONS = ((0, SEQ, 0), (SAMPLE0, DEC_SEQ, 1))
NBLK = 5
BLOCK_COL = [0] + [SAMPLE0 + P * b for b in range(4)]
KEYS = DEC_SEQ + PAST
NKEY = KEYS + SEQ

SLOTS = 4
TILES = 4
WBLK = TILES * P
P1_TILES = 16
P1_BLOCKS = P1_TILES * DC // TILES
OUT_BLOCKS = DC * DC // TILES
UP_BLOCKS = 2 * FFC * DC // TILES
DOWN_BLOCKS = 2 * FFC
MERGE_SIZES = (4, 4, 4, 4, 4, 2, 4, 4, 2, 4, 4, 2)
MERGE_TILES = sum(MERGE_SIZES)
MERGE_ROUNDS = len(MERGE_SIZES) // SLOTS
RING0, RING_LAYER, LIN0, LIN_BLOCKS = {}, 0, {}, 0
for _name, _n in (("p1", P1_BLOCKS), ("merge", DC * len(MERGE_SIZES)), ("out", OUT_BLOCKS), ("up", UP_BLOCKS), ("down", DOWN_BLOCKS)):
    assert _n % SLOTS == 0
    RING0[_name] = RING_LAYER
    RING_LAYER += _n // SLOTS
    if _name != "merge":
        LIN0[_name] = LIN_BLOCKS
        LIN_BLOCKS += _n

ADA = 3 * DC
ADA_SLOTS = 3
ADA_LOADS = 4
ADA_OUT = ADA - FFC
ADA_LAYER = (DC + FFC // 2, DC + FFC // 2, DC + 2)
assert FFC + 2 == ADA and DC * ADA_SLOTS == ADA

N_PAIRS = HEADS // 2
SET_ORDER = (("head", (0, 1, 0, 1)), ("p1", (6, 6, 6, 6)), ("expand", (2, 2, 1, 1)),
             ("pair", (7 * 3, 7 * 3, 10 * 3, 2 * 3)), ("ln", (1, 1, 0, 0)), ("lastpair", (5, 5, 10, 2)), ("lnback", (0, 0, 1, 1)),
             ("merge", (2 * DC,) * 4), ("out", (2,) * 4), ("gap2", (0, 2, 1, 1)), ("up", (FFC // 2,) * 4), ("down", (2,) * 4),
             ("tail", (0, 1, 1, 0)))
SET0 = {}
SET_PRE = (1, 0, 0, 0)
SET_LAYER = (0, 0, 0, 0)
for _name, _uses in SET_ORDER:
    SET0[_name] = SET_LAYER
    SET_LAYER = tuple(a + b for a, b in zip(SET_LAYER, _uses))

PAIR_USES = (7, 7, 10, 2)
P1_SET = (0, 1, 2, 3, 0, 1, 2, 3, 2, 3, 2, 3, 2, 3, 2, 3)
BRANCHES = (0, 2, 3, 1)
BRANCH_CHUNKS = ((0, 4), (6, 2), (8, 2), (4, 2))
BRANCH_SPLIT = tuple(sum(n for _, n in BRANCH_CHUNKS[:b + 1]) for b in range(4))
SPLIT_ORDER = (0, 1, 2, 3, 6, 7, 8, 9, 4, 5)
MERGE_PLAN = ((0, 0, None), (2, 0, 0), (1, 0, None), (3, 0, 1), (0, 1, None), (2, 1, 2), (1, 1, None), (3, 1, 3))
GATE_LAST_SLOT = tuple((3 * b + 1) % SLOTS for b in range(4))
BRANCH_LAST_SLOT = tuple((3 * b + 2) % SLOTS for b in range(4))
SQ_HEAD, SQ_P1, SQ_OUT, SQ_GAP2, SQ_DOWN, SQ_LAYER = 0, 8, 13, 21, 29, 37
NSUM, NDIAG, NINV = 4, 6, 4

PARAMS = (("pre_mix_g", DC), ("post_mix_g", DC), ("pre_ffn_g", DC), ("post_ffn_g", DC), ("q_norm_g", QC), ("kv_norm_g", KVC),
          ("b_gate", 4 * DC), ("conv_dw", 2 * CONV_K), ("conv_dw_b", 2), ("conv_ln_g", 2), ("conv_ln_b", 2), ("pool_scale", 2),
          ("ffn_dw", 3 * 2 * FFC), ("ffn_dw_b", 2 * FFC), ("ada_b", 48))
PCOL, NPARAM = {}, 0
for _name, _n in PARAMS:
    PCOL[_name] = NPARAM
    NPARAM += _n
TABLES = 2 * GMLP_W + 2 * P + 2 * P + 4 * P
POOL_WINDOWS = (2, 4, 8, 16)
EDGE = 8
CPAD = HALO + SEQ + HALO + DEC_SEQ + HALO
CLEN = SEQ + HALO + DEC_SEQ
N_CONST = 2 * P + DEC_SEQ + 4 * EDGE + 2 + NBLK
PPAD = EDGE + SEQ + EDGE + DEC_SEQ + EDGE


def trunk_kernel(nc, x_in, cond_in, w_ada, w_lin, w_merge, w_pair, params_in, tables_in, ctx_ckv, ctx_kpe, const_in,
                 y_out, ckv_out, kpe_out):
    with ExitStack() as ctx:
        end = [16512]

        def sb(name, words, dt=F32, at=None, shape=None):
            offset = end[0] if at is None else at
            if at is None:
                end[0] += (words * 4 + 31) // 32 * 32
            return nc.alloc_sbuf_tensor_at(name, [P] + (shape or [words]), dt, offset=offset)

        x = sb("x", DC * TOK, shape=[DC, TOK])
        h_hi = sb("h_hi", DC * TOK, F32R, shape=[DC, TOK])
        h_lo = sb("h_lo", DC * TOK, F32R, shape=[DC, TOK])
        w_raw = sb("w_raw", SLOTS * WBLK, shape=[SLOTS, WBLK])
        w_hi = sb("w_hi", SLOTS * WBLK, F32R, shape=[SLOTS, WBLK])
        w_lo = sb("w_lo", SLOTS * WBLK, F32R, shape=[SLOTS, WBLK])
        const = sb("const", N_CONST)
        ident = const[:, 0:P]
        ones = const[:, P:2 * P]
        rope = const[:, 2 * P:2 * P + DEC_SEQ]
        edge = const[:, 2 * P + DEC_SEQ:2 * P + DEC_SEQ + 4 * EDGE].rearrange("p (c s e) -> p c s e", c=2, s=2)
        inv_window = const[:, N_CONST - NBLK - 2:N_CONST - NBLK]
        zeros = const[:, N_CONST - NBLK:]
        par = sb("par", NPARAM)
        half_gate = sb("half_gate", 4 * DC)
        cond = sb("cond", 2 * DC, shape=[DC, 2])
        cond_t = sb("cond_t", 2 * DC, shape=[DC, 2])
        mod_mix = sb("mod_mix", 2 * ADA, shape=[ADA, 2])
        mod_ffn = sb("mod_ffn", 2 * ADA, shape=[ADA, 2])
        mod_a = sb("mod_a", 2 * DC, shape=[DC, 2])
        mod_b = sb("mod_b", 2 * DC, shape=[DC, 2])
        mod_g = sb("mod_g", 2 * DC, shape=[DC, 2])
        small = sb("small", 96)
        var_e, rstd, nw_a, nw_b = (small[:, 8 * i:8 * i + NBLK] for i in range(4))
        neg_max, exp_sum, inv_sum = (small[:, 32 + 2 * i:34 + 2 * i] for i in range(3))
        bn = small[:, 48:48 + 6 * NBLK].rearrange("p (b n) -> p b n", b=NBLK)
        mean_var = small[:, 80:80 + 2 * NBLK].rearrange("p (b n) -> p b n", b=NBLK)
        u0 = end[0]
        U_WORDS = (nc.sbuf_usable_end - u0) // 4

        def u(name, start, words, dt=F32, shape=None):
            assert start % 8 == 0 and start + words <= U_WORDS, (name, start + words, U_WORDS)
            return sb(name, words, dt, u0 + 4 * start, shape)

        yb = u("yb", 0, DC * TOK, shape=[DC, TOK])
        qa = u("qa", 0, QC * TOK, shape=[QC, TOK])
        ckv = u("ckv", 1936, KVC * NKEY, shape=[KVC, NKEY])
        v_pair = u("v_pair", 3472, NKEY, shape=[6, P])
        q_raw = u("q_raw", 4240, 2 * TOK, shape=[2, TOK])
        q_rot = u("q_rot", 5528, 2 * DEC_SEQ, shape=[2, DEC_SEQ])
        k_t = u("k_t", 6552, 2 * NKEY, shape=[2, NKEY])
        probs = u("probs", 8088, 2 * KEYS, shape=[2, KEYS])
        probs_t = u("probs_t", 9368, 5 * DEC_SEQ, shape=[5, DEC_SEQ])
        probs_tp = u("probs_tp", 11928, SEQ)
        diag_kv = u("diag_kv", 12056, NBLK * P, shape=[NBLK, P])
        kv_raw = u("kv_raw", 9368, KVC * TOK, shape=[KVC, TOK])
        kpe_raw = u("kpe_raw", 10656, TOK)
        pool_x = u("pool_x", 8088, PPAD)
        sum_a = u("sum_a", 9368, PPAD)
        sum_b = u("sum_b", 10040, PPAD)
        sq_sum_kv = u("sq_sum_kv", 5568, TOK)
        br_hi = u("br_hi", 0, 10 * TOK, F32R, shape=[10, TOK])
        br_lo = u("br_lo", 10 * TOK, 10 * TOK, F32R, shape=[10, TOK])
        A_END = 20 * TOK
        br = u("br", A_END, 10 * TOK, shape=[10, TOK])
        conv_x = u("conv_x", A_END + 6440, 2 * 688, shape=[2, 688])
        conv_tok = u("conv_tok", A_END + 6440, NBLK * 256, shape=[NBLK, 256])
        conv_acc = u("conv_acc", A_END + 6440 + 1376, 2 * 656, shape=[2, 656])
        tables = u("tables", A_END + 9128, 1024)
        tok_major = u("tok_major", 4240, NBLK * 256, shape=[NBLK, 256])
        mg_hi = u("mg_hi", A_END, DC * TOK, F32R, shape=[DC, TOK])
        mg_lo = u("mg_lo", A_END + DC * TOK, DC * TOK, F32R, shape=[DC, TOK])
        E0 = A_END + 2 * DC * TOK
        sq = u("sq", E0, 2 * TOK, shape=[2, TOK])
        sq_sum = u("sq_sum", E0 + 2 * TOK, TOK)
        inv_rms = u("inv_rms", E0 + 2 * TOK, TOK)
        ada_pre = u("ada_pre", 0, ADA * D_MODEL, shape=[ADA, D_MODEL])
        conv_tmp = u("conv_tmp", E0, 656)
        hx = u("hx", E0 + 1936, 2 * TOK, shape=[2, TOK])
        diag = u("diag", E0 + 3224, NBLK * P, shape=[NBLK, P])
        gate_t = u("gate_t", E0, 4 * TOK, shape=[4, TOK])
        macc = u("macc", E0 + 4 * TOK, TOK)
        mtmp = u("mtmp", E0 + 3224, TOK)
        ws_t = u("ws_t", E0 + 3872, 4 * P)
        pw = u("pw", E0 + 4512, 10 * P)
        act = u("act", DC * TOK, FFC * TOK, shape=[FFC, TOK])
        F0 = (DC + FFC) * TOK
        up_x = u("up_x", 0, 4 * 648, shape=[4, 648])
        up_y = u("up_y", E0, 4 * TOK, shape=[4, TOK])
        up_t = u("up_t", E0 + 4 * TOK, 2 * TOK, shape=[2, TOK])
        ada_raw = u("ada_raw", E0 + 3872, ADA_SLOTS * D_MODEL, shape=[ADA_SLOTS, D_MODEL])
        a_hi = u("a_hi", F0, 2 * TOK, F32R, shape=[2, TOK])
        a_lo = u("a_lo", F0 + 2 * TOK, 2 * TOK, F32R, shape=[2, TOK])

        ps = ctx.enter_context(nc.psum_tensor("ps", [P, 8, 512], F32))

        def pset(s):
            return ps[:, 2 * s:2 * s + 2, :]

        def halves(s, lo=0, hi=P):
            return ps[lo:hi, 2 * s:2 * s + 2, 0:HALF]

        def line(s, n, lo=0, hi=P):
            return pset(s).rearrange("p a b -> p (a b)")[lo:hi, 0:n]

        def region(s, g, lo=0, hi=P):
            return ps[lo:hi, 2 * s + g, 0:(SEQ, DEC_SEQ)[g]]

        def two(ap):
            return ap.rearrange("p (a b) -> p a b", a=2)

        def sem(name):
            return ctx.enter_context(nc.semaphore(name))

        const_in_place = sem("const_in_place")
        x_loaded = sem("x_loaded")
        raw_loaded = [sem(f"raw_loaded{s}") for s in range(SLOTS)]
        raw_empty = [sem(f"raw_empty{s}") for s in range(SLOTS)]
        w_split = [sem(f"w_split{s}") for s in range(SLOTS)]
        w_used = [sem(f"w_used{s}") for s in range(SLOTS)]
        set_full = [sem(f"set_full{s}") for s in range(4)]
        set_empty = [sem(f"set_empty{s}") for s in range(4)]
        layer_free = sem("layer_free")
        par_loaded = sem("par_loaded")
        ws_loaded = sem("ws_loaded")
        ada_loaded = [sem(f"ada_loaded{s}") for s in range(ADA_SLOTS)]
        ada_pre_loaded = [sem(f"ada_pre_loaded{i}") for i in range(ADA_LOADS)]
        inv_ready = sem("inv_ready")
        mod_ready = sem("mod_ready")
        conv1_done = sem("conv1_done")
        ctx_loaded = sem("ctx_loaded")
        pw_loaded = sem("pw_loaded")
        pw_used = sem("pw_used")
        halo_zero = sem("halo_zero")
        cond_tanh = sem("cond_tanh")
        cond_ready = sem("cond_ready")
        sum_ready = sem("sum_ready")
        diag_ready = sem("diag_ready")
        x_new = sem("x_new")
        sq_ready = sem("sq_ready")
        sq_used = sem("sq_used")
        t_ready = sem("t_ready")
        hi_ready = sem("hi_ready")
        h_ready = sem("h_ready")
        p1_copied = sem("p1_copied")
        gmlp_in = sem("gmlp_in")
        gmlp_norm = sem("gmlp_norm")
        pool_x_free = sem("pool_x_free")
        pool_ready = sem("pool_ready")
        conv_in = sem("conv_in")
        conv_done = sem("conv_done")
        conv_norm = sem("conv_norm")
        conv_pre = sem("conv_pre")
        conv_silu = sem("conv_silu")
        qkv_ready = sem("qkv_ready")
        qkv_out = sem("qkv_out")
        q_part = sem("q_part")
        q_ready = sem("q_ready")
        k_ready = sem("k_ready")
        k2_ready = sem("k2_ready")
        v_ready = sem("v_ready")
        max_ready = sem("max_ready")
        exp_ready = sem("exp_ready")
        probs_ready = sem("probs_ready")
        pt_ready = sem("pt_ready")
        attn_ready = sem("attn_ready")
        br_part = sem("br_part")
        br_ready = sem("br_ready")
        gate_ready = sem("gate_ready")
        merge_sum = sem("merge_sum")
        mg_part = sem("mg_part")
        mg_ready = sem("mg_ready")
        up_copied = sem("up_copied")
        up_conv = sem("up_conv")
        up_tanh = sem("up_tanh")
        act_ready = sem("act_ready")
        a_part = sem("a_part")
        a_ready = sem("a_ready")
        pool_steps = sem("pool_steps")
        y_stored = sem("y_stored")

        def ring_round(L, phase, k):
            return L * RING_LAYER + (RING0[phase] + k)

        def set_use(L, phase, s, k):
            return L * SET_LAYER[s] + (SET_PRE[s] + SET0[phase][s] + k)

        def ada_use(L, slot, k):
            return L * ADA_LAYER[slot] + k

        block = ctx.enter_context(nc.Block())

        @block.sync
        def _(sp):
            sp.dma_start(const[:, :], const_in).then_inc(const_in_place, 16)
            sp.dma_start(cond[:, :, :], cond_in).then_inc(const_in_place, 16)
            for c in range(DC):
                sp.dma_start(x[:, c, :], x_in[c]).then_inc(x_loaded, 16)

            def load_linear(L, phase, first_round, rounds):
                with sp.Fori(0, rounds) as r:
                    for s in range(SLOTS):
                        sp.wait_ge(raw_empty[s], ring_round(L, phase, first_round + 1) + r)
                        src = w_lin[bass.ds(L * LIN_BLOCKS + r * SLOTS + (LIN0[phase] + first_round * SLOTS + s), 1)]
                        sp.dma_start(w_raw[:, s, :], src.rearrange("a p n -> (a p) n")).then_inc(raw_loaded[s], 16)

            with sp.Fori(0, DEPTH) as L:
                load_linear(L, "p1", 0, 2)
                sp.wait_ge(layer_free, L + 1)
                sp.dma_start(par[:, :], params_in[bass.ds(L, 1)].rearrange("a p n -> (a p) n")).then_inc(par_loaded, 16)
                sp.dma_start(tables[:, :], tables_in[bass.ds(L, 1), :, 0:1024].rearrange("a p n -> (a p) n")).then_inc(par_loaded, 16)
                sp.wait_ge(h_ready, L * 2 * DC + DC)
                sp.dma_start(ckv[:, :, DEC_SEQ:KEYS], ctx_ckv[bass.ds(L, 1)].rearrange("a p c n -> (a p) c n")).then_inc(ctx_loaded, 16)
                for hd in range(2):
                    sp.dma_start(k_t[QK_NOPE:QK, hd, DEC_SEQ:KEYS], ctx_kpe[bass.ds(L, 1)].rearrange("a p n -> (a p) n")).then_inc(ctx_loaded, 16)
                sp.dma_start(ws_t[:, :], tables_in[bass.ds(L, 1), :, 1024:1536].rearrange("a p n -> (a p) n")).then_inc(ws_loaded, 16)
                load_linear(L, "p1", 2, P1_BLOCKS // SLOTS - 2)
                for p in range(N_PAIRS):
                    sp.wait_ge(pw_used, L * N_PAIRS + (p + 1))
                    sp.dma_start(pw[:, :], w_pair[bass.ds(L * N_PAIRS + p, 1)].rearrange("a p n -> (a p) n")).then_inc(pw_loaded, 16)
                with sp.Fori(0, DC) as d:
                    at = 0
                    for b, n in enumerate(MERGE_SIZES):
                        s, k = b % SLOTS, b // SLOTS
                        sp.wait_ge(raw_empty[s], ring_round(L, "merge", k + 1) + d * MERGE_ROUNDS)
                        src = w_merge[bass.ds(L * DC + d, 1), :, at * P:(at + n) * P]
                        sp.dma_start(w_raw[:, s, 0:n * P], src.rearrange("a p n -> (a p) n")).then_inc(raw_loaded[s], 16)
                        at += n
                load_linear(L, "out", 0, OUT_BLOCKS // SLOTS)
                load_linear(L, "up", 0, UP_BLOCKS // SLOTS)
                load_linear(L, "down", 0, DOWN_BLOCKS // SLOTS)
            for c in range(DC):
                sp.wait_ge(x_new, 2 * DC * DEPTH + c + 1)
                sp.dma_start(y_out[c], x[:, c, :]).then_inc(y_stored, 16)
            sp.wait_ge(y_stored, 16 * DC)

        @block.gpsimd
        def _(pool):
            for s in range(SLOTS):
                pool.sem_inc(raw_empty[s], 1)
            pool.sem_inc(pw_used, 1)

            def split(L, phase, r, nth, s, n):
                pool.wait_ge(raw_loaded[s], (ring_round(L, phase, nth + 1) + r) * 16)
                pool.wait_ge(w_used[s], ring_round(L, phase, nth + 1) + r)
                pool.sem_inc(pool_steps, 1)
                raw = w_raw[:, s, 0:n * P]
                pool.tensor_scalar(w_hi[:, s, 0:n * P], raw, 1.0, 0.0, ALU.mult, ALU.add)
                pool.drain()
                pool.tensor_tensor(w_lo[:, s, 0:n * P], raw, w_hi[:, s, 0:n * P], ALU.subtract).then_inc(w_split[s], 1)
                pool.wait_ge(w_split[s], ring_round(L, phase, nth + 1) + r)
                pool.sem_inc(raw_empty[s], 1)

            def split_linear(L, phase, rounds):
                with pool.Fori(0, rounds) as r:
                    for s in range(SLOTS):
                        split(L, phase, r, 0, s, TILES)

            for s in range(SLOTS):
                pool.sem_inc(w_used[s], 1)
            with pool.Fori(0, DEPTH) as L:
                pool.wait_ge(layer_free, L + 1)
                pool.sem_inc(pool_steps, 1)
                pool.memset(conv_x[:, :, :], 0.0).then_inc(halo_zero, 1)
                split_linear(L, "p1", P1_BLOCKS // SLOTS)
                pool.wait_ge(conv_in, 2 * L + 1)
                pool.sem_inc(pool_steps, 1)
                for k in range(CONV_K):
                    dst = conv_tmp[:, 0:CLEN] if k else conv_acc[:, 0, 0:CLEN]
                    pool.tensor_scalar(dst, conv_x[:, 0, k:k + CLEN], par[:, PCOL["conv_dw"] + k:PCOL["conv_dw"] + k + 1],
                                       0.0 if k else par[:, PCOL["conv_dw_b"]:PCOL["conv_dw_b"] + 1], ALU.mult, ALU.add)
                    pool.drain()
                    if k:
                        pool.tensor_tensor(conv_acc[:, 0, 0:CLEN], conv_acc[:, 0, 0:CLEN], dst, ALU.add)
                        pool.drain()
                pool.sem_inc(conv_done, 1)
                with pool.Fori(0, DC) as d:
                    for b, n in enumerate(MERGE_SIZES):
                        split(L, "merge", d * MERGE_ROUNDS, b // SLOTS, b % SLOTS, n)
                split_linear(L, "out", OUT_BLOCKS // SLOTS)
                split_linear(L, "up", UP_BLOCKS // SLOTS)
                split_linear(L, "down", DOWN_BLOCKS // SLOTS)

        @block.tensor
        def _(pe):
            def begin(L, phase, s, k):
                pe.wait_ge(set_empty[s], set_use(L, phase, s, k + 1))

            def product(L, phase, r, s, blocks, rhs, k_wait=None):
                total = sum(n for _, _, n in blocks)
                k = 0
                for b, (slot, nth, n) in enumerate(blocks):
                    pe.wait_ge(w_split[slot], ring_round(L, phase, nth + 1) + r)
                    for t in range(n):
                        if k_wait is not None:
                            k_wait(k)
                        hi, lo = rhs(k)
                        whi, wlo = w_hi[:, slot, t * P:(t + 1) * P], w_lo[:, slot, t * P:(t + 1) * P]
                        for i, (w, a) in enumerate(((whi, hi), (whi, lo), (wlo, hi))):
                            for j in range(2):
                                last = pe.matmul(ps[:, 2 * s + j, 0:HALF], w, a[:, j * HALF:(j + 1) * HALF],
                                                 start=(k == 0 and i == 0), stop=(k == total - 1 and i == 2))
                        k += 1
                    last.then_inc(set_full[s] if b == len(blocks) - 1 else w_used[slot], 1)

            def h_part(k):
                return h_hi[:, k, :], h_lo[:, k, :]

            def first_group(L, phase, rhs, k_wait):
                for k in range(DC):
                    pe.wait_ge(w_split[k % SLOTS], ring_round(L, phase, k // SLOTS + 1))
                    k_wait(k)
                    hi, lo = rhs(k)
                    for s in range(4):
                        whi, wlo = w_hi[:, k % SLOTS, s * P:(s + 1) * P], w_lo[:, k % SLOTS, s * P:(s + 1) * P]
                        for i, (w, a) in enumerate(((whi, hi), (whi, lo), (wlo, hi))):
                            for j in range(2):
                                last = pe.matmul(ps[:, 2 * s + j, 0:HALF], w, a[:, j * HALF:(j + 1) * HALF],
                                                 start=(k == 0 and i == 0), stop=(k == DC - 1 and i == 2))
                        if k == DC - 1:
                            last.then_inc(set_full[s], 1)
                    if k < DC - 1:
                        last.then_inc(w_used[k % SLOTS], 1)

            def ada(slot, use, s, signal=None):
                pe.wait_ge(ada_loaded[slot], use * 16)
                for k in range(DC):
                    last = pe.matmul(ps[:, 2 * s, HALF:HALF + 2], ada_raw[:, slot, k * P:(k + 1) * P], cond[:, k, :],
                                     start=(k == 0), stop=(k == DC - 1))
                if signal is not None:
                    last.then_inc(signal, 1)

            def two_blocks(j):
                return [((2 * j) % SLOTS, 2 * j // SLOTS, TILES), ((2 * j + 1) % SLOTS, (2 * j + 1) // SLOTS, TILES)]

            def sum_over_partitions(L, phase, s, k, n, src=sq_sum):
                begin(L, phase, s, k)
                pe.wait_ge(sum_ready, n)
                for b in range(NBLK):
                    last = pe.matmul(ps[:, 2 * s, b:b + 1], src[:, BLOCK_COL[b]:BLOCK_COL[b] + P], ones[:, 0:1],
                                     start=True, stop=True)
                last.then_inc(set_full[s], 1)

            def spread(L, phase, s, k, n, src=diag):
                begin(L, phase, s, k)
                pe.wait_ge(diag_ready, n)
                pe.matmul(ps[:, 2 * s, 0:P], ones, src[:, 0, :], start=True, stop=True)
                pe.matmul(ps[:, 2 * s + 1, :], ones, src[:, 1:NBLK, :].rearrange("p a b -> p (a b)"),
                          start=True, stop=True).then_inc(set_full[s], 1)

            def output_rms(L, phase, n_sum, n_diag):
                sum_over_partitions(L, phase, 1, 0, n_sum + 1)
                spread(L, phase, 2, 0, n_diag + 1)

            def x_rms(L, phase, k, n_diag, sq0):
                begin(L, phase, 3, 0)
                pe.matmul(ps[:, 6, 0:NBLK], ident, zeros, start=True, stop=False)
                for c in range(DC):
                    pe.wait_ge(sq_ready, L * SQ_LAYER + (sq0 + c + 1))
                    for b in range(NBLK):
                        last = pe.matmul(ps[:, 6, b:b + 1], sq[:, c % 2, BLOCK_COL[b]:BLOCK_COL[b] + P], ones[:, 0:1],
                                         start=False, stop=(c == DC - 1 and b == NBLK - 1))
                    last.then_inc(sq_used if c < DC - 1 else set_full[3], 1)
                spread(L, phase, 1, k, n_diag + 1)

            pe.wait_ge(const_in_place, 32)
            pe.wait_ge(cond_ready, 1)
            pe.wait_ge(set_empty[0], 1)
            for i in range(ADA_LOADS):
                pe.wait_ge(ada_pre_loaded[i], 16)
                for t in range(i * ADA // ADA_LOADS, (i + 1) * ADA // ADA_LOADS):
                    for k in range(DC):
                        last = pe.matmul(ps[:, 0, 2 * t:2 * t + 2], ada_pre[:, t, k * P:(k + 1) * P], cond[:, k, :],
                                         start=(k == 0), stop=(k == DC - 1))
            last.then_inc(set_full[0], 1)
            with pe.Fori(0, DEPTH) as L:
                x_rms(L, "head", 0, L * NDIAG, SQ_HEAD)

                uses = [0, 0, 0, 0]

                def p1_tile(t):
                    s = P1_SET[t]
                    begin(L, "p1", s, uses[s])
                    product(L, "p1", t // 2, s, [((2 * t) % SLOTS, 0, TILES), ((2 * t + 1) % SLOTS, 0, TILES)], h_part)
                    uses[s] += 1

                for s in range(4):
                    begin(L, "p1", s, uses[s])
                    uses[s] += 1
                first_group(L, "p1", h_part, lambda k: pe.wait_ge(h_ready, L * 2 * DC + k + 1))
                for t in range(4, 8):
                    p1_tile(t)
                sum_over_partitions(L, "p1", 0, uses[0], L * NSUM + 1)
                sum_over_partitions(L, "p1", 1, uses[1], L * NSUM + 2, sq_sum_kv)
                uses[0] += 1
                uses[1] += 1
                p1_tile(8)
                p1_tile(9)
                spread(L, "p1", 0, uses[0], L * NDIAG + 2)
                uses[0] += 1
                spread(L, "p1", 1, uses[1], L * NDIAG + 3, diag_kv)
                uses[1] += 1
                p1_tile(10)
                p1_tile(11)
                pe.wait_ge(gmlp_in, 2 * (L + 1))
                for b in range(NBLK):
                    s, bank = (0, b // 2) if b < 4 else (1, 0)
                    if b in (0, 4):
                        begin(L, "p1", s, uses[s])
                        uses[s] += 1
                    for c in range(2):
                        last = pe.transpose(ps[:, 2 * s + bank, (b % 2) * 256 + c * P:(b % 2) * 256 + (c + 1) * P],
                                            br[:, c, BLOCK_COL[b]:BLOCK_COL[b] + P], ident)
                    if b >= 3:
                        last.then_inc(set_full[s], 1)
                p1_tile(12)
                p1_tile(13)
                pe.wait_ge(ws_loaded, (L + 1) * 16)
                pe.wait_ge(gmlp_norm, L + 1)
                for c in range(2):
                    begin(L, "p1", c, uses[c])
                    uses[c] += 1
                    for b in range(NBLK):
                        for g in range(2):
                            out = ps[64 * g:64 * g + 64, 2 * c + min(b, 1), max(b - 1, 0) * P:max(b - 1, 0) * P + P]
                            last = pe.matmul(out, tok_major[:, b, c * P + 64 * g:c * P + 64 * g + 64],
                                             ws_t[:, (2 * c + g) * P:(2 * c + g + 1) * P], start=True, stop=True)
                    last.then_inc(set_full[c], 1)
                p1_tile(14)
                p1_tile(15)
                assert tuple(uses) == (6, 6, 6, 6), uses

                pe.wait_ge(qkv_ready, L + 1)
                pe.wait_ge(ctx_loaded, (L + 1) * 48)

                def expand_qk(phase, p, use, k0, k1):
                    pe.wait_ge(pw_loaded, (L * N_PAIRS + p + 1) * 16)
                    for hd in range(2):
                        pe.wait_ge(set_empty[hd], use(hd, (k0, k1)[hd]) + 1)
                        for g, (c0, n, _) in enumerate(REGIONS):
                            for k in range(QC):
                                last = pe.matmul(ps[:, 2 * hd + g, 0:n], pw[:, (3 * hd + k) * P:(3 * hd + k + 1) * P],
                                                 qa[:, k, c0:c0 + n], start=(k == 0), stop=(k == QC - 1))
                        last.then_inc(set_full[hd], 1)
                    pe.wait_ge(set_empty[0], use(0, k0 + 1) + 1)
                    for bank, (c0, n) in enumerate(((0, 512), (512, NKEY - 512))):
                        for k in range(KVC):
                            last = pe.matmul(ps[:, bank, 0:n], pw[:, (6 + k) * P:(7 + k) * P], ckv[:, k, c0:c0 + n],
                                             start=(k == 0), stop=(k == KVC - 1))
                    last.then_inc(set_full[0], 1)

                def expand_v(use, k1):
                    pe.wait_ge(set_empty[1], use(1, k1) + 1)
                    for b in range(6):
                        for k in range(KVC):
                            last = pe.matmul(ps[:, 2 + b // 4, (b % 4) * P:(b % 4 + 1) * P], ckv[:, k, b * P:(b + 1) * P],
                                             pw[:, (8 + k) * P:(9 + k) * P], start=(k == 0), stop=(k == KVC - 1))
                    last.then_inc(set_full[1], 1)

                def scores(p, i, use):
                    hd, j, s = i // 5, i % 5, i % 2
                    pe.wait_ge(set_empty[s], use(s, i // 2) + 1)
                    if j == 0:
                        pe.wait_ge(q_ready, (L * N_PAIRS + p) * 2 + (hd + 1))
                        pe.wait_ge((k_ready, k2_ready)[hd], L * N_PAIRS + p + 1)
                    if j < 4:
                        pe.matmul(ps[:, 2 * s, :], q_rot[0:QK, hd, j * P:(j + 1) * P], k_t[0:QK, hd, 0:DEC_SEQ],
                                  start=True, stop=True)
                        last = pe.matmul(ps[:, 2 * s + 1, 0:PAST], q_raw[0:QK, hd, SAMPLE0 + j * P:SAMPLE0 + (j + 1) * P],
                                         k_t[0:QK, hd, DEC_SEQ:KEYS], start=True, stop=True)
                    else:
                        last = pe.matmul(ps[:, 2 * s, 0:SEQ], q_raw[0:QK, hd, 0:SEQ], k_t[0:QK, hd, KEYS:NKEY],
                                         start=True, stop=True)
                    last.then_inc(set_full[s], 1)

                def transposes(p, i, use):
                    pe.wait_ge(set_empty[2], use(2, i) + 1)
                    pe.wait_ge(probs_ready, (L * N_PAIRS + p) * 10 + (i + 1))
                    for b in range(5 if i % 5 < 4 else 1):
                        last = pe.transpose(ps[:, 4 + b // 4, (b % 4) * P:(b % 4 + 1) * P], probs[:, i % 2, b * P:(b + 1) * P], ident)
                    last.then_inc(set_full[2], 1)

                def weighted(p, hd, use):
                    pe.wait_ge(set_empty[3], use(3, hd) + 1)
                    pe.wait_ge(pt_ready, (L * N_PAIRS + p) * 10 + 5 * (hd + 1))
                    if hd == 0:
                        pe.wait_ge(v_ready, L * N_PAIRS + p + 1)
                    vs = slice(hd * V_HEAD, (hd + 1) * V_HEAD)
                    for b in range(5):
                        pe.matmul(ps[0:V_HEAD, 7, :], v_pair[:, b, vs], probs_t[:, b, :], start=(b == 0), stop=(b == 4))
                    pe.matmul(ps[0:V_HEAD, 6, 0:SEQ], v_pair[:, 5, vs], probs_tp[:, :], start=True, stop=True).then_inc(set_full[3], 1)

                def pair(p, use, expand_next):
                    scores(p, 0, use)
                    scores(p, 1, use)
                    for i in range(10):
                        if i + 2 < 10:
                            scores(p, i + 2, use)
                        transposes(p, i, use)
                        if i == 5:
                            weighted(p, 0, use)
                    if expand_next:
                        expand_qk("pair", p + 1, use, 5, 5)
                    weighted(p, 1, use)
                    if expand_next:
                        expand_v(use, 6)

                def first_use(s, k):
                    return set_use(L, "expand", s, k)

                expand_qk("expand", 0, first_use, 0, 0)
                expand_v(first_use, 1)
                for c in range(2):
                    begin(L, "expand", 2 + c, 0)
                    pe.wait_ge(pool_ready, L * 2 + (c + 1))
                    w = tables[:, 768 + c * P:768 + (c + 1) * P]
                    for j in range(2):
                        last = pe.matmul(ps[:, 2 * (2 + c) + j, 0:HALF], w, br[:, 8 + c, j * HALF:(j + 1) * HALF], start=True, stop=True)
                    last.then_inc(set_full[2 + c], 1)
                with pe.Fori(0, N_PAIRS - 1) as p:
                    pair(p, lambda s, k: set_use(L, "pair", s, k) + p * PAIR_USES[s], True)
                pe.wait_ge(conv_done, L + 1)
                pe.wait_ge(conv1_done, L + 1)
                for b in range(NBLK):
                    s, bank = (0, b // 2) if b < 4 else (1, 0)
                    if b in (0, 4):
                        begin(L, "ln", s, 0)
                    at = 0 if b == 0 else SEQ + HALO + (b - 1) * P
                    for c in range(2):
                        last = pe.transpose(ps[:, 2 * s + bank, (b % 2) * 256 + c * P:(b % 2) * 256 + (c + 1) * P],
                                            conv_acc[:, c, at:at + P], ident)
                    if b >= 3:
                        last.then_inc(set_full[s], 1)
                pair(N_PAIRS - 1, lambda s, k: set_use(L, "lastpair", s, k), False)
                pe.wait_ge(conv_norm, L + 1)
                for c in range(2):
                    begin(L, "lnback", 2 + c, 0)
                    for b in range(NBLK):
                        last = pe.transpose(ps[:, 2 * (2 + c) + min(b, 1), max(b - 1, 0) * P:max(b - 1, 0) * P + P],
                                            conv_tok[:, b, c * P:(c + 1) * P], ident)
                    last.then_inc(set_full[2 + c], 1)

                with pe.Fori(0, DC) as d:
                    b0 = gate = 0
                    for s, half, branch in MERGE_PLAN:
                        n_blocks = 2 if branch is None else 1
                        blocks = [((b0 + i) % SLOTS, (b0 + i) // SLOTS, MERGE_SIZES[b0 + i]) for i in range(n_blocks)]
                        b0 += n_blocks
                        pe.wait_ge(set_empty[s], set_use(L, "merge", s, half + 1) + d * 2)
                        if branch is None:
                            rhs = h_part
                            if gate < ADA_SLOTS:
                                ada(gate, ada_use(L, gate, 1) + d, s)
                            gate += 1
                        else:
                            first, n = BRANCH_CHUNKS[branch]
                            pe.wait_ge(br_ready, L * 10 + BRANCH_SPLIT[branch])
                            rhs = lambda k, first=first: (br_hi[:, first + k, :], br_lo[:, first + k, :])
                        product(L, "merge", d * MERGE_ROUNDS, s, blocks, rhs)

                def merged(k):
                    return mg_hi[:, k, :], mg_lo[:, k, :]

                for s in range(4):
                    begin(L, "out", s, 0)
                ada(2, ada_use(L, 2, DC + 1), 0)
                first_group(L, "out", merged, lambda k: pe.wait_ge(mg_ready, L * DC + k + 1))
                for s in range(4):
                    begin(L, "out", s, 1)
                    if s == 0:
                        ada(2, ada_use(L, 2, DC + 2), 0)
                    product(L, "out", 2, s, two_blocks(s), merged)

                output_rms(L, "gap2", L * NSUM + 2, L * NDIAG + 3)
                x_rms(L, "gap2", 1, L * NDIAG + 4, SQ_GAP2)

                for s in range(4):
                    begin(L, "up", s, 0)
                    if s < 2:
                        ada(s, ada_use(L, s, DC + 1), s)
                first_group(L, "up", h_part, lambda k: pe.wait_ge(h_ready, L * 2 * DC + (DC + k + 1)))
                with pe.Fori(0, FFC // 2 - 1) as i:
                    for j in range(4):
                        pe.wait_ge(set_empty[j], set_use(L, "up", j, 2) + i)
                        if j < 2:
                            ada(j, ada_use(L, j, DC + 2) + i, j)
                        product(L, "up", i * 2 + 2, j, two_blocks(j), h_part)

                def down_chunk(pass_, chunk, nth, slot, par_, start, stop):
                    pe.wait_ge(w_split[slot], ring_round(L, "down", 1) + nth)
                    pe.wait_ge(a_ready, L * (2 * FFC) + chunk + 1)
                    for s in range(4):
                        if start:
                            begin(L, "down", s, pass_)
                        hi, lo = a_hi[:, par_, :], a_lo[:, par_, :]
                        whi, wlo = w_hi[:, slot, s * P:(s + 1) * P], w_lo[:, slot, s * P:(s + 1) * P]
                        for i, (w, a) in enumerate(((whi, hi), (whi, lo), (wlo, hi))):
                            for j in range(2):
                                last = pe.matmul(ps[:, 2 * s + j, 0:HALF], w, a[:, j * HALF:(j + 1) * HALF],
                                                 start=(start and i == 0), stop=(stop and i == 2))
                        if stop:
                            last.then_inc(set_full[s], 1)
                    if not stop:
                        last.then_inc(w_used[slot], 1)

                for q in range(2):
                    c0 = q * FFC
                    for k in (0, 1):
                        down_chunk(q, c0 + k, (c0 + k) // SLOTS, (c0 + k) % SLOTS, k % 2, k == 0, False)
                    with pe.Fori(0, (FFC - 6) // SLOTS) as i:
                        for k in range(2, 6):
                            down_chunk(q, i * SLOTS + (c0 + k), i + (c0 + k) // SLOTS, (c0 + k) % SLOTS, k % 2, False, False)
                    for k in range(FFC - 4, FFC):
                        down_chunk(q, c0 + k, (c0 + k) // SLOTS, (c0 + k) % SLOTS, k % 2, False, k == FFC - 1)

                output_rms(L, "tail", L * NSUM + 3, L * NDIAG + 5)

        @block.scalar
        def _(ac):
            def full(L, phase, s, k):
                ac.wait_ge(set_full[s], set_use(L, phase, s, k + 1))

            def square(dst, src, L, n, first, i=0):
                ac.wait_ge(sq_used, L * SQ_LAYER + (n + (1 if first else 0)) + i)
                ac.activation(dst, src, ACT.Square).then_inc(sq_ready, 1)

            def release_after_square(s, L, n, i=0):
                ac.wait_ge(sq_ready, L * SQ_LAYER + (n + 1) + i)
                ac.sem_inc(set_empty[s], 1)

            def chunk(t, k):
                return t[:, bass.ds(k, 1), :].rearrange("p a b -> p (a b)")

            def keep_inv_rms(L, phase, s, k, n):
                full(L, phase, s, k)
                for c0, m, g in REGIONS:
                    last = ac.activation(inv_rms[:, c0:c0 + m], region(s, g), ACT.Copy)
                last.then_inc(inv_ready, 1)
                ac.wait_ge(inv_ready, n)
                ac.sem_inc(set_empty[s], 1)

            def next_h(L, phase, k, sq0, n, n_inv):
                for c in range(DC):
                    ac.wait_ge(x_new, n * DC + (c + 1))
                    square(sq[:, c % 2, :], x[:, c, :], L, sq0 + c, c == 0)
                keep_inv_rms(L, phase, 1, k, n_inv)
                for c in range(DC):
                    ac.wait_ge(t_ready, n * DC + (c + 1))
                    for c0, m, g in REGIONS:
                        last = ac.activation(h_hi[:, c, c0:c0 + m], hx[:, c % 2, c0:c0 + m], ACT.Identity, bias=mod_b[:, c, g:g + 1])
                    last.then_inc(hi_ready, 1)

            for s in range(4):
                ac.sem_inc(set_empty[s], 1)
            ac.wait_ge(const_in_place, 32)
            ac.activation(cond_t[:, :, :], cond[:, :, :], ACT.Tanh, scale=0.5).then_inc(cond_tanh, 1)

            def load_ada(slot, row):
                ac.dma_start(ada_raw[:, slot, :], w_ada[bass.ds(row, 1)].rearrange("a p n -> (a p) n")).then_inc(ada_loaded[slot], 16)

            def keep_ada(s, dst):
                ac.activation(dst, ps[:, 2 * s, HALF:HALF + 2], ACT.Copy).then_inc(mod_ready, 1)

            def column(t, k):
                return t[:, bass.ds(k, 1), :].rearrange("p a b -> p (a b)")

            for i in range(ADA_LOADS):
                part = slice(i * ADA // ADA_LOADS, (i + 1) * ADA // ADA_LOADS)
                ac.dma_start(ada_pre[:, part, :], w_ada[part].rearrange("a p n -> p a n")).then_inc(ada_pre_loaded[i], 16)
            full(0, "head", 0, -1)
            ac.activation(mod_mix[:, :, :].rearrange("p a b -> p (a b)"), ps[:, 0, 0:2 * ADA], ACT.Copy).then_inc(mod_ready, 1)
            ac.wait_ge(mod_ready, 1)
            ac.sem_inc(mod_ready, ADA - 1)
            ac.sem_inc(set_empty[0], 1)
            ac.sem_inc(layer_free, 1)
            with ac.Fori(0, DEPTH) as L:
                next_h(L, "head", 0, SQ_HEAD, L * 2, L * NINV + 1)

                uses = [0, 0, 0, 0]

                def tile_done(t):
                    s = P1_SET[t]
                    full(L, "p1", s, uses[s])
                    if t >= 3:
                        ac.sem_inc(w_used[(2 * t + 1) % SLOTS], 1)
                    uses[s] += 1
                    return s

                for t in range(QC + KVC):
                    s = tile_done(t)
                    dst = qa[:, t, :] if t < QC else kv_raw[:, t - QC, :]
                    ac.activation(two(dst), halves(s), ACT.Copy).then_inc(p1_copied, 1)
                    square(two(sq[:, t % 2, :]), halves(s), L, SQ_P1 + t, t == 0)
                    release_after_square(s, L, SQ_P1 + t)

                def copied(s):
                    ac.wait_ge(set_empty[s], set_use(L, "p1", s, uses[s] + 1))
                    ac.sem_inc(p1_copied, 1)

                s = tile_done(5)
                ac.activation(two(kpe_raw[64:P, :]), halves(s, 64, P), ACT.Copy).then_inc(set_empty[s], 1)
                copied(s)
                for c in range(2):
                    s = tile_done(6 + c)
                    ac.activation(two(br[:, c, :]), halves(s), ACT.Gelu).then_inc(set_empty[s], 1)
                    ac.wait_ge(set_empty[s], set_use(L, "p1", s, uses[s] + 1))
                    ac.sem_inc(gmlp_in, 1)
                uses[0] += 2
                uses[1] += 2
                for c in range(2):
                    s = tile_done(8 + c)
                    ac.activation(two(br[:, 6 + c, :]), halves(s), ACT.Gelu).then_inc(set_empty[s], 1)
                for c in range(2):
                    s = tile_done(10 + 3 * c)
                    ac.activation(two(br[:, 2 + c, :]), halves(s), ACT.Tanh, scale=0.5).then_inc(set_empty[s], 1)
                    s = tile_done(11 + 3 * c)
                    ac.activation(two(br[:, 4 + c, :]), halves(s), ACT.Copy).then_inc(set_empty[s], 1)
                    copied(s)
                    s = tile_done(12 + 3 * c)
                    ac.wait_ge(pool_x_free, L * 3 + (c + 1))
                    p0, in_first = 2 * EDGE + SEQ, HALF - SAMPLE0
                    ac.activation(pool_x[:, EDGE:EDGE + SEQ], ps[:, 2 * s, 0:SEQ], ACT.Copy)
                    ac.activation(pool_x[:, p0:p0 + in_first], ps[:, 2 * s, SAMPLE0:HALF], ACT.Copy)
                    ac.activation(pool_x[:, p0 + in_first:p0 + DEC_SEQ], ps[:, 2 * s + 1, 0:DEC_SEQ - in_first], ACT.Copy)\
                        .then_inc(set_empty[s], 1)
                    copied(s)
                assert uses == [4, 4, 6, 6], uses

                ac.wait_ge(qkv_ready, L + 1)
                ac.dma_start(ckv_out[bass.ds(L, 1)].rearrange("a p c n -> (a p) c n"), ckv[:, :, KEYS:NKEY]).then_inc(qkv_out, 16)
                ac.dma_start(kpe_out[bass.ds(L, 1)].rearrange("a p n -> (a p) n"), k_t[QK_NOPE:QK, 0, KEYS:NKEY]).then_inc(qkv_out, 16)
                def expand(p, use, k):
                    n = L * N_PAIRS + p
                    for hd in range(2):
                        ac.wait_ge(set_full[hd], use(hd, k) + 1)
                        ac.activation(q_raw[:, hd, 0:SEQ], region(hd, 0), ACT.Copy, scale=SOFTMAX_SCALE)
                        ac.activation(q_raw[:, hd, SAMPLE0:SAMPLE0 + DEC_SEQ], region(hd, 1), ACT.Copy, scale=SOFTMAX_SCALE)
                        ac.activation(q_rot[0:QK_NOPE, hd, :], region(hd, 1, 0, QK_NOPE), ACT.Copy, scale=SOFTMAX_SCALE).then_inc(q_part, 1)
                        ac.wait_ge(q_part, n * 2 + (hd + 1))
                        ac.sem_inc(set_empty[hd], 1)
                    ac.wait_ge(set_full[0], use(0, k + 1) + 1)
                    ac.activation(k_t[0:QK_NOPE, 0, :], line(0, NKEY, 0, QK_NOPE), ACT.Copy).then_inc(k_ready, 1)
                    ac.wait_ge(set_full[1], use(1, k + 1) + 1)
                    ac.activation(v_pair[:, :, :].rearrange("p a b -> p (a b)"), line(1, NKEY), ACT.Copy).then_inc(v_ready, 1)
                    ac.wait_ge(v_ready, n + 1)
                    ac.sem_inc(set_empty[1], 1)
                    ac.sem_inc(pw_used, 1)

                def exp_item(p, i, use):
                    n, s, keys = (L * N_PAIRS + p) * 10 + (i + 1), i % 2, KEYS if i % 5 < 4 else SEQ
                    ac.wait_ge(max_ready, n)
                    ac.activation(probs[:, s, 0:keys], line(s, keys), ACT.Exp, bias=neg_max[:, s:s + 1],
                                  accum_out=exp_sum[:, s:s + 1]).then_inc(exp_ready, 1)
                    ac.wait_ge(exp_ready, n)
                    ac.sem_inc(set_empty[s], 1)

                def copy_item(p, i, use):
                    j = i % 5
                    ac.wait_ge(set_full[2], use(2, i) + 1)
                    if i == 0:
                        ac.wait_ge(attn_ready, (L * N_PAIRS + p) * 2 + 1)
                    if i == 5:
                        ac.wait_ge(set_full[3], use(3, 0) + 1)
                    if j < 4:
                        ac.activation(probs_t[:, :, j * P:(j + 1) * P], line(2, KEYS).rearrange("p (a b) -> p a b", a=5),
                                      ACT.Copy).then_inc(pt_ready, 1)
                    else:
                        ac.activation(probs_tp[:, :], line(2, SEQ), ACT.Copy).then_inc(pt_ready, 1)
                    ac.wait_ge(pt_ready, (L * N_PAIRS + p) * 10 + (i + 1))
                    ac.sem_inc(set_empty[2], 1)

                def pair(p, use, expand_next):
                    for i in range(11):
                        if i < 10:
                            exp_item(p, i, use)
                        if i >= 1:
                            copy_item(p, i - 1, use)
                    if expand_next:
                        expand(p + 1, use, 5)

                expand(0, lambda s, k: set_use(L, "expand", s, k), 0)
                for c in range(2):
                    full(L, "expand", 2 + c, 0)
                    ac.activation(two(br[:, 8 + c, :]), halves(2 + c), ACT.Copy, scale=par[:, PCOL["pool_scale"] + c:PCOL["pool_scale"] + c + 1])\
                        .then_inc(set_empty[2 + c], 1)
                with ac.Fori(0, N_PAIRS - 1) as p:
                    pair(p, lambda s, k: set_use(L, "pair", s, k) + p * PAIR_USES[s], True)
                pair(N_PAIRS - 1, lambda s, k: set_use(L, "lastpair", s, k), False)

                def convolution_branch():
                    for c in range(2):
                        full(L, "lnback", 2 + c, 0)
                        for c0, m, g in REGIONS:
                            last = ac.activation(br[:, 4 + c, c0:c0 + m], region(2 + c, g), ACT.Identity,
                                                 scale=par[:, PCOL["conv_ln_g"] + c:PCOL["conv_ln_g"] + c + 1],
                                                 bias=par[:, PCOL["conv_ln_b"] + c:PCOL["conv_ln_b"] + c + 1])
                        last.then_inc(set_empty[2 + c], 1)
                        ac.wait_ge(set_empty[2 + c], set_use(L, "lnback", 2 + c, 2))
                        for c0, m, g in REGIONS:
                            last = ac.activation(hx[:, c, c0:c0 + m], br[:, 4 + c, c0:c0 + m], ACT.Tanh, scale=0.5)
                        last.then_inc(conv_pre, 1)

                ac.wait_ge(attn_ready, (L + 1) * HEADS + 1)
                ac.wait_ge(qkv_out, (L + 1) * 32)
                for s in range(ADA_SLOTS):
                    load_ada(s, L * (2 * ADA) + (ADA + s))
                for n, c in enumerate(SPLIT_ORDER):
                    if n == BRANCH_SPLIT[2]:
                        convolution_branch()
                        ac.wait_ge(conv_silu, (L + 1) * 2)
                    ac.activation(br_hi[:, c, :], br[:, c, :], ACT.Copy).then_inc(br_part, 1)

                ac.wait_ge(br_ready, (L + 1) * 10)
                with ac.Fori(0, DC) as d:
                    for b, (s, k) in enumerate((s, k) for s, k, branch in MERGE_PLAN if branch is None):
                        ac.wait_ge(set_full[s], set_use(L, "merge", s, k + 1) + d * 2)
                        ac.sem_inc(w_used[GATE_LAST_SLOT[b]], 1)
                        if b < ADA_SLOTS:
                            load_ada(b, L * (2 * ADA) + (ADA + ADA_SLOTS + b) + d * ADA_SLOTS)
                            keep_ada(s, column(mod_ffn, d * ADA_SLOTS + b))
                        if b == 0:
                            ac.wait_ge(merge_sum, (L * DC + d) + 1)
                        ac.activation(two(gate_t[:, b, :]), halves(s), ACT.Tanh, scale=0.5, bias=half_gate[:, bass.ds(d + BRANCHES[b] * DC, 1)])\
                            .then_inc(gate_ready, 1)
                        ac.wait_ge(gate_ready, (L * DC + d) * 4 + (b + 1))
                        ac.sem_inc(set_empty[s], 1)
                    ac.wait_ge(merge_sum, (L * DC + d) + 2)
                    ac.activation(chunk(mg_hi, d), macc[:, :], ACT.Copy, scale=0.5).then_inc(mg_part, 1)

                ac.wait_ge(mg_ready, (L + 1) * DC)
                for i in range(2):
                    for j in range(4):
                        full(L, "out", j, i)
                        if i or j == 3:
                            ac.sem_inc(w_used[(2 * j + 1) % SLOTS], 1)
                        if j == 0:
                            if i == 0:
                                load_ada(2, L * (2 * ADA) + (2 * ADA + 3))
                            keep_ada(0, mod_mix[:, FFC + i, :])
                        ac.activation(two(yb[:, i * 4 + j, :]), halves(j), ACT.Copy)
                        square(two(sq[:, j % 2, :]), halves(j), L, SQ_OUT + 4 * i + j, False)
                        release_after_square(j, L, SQ_OUT + 4 * i + j)

                keep_inv_rms(L, "gap2", 2, 0, L * NINV + 2)
                next_h(L, "gap2", 1, SQ_GAP2, L * 2 + 1, L * NINV + 3)

                def up_step(i, first=False, last=False):
                    for j in range(4):
                        q = j // 2
                        ac.wait_ge(set_full[j], set_use(L, "up", j, 1) + i)
                        if not first or j == 3:
                            ac.sem_inc(w_used[(2 * j + 1) % SLOTS], 1)
                        if j < 2:
                            if not last:
                                load_ada(j, L * (2 * ADA) + (2 * ADA + 4 + j) + i * 2)
                            keep_ada(j, column(mod_mix, i * 2 + j))
                        if j % 2 == 0:
                            ac.wait_ge(up_conv, L * FFC + (q + 1) + i * 2)
                        ac.activation(two(up_x[:, j, 2:2 + TOK]), halves(j), ACT.Copy).then_inc(up_copied, 1)
                        ac.wait_ge(up_copied, L * (2 * FFC) + (j + 1) + i * 4)
                        ac.sem_inc(set_empty[j], 1)
                        if j % 2 == 1:
                            if last and j == 3:
                                hi_part(0, 0)
                                hi_part(1, 1)
                            ac.wait_ge(up_conv, L * FFC + (q + 3) + i * 2)
                            ac.activation(up_t[:, q, :], up_y[:, 2 * q, :], ACT.Tanh, scale=0.5).then_inc(up_tanh, 1)

                def hi_part(n, k, i=0):
                    if n >= 2:
                        ac.wait_ge(w_used[(n - 2) % SLOTS], ring_round(L, "down", (n - 2) // SLOTS + 2) + i)
                    if n < FFC:
                        ac.wait_ge(act_ready, L * FFC + (n + 1) + i * SLOTS)
                    src = act[:, k, :] if isinstance(k, int) else chunk(act, k)
                    ac.activation(a_hi[:, n % 2, :], src, ACT.Copy).then_inc(a_part, 1)

                up_step(0, first=True)
                with ac.Fori(1, FFC // 2 - 1) as i:
                    up_step(i)
                up_step(FFC // 2 - 1, last=True)

                def outputs(q):
                    for s in range(4):
                        full(L, "down", s, q)
                        if s == 3:
                            ac.sem_inc(w_used[((q + 1) * FFC - 1) % SLOTS], 1)
                        ac.activation(two(yb[:, 4 * q + s, :]), halves(s), ACT.Copy)
                        square(two(sq[:, s % 2, :]), halves(s), L, SQ_DOWN + 4 * q + s, q == 0 and s == 0)
                        release_after_square(s, L, SQ_DOWN + 4 * q + s)

                for q in range(2):
                    n0 = q * FFC
                    if q == 1:
                        hi_part(n0, 0)
                        outputs(0)
                        hi_part(n0 + 1, 1)
                    with ac.Fori(0, (FFC - 2) // SLOTS) as i:
                        for k in range(2, 2 + SLOTS):
                            hi_part(n0 + k, i * SLOTS + k, i)
                outputs(1)
                ac.sem_inc(layer_free, 1)
                keep_inv_rms(L, "tail", 2, 0, L * NINV + 4)

        @block.vector
        def _(dv):
            def full(L, phase, s, k):
                dv.wait_ge(set_full[s], set_use(L, phase, s, k + 1))

            def chunk(t, k):
                return t[:, bass.ds(k, 1), :].rearrange("p a b -> p (a b)")

            def add_square(sums, b, L, n, i=0):
                dv.wait_ge(sq_ready, L * SQ_LAYER + (n + 1) + i)
                dv.tensor_tensor(sums[:, :], sums[:, :], sq[:, b, :], ALU.add).then_inc(sq_used, 1)
                dv.drain()

            def inverse_root(src, scale):
                dv.tensor_scalar(var_e, src, scale, EPS, ALU.mult, ALU.add)
                dv.drain()
                dv.tensor_scalar(rstd.bitcast(I32), var_e.bitcast(I32), -0.5, 1597463007.0, ALU.mult, ALU.add)
                dv.drain()
                for _ in range(3):
                    dv.tensor_tensor(nw_a, rstd, rstd, ALU.mult)
                    dv.drain()
                    dv.scalar_tensor_tensor(out=nw_b, in0=nw_a, scalar=-0.5, in1=var_e, op0=ALU.mult, op1=ALU.mult)
                    dv.drain()
                    dv.scalar_tensor_tensor(out=rstd, in0=nw_b, scalar=1.5, in1=rstd, op0=ALU.add, op1=ALU.mult)
                    dv.drain()

            def diagonals(dst):
                dv.tensor_tensor(dst[:, :, :], ident[:, None, :].broadcast_to([P, NBLK, P]),
                                 rstd[:, :, None].broadcast_to([P, NBLK, P]), ALU.mult).then_inc(diag_ready, 1)

            def rms(L, phase, s, k, width, dst):
                full(L, phase, s, k)
                inverse_root(ps[:, 2 * s, 0:NBLK], 1.0 / width)
                dv.sem_inc(set_empty[s], 1)
                diagonals(dst)

            def update_x(L, phase, n_inv):
                rms(L, phase, 1, 0, D_MODEL, diag)
                dv.wait_ge(inv_ready, n_inv)
                for c in range(DC + 1):
                    if c < DC:
                        for c0, m, g in REGIONS:
                            dv.scalar_tensor_tensor(out=yb[:, c, c0:c0 + m], in0=yb[:, c, c0:c0 + m], scalar=mod_g[:, c, g:g + 1],
                                                    in1=inv_rms[:, c0:c0 + m], op0=ALU.mult, op1=ALU.mult)
                    if 1 <= c <= DC:
                        for c0, m, g in REGIONS:
                            last = dv.tensor_tensor(x[:, c - 1, c0:c0 + m], x[:, c - 1, c0:c0 + m], yb[:, c - 1, c0:c0 + m], ALU.add)
                        last.then_inc(x_new, 1)
                    dv.drain()

            def next_h(L, phase, n, n_inv, mod, ada0, pre_g, post_g):
                if phase == "head":
                    dv.wait_ge(par_loaded, (L + 1) * 32)
                    dv.tensor_scalar(half_gate[:, :], par[:, PCOL["b_gate"]:PCOL["b_gate"] + 4 * DC], 0.5, None, ALU.mult)
                dv.wait_ge(mod_ready, (n + 1) * ADA)
                bias = par[:, PCOL["ada_b"] + ada0:PCOL["ada_b"] + ada0 + ADA, None].broadcast_to([P, ADA, 2])
                dv.tensor_tensor(mod[:, :, :], mod[:, :, :], bias, ALU.add)
                dv.drain()
                g = par[:, PCOL[pre_g]:PCOL[pre_g] + DC, None].broadcast_to([P, DC, 2])
                dv.scalar_tensor_tensor(out=mod_a[:, :, :], in0=mod[:, DC:2 * DC, :], scalar=1.0, in1=g, op0=ALU.add, op1=ALU.mult)
                dv.tensor_copy(mod_b[:, :, :], mod[:, 0:DC, :])
                g = par[:, PCOL[post_g]:PCOL[post_g] + DC, None].broadcast_to([P, DC, 2])
                dv.tensor_tensor(mod_g[:, :, :], mod[:, 2 * DC:ADA, :], g, ALU.mult)
                dv.drain()
                full(L, phase, 3, 0)
                dv.sem_inc(sq_used, 1)
                rms(L, phase, 3, 0, D_MODEL, diag)
                dv.wait_ge(inv_ready, n_inv)
                for c in range(DC + 1):
                    if c < DC:
                        for c0, m, g in REGIONS:
                            last = dv.scalar_tensor_tensor(out=hx[:, c % 2, c0:c0 + m], in0=x[:, c, c0:c0 + m], scalar=mod_a[:, c, g:g + 1],
                                                           in1=inv_rms[:, c0:c0 + m], op0=ALU.mult, op1=ALU.mult)
                        last.then_inc(t_ready, 1)
                    if c >= 1:
                        dv.wait_ge(hi_ready, n * DC + c)
                        for c0, m, g in REGIONS:
                            last = dv.scalar_tensor_tensor(out=h_lo[:, c - 1, c0:c0 + m], in0=hx[:, (c - 1) % 2, c0:c0 + m],
                                                           scalar=mod_b[:, c - 1, g:g + 1], in1=h_hi[:, c - 1, c0:c0 + m],
                                                           op0=ALU.add, op1=ALU.subtract)
                        last.then_inc(h_ready, 1)
                    dv.drain()

            def layernorm(L, phase, k, dst):
                def src(b):
                    return ps[:, b // 2, (b % 2) * 256:(b % 2) * 256 + 256]
                for b in range(NBLK):
                    if b in (0, 4):
                        full(L, phase, b // 4, k)
                    dv.bn_stats(bn[:, b, :], src(b))
                dv.drain()
                for b in range(NBLK):
                    dv.bn_aggr(mean_var[:, b, :], bn[:, b, :])
                dv.drain()
                inverse_root(mean_var[:, :, 1], 1.0)
                for b in range(NBLK):
                    dv.tensor_scalar(dst[:, b, :], src(b), mean_var[:, b, 0:1], rstd[:, b:b + 1], ALU.subtract, ALU.mult)
                dv.drain()
                dv.sem_inc(set_empty[0], 1)
                dv.sem_inc(set_empty[1], 1)

            def rotate(dst, pe_rows, swapped_rows):
                dv.scalar_tensor_tensor(out=hx[64:96, 0, 0:DEC_SEQ], in0=pe_rows, scalar=1.0, in1=rope[64:96, :], op0=ALU.mult, op1=ALU.mult)
                dv.scalar_tensor_tensor(out=hx[64:96, 1, 0:DEC_SEQ], in0=swapped_rows, scalar=1.0, in1=rope[96:P, :], op0=ALU.mult, op1=ALU.mult)
                dv.drain()
                return dv.tensor_tensor(dst, hx[64:96, 0, 0:DEC_SEQ], hx[64:96, 1, 0:DEC_SEQ], ALU.add)

            dv.sem_inc(sq_used, 1)
            dv.sem_inc(attn_ready, 1)
            dv.sem_inc(merge_sum, 1)
            dv.sem_inc(up_conv, 2)
            for c in (SEQ, TOK - 2):
                dv.memset(h_hi[:, :, c:c + 2].bitcast(F32), 0.0)
                dv.memset(h_lo[:, :, c:c + 2].bitcast(F32), 0.0)
            dv.wait_ge(cond_tanh, 1)
            dv.tensor_scalar(cond_t[:, :, :], cond_t[:, :, :], 0.5, 0.5, ALU.mult, ALU.add)
            dv.drain()
            dv.tensor_tensor(cond[:, :, :], cond[:, :, :], cond_t[:, :, :], ALU.mult).then_inc(cond_ready, 1)
            dv.wait_ge(x_loaded, 16 * DC)
            dv.sem_inc(x_new, DC)

            with dv.Fori(0, DEPTH) as L:
                next_h(L, "head", L * 2, L * NINV + 1, mod_mix, 0, "pre_mix_g", "post_mix_g")

                dv.memset(sq_sum[:, :], 0.0)
                dv.memset(sq_sum_kv[:, :], 0.0)
                dv.memset(pool_x[:, :], 0.0)
                dv.drain()
                dv.sem_inc(pool_x_free, 1)
                for c in range(QC):
                    add_square(sq_sum, c % 2, L, SQ_P1 + c)
                dv.sem_inc(sum_ready, 1)
                for c in range(KVC):
                    add_square(sq_sum_kv, (QC + c) % 2, L, SQ_P1 + QC + c)
                dv.sem_inc(sum_ready, 1)
                dv.wait_ge(p1_copied, L * 10 + 6)
                rotate(k_t[64:96, 0, 0:DEC_SEQ], kpe_raw[64:96, SAMPLE0:SAMPLE0 + DEC_SEQ], kpe_raw[96:P, SAMPLE0:SAMPLE0 + DEC_SEQ])
                for hd in range(2):
                    dv.tensor_copy(k_t[64:96, hd, KEYS:NKEY], kpe_raw[64:96, 0:SEQ])
                dv.drain()
                dv.tensor_copy(k_t[64:96, 1, 0:DEC_SEQ], k_t[64:96, 0, 0:DEC_SEQ])
                rms(L, "p1", 0, 2, Q_LORA, diag)
                dv.drain()
                rms(L, "p1", 1, 2, KV_LORA, diag_kv)
                full(L, "p1", 0, 3)
                for c in range(QC):
                    for c0, m, g in REGIONS:
                        dv.scalar_tensor_tensor(out=qa[:, c, c0:c0 + m], in0=qa[:, c, c0:c0 + m], scalar=par[:, PCOL["q_norm_g"] + c:PCOL["q_norm_g"] + c + 1],
                                                in1=region(0, g), op0=ALU.mult, op1=ALU.mult)
                dv.drain()
                dv.sem_inc(set_empty[0], 1)
                full(L, "p1", 1, 3)
                for c in range(KVC):
                    for c0, m, g in REGIONS:
                        to = 0 if g else KEYS
                        dv.scalar_tensor_tensor(out=ckv[:, c, to:to + m], in0=kv_raw[:, c, c0:c0 + m], scalar=par[:, PCOL["kv_norm_g"] + c:PCOL["kv_norm_g"] + c + 1],
                                                in1=region(1, g), op0=ALU.mult, op1=ALU.mult)
                dv.drain()
                dv.sem_inc(set_empty[1], 1)
                dv.sem_inc(qkv_ready, 1)

                dv.wait_ge(halo_zero, L + 1)

                def gated_input(c):
                    dv.wait_ge(p1_copied, L * 10 + (7 + 2 * c))
                    dv.tensor_scalar(br[:, 2 + c, :], br[:, 2 + c, :], 0.5, 0.5, ALU.mult, ALU.add)
                    dv.drain()
                    for c0, m, g in REGIONS:
                        to = HALO + (SEQ + HALO) * g
                        last = dv.tensor_tensor(conv_x[:, c, to:to + m], br[:, 2 + c, c0:c0 + m], br[:, 4 + c, c0:c0 + m], ALU.mult)
                    last.then_inc(conv_in, 1)

                def pool(c):
                    dv.wait_ge(p1_copied, L * 10 + (8 + 2 * c))
                    n = PPAD
                    dv.tensor_tensor(sum_a[:, 1:n], pool_x[:, 0:n - 1], pool_x[:, 1:n], ALU.add)
                    dv.drain()
                    dv.tensor_tensor(sum_b[:, 2:n - 1], sum_a[:, 1:n - 2], sum_a[:, 3:n], ALU.add)
                    dv.drain()
                    if c == 1:
                        dv.tensor_tensor(sum_a[:, 4:n - 3], sum_b[:, 2:n - 5], sum_b[:, 6:n - 1], ALU.add)
                        dv.drain()
                        dv.tensor_tensor(sum_b[:, 8:n - 7], sum_a[:, 4:n - 11], sum_a[:, 12:n - 3], ALU.add)
                        dv.drain()
                    dv.tensor_copy(sum_a[64:P, 8:n - 8], sum_b[64:P, 8:n - 8])
                    dv.drain()
                    for g, m in enumerate((SEQ, DEC_SEQ)):
                        p0 = EDGE + (SEQ + EDGE) * g
                        for side in range(2):
                            at = p0 + side * (m - EDGE)
                            dv.tensor_tensor(sum_a[:, at:at + EDGE], sum_a[:, at:at + EDGE], edge[:, c, side, :], ALU.mult)
                    dv.drain()
                    for c0, m, g in REGIONS:
                        p0 = EDGE + (SEQ + EDGE) * g
                        dv.scalar_tensor_tensor(out=br[:, 8 + c, c0:c0 + m], in0=sum_a[:, p0:p0 + m], scalar=inv_window[:, c:c + 1],
                                                in1=pool_x[:, p0:p0 + m], op0=ALU.mult, op1=ALU.subtract)
                        dv.memset(br[:, 8 + c, c0 + m:c0 + m + 2], 0.0)
                    dv.drain()
                    dv.sem_inc(pool_ready, 1)
                    dv.sem_inc(pool_x_free, 1)

                gated_input(0)
                layernorm(L, "p1", 4, tok_major)
                for i, op in enumerate((ALU.mult, ALU.add)):
                    t = tables[:, None, i * GMLP_W:(i + 1) * GMLP_W].broadcast_to([P, NBLK, GMLP_W])
                    dv.tensor_tensor(tok_major[:, :, :], tok_major[:, :, :], t, op)
                    dv.drain()
                dv.sem_inc(gmlp_norm, 1)
                pool(0)
                for c in range(2):
                    full(L, "p1", c, 5)
                    t = tables[:, 512 + c * P:512 + (c + 1) * P]
                    dv.tensor_tensor(hx[:, c, 0:SEQ], region(c, 0), t, ALU.add)
                    dv.tensor_tensor(hx[:, c, SAMPLE0:SAMPLE0 + DEC_SEQ].rearrange("p (a b) -> p a b", a=4),
                                     region(c, 1).rearrange("p (a b) -> p a b", a=4), t[:, None, :].broadcast_to([P, 4, P]), ALU.add)
                    dv.drain()
                    dv.sem_inc(set_empty[c], 1)
                    for c0, m, g in REGIONS:
                        dv.tensor_tensor(br[:, 6 + c, c0:c0 + m], br[:, 6 + c, c0:c0 + m], hx[:, c, c0:c0 + m], ALU.mult)
                gated_input(1)
                dv.drain()
                tap1 = PCOL["conv_dw"] + CONV_K
                dv.tensor_scalar(conv_acc[:, 1, 0:CLEN], conv_x[:, 1, 0:CLEN], par[:, tap1:tap1 + 1],
                                 par[:, PCOL["conv_dw_b"] + 1:PCOL["conv_dw_b"] + 2], ALU.mult, ALU.add)
                pool(1)
                for c in (SEQ, TOK - 2):
                    dv.memset(br[:, 0:4, c:c + 2], 0.0)
                dv.drain()

                def expand(p, use, k):
                    n = L * N_PAIRS + p
                    for hd in range(2):
                        dv.wait_ge(q_part, n * 2 + (hd + 1))
                        sample = slice(SAMPLE0, SAMPLE0 + DEC_SEQ)
                        rotate(q_rot[64:96, hd, :], q_raw[64:96, hd, sample], q_raw[96:P, hd, sample])
                        dv.drain()
                        dv.sem_inc(q_ready, 1)
                    dv.wait_ge(set_full[0], use(0, k + 1) + 1)
                    dv.tensor_copy(k_t[0:QK_NOPE, 1, :], line(0, NKEY, 64, P)).then_inc(k2_ready, 1)
                    dv.wait_ge(k2_ready, n + 1)
                    dv.wait_ge(k_ready, n + 1)
                    dv.sem_inc(set_empty[0], 1)

                def max_item(p, i, use):
                    s, keys = i % 2, KEYS if i % 5 < 4 else SEQ
                    dv.wait_ge(set_full[s], use(s, i // 2) + 1)
                    dv.tensor_reduce(neg_max[:, s:s + 1], line(s, keys), AX.X, ALU.max, negate=True).then_inc(max_ready, 1)

                def normalise_item(p, i):
                    s, keys = i % 2, KEYS if i % 5 < 4 else SEQ
                    dv.wait_ge(exp_ready, (L * N_PAIRS + p) * 10 + (i + 1))
                    dv.reciprocal(inv_sum[:, s:s + 1], exp_sum[:, s:s + 1])
                    dv.drain()
                    dv.tensor_scalar(probs[:, s, 0:keys], probs[:, s, 0:keys], inv_sum[:, s:s + 1], None, ALU.mult).then_inc(probs_ready, 1)

                def head_out(p, hd, use):
                    dv.wait_ge(set_full[3], use(3, hd) + 1)
                    rows = slice(64 * hd, 64 * hd + 64)
                    for c0, m, g in REGIONS:
                        dst = br[rows, p, c0:c0 + m] if isinstance(p, int) else br[rows, bass.ds(p, 1), c0:c0 + m].rearrange("p a b -> p (a b)")
                        dv.tensor_copy(dst, region(3, g, 0, V_HEAD))
                    dv.drain()
                    dv.sem_inc(set_empty[3], 1)
                    dv.sem_inc(attn_ready, 1)

                def tap(k):
                    dv.scalar_tensor_tensor(out=conv_acc[:, 1, 0:CLEN], in0=conv_x[:, 1, bass.ds(k, CLEN)],
                                            scalar=par[:, bass.ds(k + tap1, 1)], in1=conv_acc[:, 1, 0:CLEN], op0=ALU.mult, op1=ALU.add)

                def pair(p, use, expand_next):
                    max_item(p, 0, use)
                    for i in range(10):
                        if i + 1 < 10:
                            max_item(p, i + 1, use)
                        normalise_item(p, i)
                        if expand_next:
                            tap(p * 10 + (i + 1))
                        if i == 6:
                            head_out(p, 0, use)
                    if expand_next:
                        expand(p + 1, use, 5)
                    head_out(p, 1, use)

                expand(0, lambda s, k: set_use(L, "expand", s, k), 0)
                with dv.Fori(0, N_PAIRS - 1) as p:
                    pair(p, lambda s, k: set_use(L, "pair", s, k) + p * PAIR_USES[s], True)
                assert (N_PAIRS - 1) * 10 + 1 == CONV_K
                dv.drain()
                dv.sem_inc(conv1_done, 1)
                layernorm(L, "ln", 0, conv_tok)
                dv.sem_inc(conv_norm, 1)
                pair(N_PAIRS - 1, lambda s, k: set_use(L, "lastpair", s, k), False)

                for n, c in enumerate(SPLIT_ORDER):
                    if n == BRANCH_SPLIT[2]:
                        for b in range(2):
                            dv.wait_ge(conv_pre, L * 2 + (b + 1))
                            for c0, m, g in REGIONS:
                                dv.tensor_scalar(hx[:, b, c0:c0 + m], hx[:, b, c0:c0 + m], 0.5, 0.5, ALU.mult, ALU.add)
                            dv.drain()
                            for c0, m, g in REGIONS:
                                last = dv.tensor_tensor(br[:, 4 + b, c0:c0 + m], br[:, 4 + b, c0:c0 + m], hx[:, b, c0:c0 + m], ALU.mult)
                            last.then_inc(conv_silu, 1)
                        dv.drain()
                    dv.wait_ge(br_part, L * 10 + (n + 1))
                    dv.tensor_tensor(br_lo[:, c, :], br[:, c, :], br_hi[:, c, :], ALU.subtract).then_inc(br_ready, 1)

                with dv.Fori(0, DC) as d:
                    for b, (s, k) in enumerate((s, k) for s, k, branch in MERGE_PLAN if branch is not None):
                        dv.wait_ge(set_full[s], set_use(L, "merge", s, k + 1) + d * 2)
                        dv.sem_inc(w_used[BRANCH_LAST_SLOT[b]], 1)
                        dv.wait_ge(gate_ready, (L * DC + d) * 4 + (b + 1))
                        dst = macc if b == 0 else mtmp
                        dv.scalar_tensor_tensor(out=two(dst[:, :]), in0=two(gate_t[:, b, :]), scalar=1.0, in1=halves(s),
                                                op0=ALU.add, op1=ALU.mult).then_inc(set_empty[s], 1)
                        dv.drain()
                        if b:
                            last = dv.tensor_tensor(macc[:, :], macc[:, :], mtmp[:, :], ALU.add)
                            if b == 3:
                                last.then_inc(merge_sum, 1)
                            dv.drain()
                    dv.wait_ge(mg_part, L * DC + d + 1)
                    dv.scalar_tensor_tensor(out=chunk(mg_lo, d), in0=macc[:, :], scalar=0.5, in1=chunk(mg_hi, d),
                                            op0=ALU.mult, op1=ALU.subtract).then_inc(mg_ready, 1)
                    dv.drain()

                dv.memset(sq_sum[:, :], 0.0)
                dv.drain()
                with dv.Fori(0, 2) as i:
                    for j in range(4):
                        add_square(sq_sum, j % 2, L, SQ_OUT + j, i * 4)
                dv.sem_inc(sum_ready, 1)

                update_x(L, "gap2", L * NINV + 2)
                next_h(L, "gap2", L * 2 + 1, L * NINV + 3, mod_ffn, ADA, "pre_ffn_g", "post_ffn_g")

                for j in range(4):
                    dv.memset(up_x[:, j, 0:2], 0.0)
                    dv.memset(up_x[:, j, 2 + TOK:4 + TOK], 0.0)
                dv.drain()
                def up_step(i, last_step=False):
                    for q in range(2):
                        def col(name, v, tap=0):
                            at = PCOL[name] + tap * 2 * FFC + 2 * q + v
                            return par[:, i * 4 + at:i * 4 + at + 1] if isinstance(i, int) else par[:, bass.ds(i * 4 + at, 1)]
                        if last_step and q == 1:
                            lo_part(0, 0)
                            lo_part(1, 1)
                        dv.wait_ge(up_copied, L * (2 * FFC) + (2 * q + 2) + i * 4)
                        for v in range(2):
                            j = 2 * q + v
                            dv.tensor_scalar(up_y[:, j, :], up_x[:, j, 2:2 + TOK], col("ffn_dw", v, 1), col("ffn_dw_b", v), ALU.mult, ALU.add)
                        for tap in (0, 2):
                            dv.drain()
                            for v in range(2):
                                j = 2 * q + v
                                last = dv.scalar_tensor_tensor(out=up_y[:, j, :], in0=up_x[:, j, 1 + tap:1 + tap + TOK], scalar=col("ffn_dw", v, tap),
                                                               in1=up_y[:, j, :], op0=ALU.mult, op1=ALU.add)
                        last.then_inc(up_conv, 1)
                        dv.drain()
                        dv.wait_ge(up_tanh, L * FFC + (q + 1) + i * 2)
                        dv.scalar_tensor_tensor(out=up_t[:, q, :], in0=up_t[:, q, :], scalar=1.0, in1=up_y[:, 2 * q, :], op0=ALU.add, op1=ALU.mult)
                        dv.drain()
                        dst = act[:, 2 * i + q, :] if isinstance(i, int) else chunk(act, i * 2 + q)
                        dv.scalar_tensor_tensor(out=dst, in0=up_t[:, q, :], scalar=0.5, in1=up_y[:, 2 * q + 1, :],
                                                op0=ALU.mult, op1=ALU.mult).then_inc(act_ready, 1)

                def lo_part(n, k, i=0):
                    dv.wait_ge(a_part, L * 2 * FFC + (n + 1) + i * SLOTS)
                    src = act[:, k, :] if isinstance(k, int) else chunk(act, k)
                    dv.tensor_tensor(a_lo[:, n % 2, :], src, a_hi[:, n % 2, :], ALU.subtract).then_inc(a_ready, 1)

                with dv.Fori(0, FFC // 2 - 1) as i:
                    up_step(i)
                up_step(FFC // 2 - 1, last_step=True)

                dv.memset(sq_sum[:, :], 0.0)
                dv.drain()

                for q in range(2):
                    n0 = q * FFC
                    if q == 1:
                        lo_part(n0, 0)
                        for s in range(4):
                            add_square(sq_sum, s % 2, L, SQ_DOWN + s)
                        lo_part(n0 + 1, 1)
                    with dv.Fori(0, (FFC - 2) // SLOTS) as i:
                        for k in range(2, 2 + SLOTS):
                            lo_part(n0 + k, i * SLOTS + k, i)
                for s in range(4):
                    add_square(sq_sum, s % 2, L, SQ_DOWN + 4 + s)
                dv.sem_inc(sum_ready, 1)

                update_x(L, "tail", L * NINV + 4)


def _tiles(w, cols):
    n_l, k, _ = w.shape
    t = np.stack([w[:, :, c:c + P] for c in cols], 1)
    return t.reshape(n_l, len(cols), k // P, P, P).transpose(0, 1, 3, 2, 4)


def _blocks(t):
    n_l, n, _, k, _ = t.shape
    return t.reshape(n_l, n, P, k // TILES, WBLK).transpose(0, 1, 3, 2, 4).reshape(n_l, -1, P, WBLK)


def _first_group(b, first):
    n_l = b.shape[0]
    g = b[:, first:first + 8].reshape(n_l, 4, 2, P, TILES, P).transpose(0, 2, 4, 3, 1, 5).reshape(n_l, 8, P, WBLK)
    return np.concatenate([b[:, :first], g, b[:, first + 8:]], 1)


def _columns(v):
    return v.reshape(v.shape[0], -1, P).transpose(0, 2, 1)


_SWAP = np.concatenate([np.arange(8, 16), np.arange(0, 8), np.arange(24, 32), np.arange(16, 24)])


def _const():
    c = np.zeros((P, N_CONST), np.float32)
    c[:, 0:P] = np.eye(P)
    c[:, P:2 * P] = 1.0
    t = np.arange(DEC_SEQ)
    half = QK_ROPE // 4
    inv = (np.float32(ROPE_BASE) ** (-np.arange(half, dtype=np.float32) / np.float32(half))).astype(np.float32)
    for i in range(QK_ROPE):
        pos = (t // GRID_W if i < QK_ROPE // 2 else t % GRID_W).astype(np.float32)
        ang = pos * inv[i % half]
        c[64 + i, 2 * P:2 * P + DEC_SEQ] = np.cos(ang)
        c[96 + i, 2 * P:2 * P + DEC_SEQ] = np.sin(ang) * (-1.0 if (i // half) % 2 == 0 else 1.0)
    for p in range(P):
        for k in range(2):
            w = POOL_WINDOWS[2 * k + p // 64]
            lo, hi = w // 2, w - w // 2 - 1
            for e in range(EDGE):
                base = 2 * P + DEC_SEQ + 2 * k * EDGE
                c[p, base + e] = w / (min(e, lo) + hi + 1)
                c[p, base + EDGE + e] = w / (lo + min(EDGE - 1 - e, hi) + 1)
            c[p, 2 * P + DEC_SEQ + 4 * EDGE + k] = 1.0 / w
    return c


def kernel(**inputs):
    import concourse.bacc as _bacc
    from concourse import mybir as _mybir
    from concourse.bass_utils import run_bass_kernel_spmd as _run

    a = {k: np.asarray(v) for k, v in inputs.items()}
    f = np.float32
    ld = DEPTH
    x_in = np.zeros((DC, P, TOK), f)
    x_in[:, :, 0:SEQ] = a["x_prompt"][0].T.reshape(DC, P, SEQ)
    x_in[:, :, SAMPLE0:SAMPLE0 + DEC_SEQ] = a["x_sample"][0].T.reshape(DC, P, DEC_SEQ)
    cond_in = np.stack([a["c_ctx"].reshape(DC, P).T, a["c"][0].reshape(DC, P).T], 2)

    w_in = a["w_in"]
    kpe = w_in[:, :, OFF_KPE:OFF_CONV]
    zeros = np.zeros((ld, D_MODEL, 64), f)
    kpe_tile = np.concatenate([zeros, kpe, kpe[:, :, _SWAP]], 2)
    def t(*cols):
        return _tiles(w_in, cols)
    v0, u0, x1, x2, pl = OFF_GMLP + GMLP_W, OFF_GMLP, OFF_CONV, OFF_CONV + CONV_W, OFF_POOL
    p1 = np.concatenate([t(0, P, 2 * P, OFF_KV, OFF_KV + P), _tiles(kpe_tile, [0]), t(v0, v0 + P, u0, u0 + P),
                         t(x2, x1, pl, x2 + P, x1 + P, pl + P)], 1)
    ada = _tiles(a["ada_w"], range(0, 6 * D_MODEL, P))
    up = _tiles(a["ffn_up"], [o + c * P for c in range(FFC) for o in (0, D_FF)])
    down = a["ffn_down"].reshape(ld, FFC, P, 2, 4 * P).transpose(0, 3, 1, 2, 4).reshape(ld, 2 * FFC, P, WBLK)
    w_lin = np.concatenate([_first_group(_blocks(p1), 0), _first_group(_blocks(_tiles(a["w_out"], range(0, D_MODEL, P))), 0),
                            _first_group(_blocks(up), 0), down], 1).reshape(ld * LIN_BLOCKS, P, WBLK)
    ada = ada.reshape(ld, 2 * ADA, P, D_MODEL)
    order = [0, 1, FFC, FFC + 1] + list(range(2, FFC))
    parts = [ada[0, :ADA]]
    for n in range(ld):
        after = ada[n + 1] if n + 1 < ld else np.zeros_like(ada[0])
        parts += [ada[n, ADA:], after[order]]
    w_ada = np.concatenate(parts, 0)
    gates = [_tiles(w_in, [OFF_GATE + b * D_MODEL + d * P for d in range(DC)]) for b in range(4)]
    outs = [_tiles(a[n], range(0, D_MODEL, P)) for n in ("w_o_mla", "w_conv_out", "w_gmlp_out", "w_pool_out")]
    w_merge = np.concatenate([w for b in BRANCHES for w in (gates[b], outs[b])], 3)
    w_merge = w_merge.reshape(ld * DC, P, MERGE_TILES * P)
    wq = a["w_q_b"].reshape(ld, QC, P, HEADS, QK)
    wq = np.concatenate([wq, wq[..., QK_NOPE:][..., _SWAP]], 4).transpose(0, 3, 2, 1, 4)
    wq = wq.reshape(ld, N_PAIRS, 2, P, QC * P).transpose(0, 1, 3, 2, 4).reshape(ld, N_PAIRS, P, 2 * QC * P)
    wkv = a["w_kv_b"].reshape(ld, KVC, P, N_PAIRS, 2, 2, 64).transpose(0, 3, 2, 5, 1, 4, 6)
    w_pair = np.concatenate([wq, wkv.reshape(ld, N_PAIRS, P, 4 * P)], 3).reshape(ld * N_PAIRS, P, 10 * P)

    def taps(w, order):
        return w.reshape(ld, w.shape[1], -1, P).transpose(order).reshape(ld, P, -1)

    def interleaved(v):
        return v.reshape(ld, v.shape[1], 2, FFC, P).transpose(0, 4, 1, 3, 2).reshape(ld, P, -1)

    parts = {n: _columns(a[n]) for n in ("pre_mix_g", "post_mix_g", "pre_ffn_g", "post_ffn_g", "q_norm_g", "kv_norm_g", "b_gate",
                                         "conv_dw_b", "conv_ln_g", "conv_ln_b", "pool_scale", "ada_b")}
    parts["conv_dw"] = taps(a["conv_dw"], (0, 3, 2, 1))
    parts["ffn_dw"] = interleaved(a["ffn_dw"])
    parts["ffn_dw_b"] = interleaved(a["ffn_dw_b"][:, None, :])
    params_in = np.concatenate([parts[n] for n, _ in PARAMS], 2)

    rows = np.broadcast_to(np.concatenate([a["gmlp_ln_g"], a["gmlp_ln_b"]], 1)[:, None, :], (ld, P, 2 * GMLP_W))
    bs = np.repeat(a["gmlp_bs"], 64, axis=1).reshape(ld, 2, P, P).transpose(0, 2, 1, 3).reshape(ld, P, 2 * P)
    pool_w = np.zeros((ld, P, 2, P), f)
    for g in range(4):
        o = 64 * (g % 2)
        pool_w[:, o:o + 64, g // 2, o:o + 64] = a["pool_w"][:, g]
    ws = a["gmlp_ws"].transpose(0, 3, 1, 2).reshape(ld, P, 4 * P)
    tables_in = np.concatenate([rows, bs, pool_w.reshape(ld, P, 2 * P), ws], 2)
    ctx_ckv = a["cache_ckv"][0].reshape(ld, PAST, KVC, P).transpose(0, 3, 2, 1)
    ctx_kpe = a["cache_kpe"][0].transpose(0, 2, 1)

    nc = _bacc.Bacc("TRN2", target_bir_lowering=False, num_devices=1)
    arrays, args = {}, []
    for name, v in (("x", x_in), ("cond", cond_in), ("w_ada", w_ada), ("w_lin", w_lin), ("w_merge", w_merge), ("w_pair", w_pair), ("params", params_in),
                    ("tables", tables_in), ("ctx_ckv", ctx_ckv), ("ctx_kpe", ctx_kpe), ("const", _const())):
        v = np.ascontiguousarray(v)
        arrays[f"in_{name}_dram"] = v
        args.append(nc.dram_tensor(f"in_{name}_dram", v.shape, _mybir.dt.from_np(v.dtype), kind="ExternalInput").ap())
    for name, shape in (("y", (DC, P, TOK)), ("ckv", (ld, P, KVC, SEQ)), ("kpe", (ld, QK_ROPE, SEQ))):
        args.append(nc.dram_tensor(f"out_{name}_dram", shape, F32, kind="ExternalOutput").ap())
    trunk_kernel(nc, *args)
    r = _run(nc, [arrays], core_ids=[0]).results[0]
    y = r["out_y_dram"].reshape(D_MODEL, TOK)
    y_prompt = np.ascontiguousarray(y[:, 0:SEQ].T)[None]
    y_sample = np.ascontiguousarray(y[:, SAMPLE0:SAMPLE0 + DEC_SEQ].T)[None]
    new_ckv = np.ascontiguousarray(r["out_ckv_dram"].transpose(0, 3, 2, 1).reshape(ld, SEQ, KV_LORA))[None]
    new_kpe = np.ascontiguousarray(r["out_kpe_dram"].transpose(0, 2, 1))[None]
    return y_prompt, y_sample, new_ckv, new_kpe
```

```python
from contextlib import ExitStack

import numpy as np

import concourse.bass as bass
from concourse import mybir
from concourse.alu_op_type import AluOpType as ALU

F32 = mybir.dt.float32
F32R = mybir.dt.float32r
I32 = mybir.dt.int32
ACT = mybir.ActivationFunctionType
AX = mybir.AxisListType

P = 128
DEPTH = 2
D_MODEL = 1024
DC = D_MODEL // P
SEQ, DEC_SEQ, PAST = 128, 512, 128
GRID_W = 64
HEADS, QK_NOPE, QK_ROPE, V_HEAD = 8, 64, 32, 64
QK = QK_NOPE + QK_ROPE
SOFTMAX_SCALE = QK ** -0.5
ROPE_BASE = 10000.0
Q_LORA, KV_LORA = 384, 256
QC, KVC = Q_LORA // P, KV_LORA // P
CONV_W, CONV_K = 256, 31
GMLP_W = POOL_W = 256
HALO = CONV_K // 2
D_FF = 2816
FFC = D_FF // P
EPS = 1e-6
OFF_KV = Q_LORA
OFF_KPE = OFF_KV + KV_LORA
OFF_CONV = OFF_KPE + QK_ROPE
OFF_GMLP = OFF_CONV + 2 * CONV_W
OFF_POOL = OFF_GMLP + 2 * GMLP_W
OFF_GATE = OFF_POOL + POOL_W

SAMPLE0 = SEQ + 2
TOK = SAMPLE0 + DEC_SEQ + 2
HALF = TOK // 2
REGIONS = ((0, SEQ, 0), (SAMPLE0, DEC_SEQ, 1))
NBLK = 5
BLOCK_COL = [0] + [SAMPLE0 + P * b for b in range(4)]
KEYS = DEC_SEQ + PAST
NKEY = KEYS + SEQ

SLOTS = 4
TILES = 4
WBLK = TILES * P
P1_TILES = 16
P1_BLOCKS = P1_TILES * DC // TILES
OUT_BLOCKS = DC * DC // TILES
UP_BLOCKS = 2 * FFC * DC // TILES
DOWN_BLOCKS = 2 * FFC
MERGE_SIZES = (4, 4, 4, 4, 4, 2, 4, 4, 2, 4, 4, 2)
MERGE_TILES = sum(MERGE_SIZES)
MERGE_ROUNDS = len(MERGE_SIZES) // SLOTS
RING0, RING_LAYER, LIN0, LIN_BLOCKS = {}, 0, {}, 0
for _name, _n in (("p1", P1_BLOCKS), ("merge", DC * len(MERGE_SIZES)), ("out", OUT_BLOCKS), ("up", UP_BLOCKS), ("down", DOWN_BLOCKS)):
    assert _n % SLOTS == 0
    RING0[_name] = RING_LAYER
    RING_LAYER += _n // SLOTS
    if _name != "merge":
        LIN0[_name] = LIN_BLOCKS
        LIN_BLOCKS += _n

ADA = 3 * DC
ADA_MIX, ADA_G = 2 * DC, DC
ADA_LOADS = 4
ADA_SLOTS, ADA_PARTS = 2, 3
ADA_LAYER = (2 * DC + FFC // 2 + 1, DC + FFC // 2 + 1)
assert 3 * DC == ADA and 2 + 2 * (FFC // 2 - 1) + 2 == ADA
MOD_MIX, MOD_FFN_G, MOD_FFN, MOD_MIX_G = 0, ADA_MIX, ADA, ADA + ADA_MIX

N_PAIRS = HEADS // 2
SET_ORDER = (("head", (0, 1, 0, 1)), ("p1", (6, 6, 6, 6)), ("expand", (2, 2, 1, 1)),
             ("pair", (7 * 3, 7 * 3, 10 * 3, 2 * 3)), ("ln", (0, 0, 0, 2)), ("lastpair", (5, 5, 10, 2)), ("lnback", (0, 0, 1, 1)),
             ("merge", (2 * DC,) * 4), ("out", (2,) * 4), ("gap2", (0, 2, 1, 1)), ("up", (FFC // 2,) * 4), ("down", (2,) * 4),
             ("tail", (0, 1, 1, 0)))
SET0 = {}
SET_PRE = (1, 0, 0, 0)
SET_LAYER = (0, 0, 0, 0)
for _name, _uses in SET_ORDER:
    SET0[_name] = SET_LAYER
    SET_LAYER = tuple(a + b for a, b in zip(SET_LAYER, _uses))

PAIR_USES = (7, 7, 10, 2)
P1_SET = (0, 1, 2, 3, 0, 1, 2, 3, 2, 3, 2, 3, 2, 3, 2, 3)
BRANCHES = (0, 2, 3, 1)
BRANCH_CHUNKS = ((0, 4), (6, 2), (8, 2), (4, 2))
BRANCH_SPLIT = tuple(sum(n for _, n in BRANCH_CHUNKS[:b + 1]) for b in range(4))
SPLIT_ORDER = (0, 1, 2, 3, 6, 7, 8, 9, 4, 5)
MERGE_PLAN = ((0, 0, None), (2, 0, 0), (1, 0, None), (3, 0, 1), (0, 1, None), (2, 1, 2), (1, 1, None), (3, 1, 3))
GATE_LAST_SLOT = tuple((3 * b + 1) % SLOTS for b in range(4))
BRANCH_LAST_SLOT = tuple((3 * b + 2) % SLOTS for b in range(4))
SQ_HEAD, SQ_P1, SQ_OUT, SQ_GAP2, SQ_DOWN, SQ_LAYER = 0, 8, 13, 21, 29, 37
NSUM, NDIAG, NINV = 4, 6, 4

PARAMS = (("pre_mix_g", DC), ("post_mix_g", DC), ("pre_ffn_g", DC), ("post_ffn_g", DC), ("q_norm_g", QC), ("kv_norm_g", KVC),
          ("b_gate", 4 * DC), ("conv_dw", 2 * CONV_K), ("conv_dw_b", 2), ("conv_ln_g", 2), ("conv_ln_b", 2), ("pool_scale", 2),
          ("ffn_dw", 3 * 2 * FFC), ("ffn_dw_b", 2 * FFC), ("ada_b", 48))
PCOL, NPARAM = {}, 0
for _name, _n in PARAMS:
    PCOL[_name] = NPARAM
    NPARAM += _n
TABLES = 2 * GMLP_W + 2 * P + 2 * P + 4 * P
POOL_WINDOWS = (2, 4, 8, 16)
EDGE = 8
CPAD = HALO + SEQ + HALO + DEC_SEQ + HALO
CLEN = SEQ + HALO + DEC_SEQ
N_CONST = 2 * P + DEC_SEQ + 4 * EDGE + 2 + NBLK
PPAD = EDGE + SEQ + EDGE + DEC_SEQ + EDGE


def trunk_kernel(nc, x_in, cond_in, w_ada, w_lin, w_merge, w_pair, params_in, tables_in, ctx_ckv, ctx_kpe, const_in,
                 y_out, ckv_out, kpe_out):
    with ExitStack() as ctx:
        end = [16512]

        def sb(name, words, dt=F32, at=None, shape=None):
            offset = end[0] if at is None else at
            if at is None:
                end[0] += (words * 4 + 31) // 32 * 32
            return nc.alloc_sbuf_tensor_at(name, [P] + (shape or [words]), dt, offset=offset)

        x = sb("x", DC * TOK, shape=[DC, TOK])
        h_hi = sb("h_hi", DC * TOK, F32R, shape=[DC, TOK])
        h_lo = sb("h_lo", DC * TOK, F32R, shape=[DC, TOK])
        w_raw = sb("w_raw", SLOTS * WBLK, shape=[SLOTS, WBLK])
        w_hi = sb("w_hi", SLOTS * WBLK, F32R, shape=[SLOTS, WBLK])
        w_lo = sb("w_lo", SLOTS * WBLK, F32R, shape=[SLOTS, WBLK])
        const = sb("const", N_CONST)
        ident = const[:, 0:P]
        ones = const[:, P:2 * P]
        rope = const[:, 2 * P:2 * P + DEC_SEQ]
        edge = const[:, 2 * P + DEC_SEQ:2 * P + DEC_SEQ + 4 * EDGE].rearrange("p (c s e) -> p c s e", c=2, s=2)
        inv_window = const[:, N_CONST - NBLK - 2:N_CONST - NBLK]
        zeros = const[:, N_CONST - NBLK:]
        par = sb("par", NPARAM)
        half_gate = sb("half_gate", 4 * DC)
        cond = sb("cond", 2 * DC, shape=[DC, 2])
        cond_t = sb("cond_t", 2 * DC, shape=[DC, 2])
        mod = sb("mod", 4 * ADA, shape=[2 * ADA, 2])
        mod_a = sb("mod_a", 2 * DC, shape=[DC, 2])
        mod_b = sb("mod_b", 2 * DC, shape=[DC, 2])
        mod_g = sb("mod_g", 2 * DC, shape=[DC, 2])
        small = sb("small", 96)
        var_e, rstd, nw_a, nw_b = (small[:, 8 * i:8 * i + NBLK] for i in range(4))
        neg_max, exp_sum, inv_sum = (small[:, 32 + 2 * i:34 + 2 * i] for i in range(3))
        bn = small[:, 48:48 + 6 * NBLK].rearrange("p (b n) -> p b n", b=NBLK)
        mean_var = small[:, 80:80 + 2 * NBLK].rearrange("p (b n) -> p b n", b=NBLK)
        u0 = end[0]
        U_WORDS = (nc.sbuf_usable_end - u0) // 4

        def u(name, start, words, dt=F32, shape=None):
            assert start % 8 == 0 and start + words <= U_WORDS, (name, start + words, U_WORDS)
            return sb(name, words, dt, u0 + 4 * start, shape)

        yb = u("yb", 0, DC * TOK, shape=[DC, TOK])
        qa = u("qa", 0, QC * TOK, shape=[QC, TOK])
        ckv = u("ckv", 1936, KVC * NKEY, shape=[KVC, NKEY])
        v_pair = u("v_pair", 3472, NKEY, shape=[6, P])
        q_raw = u("q_raw", 4240, 2 * TOK, shape=[2, TOK])
        q_rot = u("q_rot", 5528, 2 * DEC_SEQ, shape=[2, DEC_SEQ])
        k_t = u("k_t", 6552, 2 * NKEY, shape=[2, NKEY])
        probs = u("probs", 8088, 2 * KEYS, shape=[2, KEYS])
        probs_t = u("probs_t", 9368, 5 * DEC_SEQ, shape=[5, DEC_SEQ])
        probs_tp = u("probs_tp", 11928, SEQ)
        diag_kv = u("diag_kv", 12056, NBLK * P, shape=[NBLK, P])
        kv_raw = u("kv_raw", 9368, KVC * TOK, shape=[KVC, TOK])
        kpe_raw = u("kpe_raw", 10656, TOK)
        pool_x = u("pool_x", 8088, PPAD)
        sum_a = u("sum_a", 9368, PPAD)
        sum_b = u("sum_b", 10040, PPAD)
        sq_sum_kv = u("sq_sum_kv", 5568, TOK)
        br_hi = u("br_hi", 0, 10 * TOK, F32R, shape=[10, TOK])
        br_lo = u("br_lo", 10 * TOK, 10 * TOK, F32R, shape=[10, TOK])
        A_END = 20 * TOK
        br = u("br", A_END, 10 * TOK, shape=[10, TOK])
        conv_x = u("conv_x", A_END + 6440, 2 * 688, shape=[2, 688])
        conv_tok = u("conv_tok", A_END + 6440, NBLK * 256, shape=[NBLK, 256])
        conv_acc = u("conv_acc", A_END + 6440 + 1376, 2 * 656, shape=[2, 656])
        tables = u("tables", A_END + 9128, 1024)
        tok_major = u("tok_major", 4240, NBLK * 256, shape=[NBLK, 256])
        mg_hi = u("mg_hi", A_END, DC * TOK, F32R, shape=[DC, TOK])
        mg_lo = u("mg_lo", A_END + DC * TOK, DC * TOK, F32R, shape=[DC, TOK])
        E0 = A_END + 2 * DC * TOK
        sq = u("sq", E0, 2 * TOK, shape=[2, TOK])
        sq_sum = u("sq_sum", E0 + 2 * TOK, TOK)
        inv_rms = u("inv_rms", E0 + 2 * TOK, TOK)
        ada_pre = u("ada_pre", 0, ADA_MIX * D_MODEL, shape=[ADA_MIX, D_MODEL])
        ada_pre_part = u("ada_pre_part", ADA_MIX * D_MODEL, ADA_MIX * P, shape=[ADA_MIX // 2, 2, P])
        conv_tmp = u("conv_tmp", E0, 656)
        hx = u("hx", E0 + 1936, 2 * TOK, shape=[2, TOK])
        diag = u("diag", E0 + 3224, NBLK * P, shape=[NBLK, P])
        gate_t = u("gate_t", E0, 4 * TOK, shape=[4, TOK])
        macc = u("macc", E0 + 4 * TOK, TOK)
        mtmp = u("mtmp", E0 + 3224, TOK)
        ws_t = u("ws_t", E0 + 3872, 4 * P)
        pw = u("pw", E0 + 4512, 10 * P)
        act = u("act", DC * TOK, FFC * TOK, shape=[FFC, TOK])
        F0 = (DC + FFC) * TOK
        up_x = u("up_x", 0, 4 * 648, shape=[4, 648])
        up_y = u("up_y", E0, 4 * TOK, shape=[4, TOK])
        up_t = u("up_t", E0 + 4 * TOK, 2 * TOK, shape=[2, TOK])
        ada_raw = u("ada_raw", E0 + 3872, ADA_SLOTS * D_MODEL, shape=[ADA_SLOTS, D_MODEL])
        ada_part = u("ada_part", E0 + 3872 + ADA_SLOTS * D_MODEL, ADA_PARTS * 2 * P, shape=[ADA_PARTS, 2, P])
        a_hi = u("a_hi", F0, 2 * TOK, F32R, shape=[2, TOK])
        a_lo = u("a_lo", F0 + 2 * TOK, 2 * TOK, F32R, shape=[2, TOK])

        ps = ctx.enter_context(nc.psum_tensor("ps", [P, 8, 512], F32))

        def pset(s):
            return ps[:, 2 * s:2 * s + 2, :]

        def halves(s, lo=0, hi=P):
            return ps[lo:hi, 2 * s:2 * s + 2, 0:HALF]

        def line(s, n, lo=0, hi=P):
            return pset(s).rearrange("p a b -> p (a b)")[lo:hi, 0:n]

        def region(s, g, lo=0, hi=P):
            return ps[lo:hi, 2 * s + g, 0:(SEQ, DEC_SEQ)[g]]

        def two(ap):
            return ap.rearrange("p (a b) -> p a b", a=2)

        def sem(name):
            return ctx.enter_context(nc.semaphore(name))

        const_in_place = sem("const_in_place")
        x_loaded = sem("x_loaded")
        raw_loaded = [sem(f"raw_loaded{s}") for s in range(SLOTS)]
        raw_empty = [sem(f"raw_empty{s}") for s in range(SLOTS)]
        w_split = [sem(f"w_split{s}") for s in range(SLOTS)]
        w_used = [sem(f"w_used{s}") for s in range(SLOTS)]
        set_full = [sem(f"set_full{s}") for s in range(4)]
        set_empty = [sem(f"set_empty{s}") for s in range(4)]
        layer_free = sem("layer_free")
        par_loaded = sem("par_loaded")
        ws_loaded = sem("ws_loaded")
        ada_loaded = [sem(f"ada_loaded{s}") for s in range(ADA_SLOTS)]
        ada_pre_loaded = [sem(f"ada_pre_loaded{i}") for i in range(ADA_LOADS)]
        ada_pre_summed = sem("ada_pre_summed")
        inv_ready = sem("inv_ready")
        ada_summed = sem("ada_summed")
        mod_ready = sem("mod_ready")
        conv1_done = sem("conv1_done")
        ctx_loaded = sem("ctx_loaded")
        pw_loaded = sem("pw_loaded")
        pw_used = sem("pw_used")
        halo_zero = sem("halo_zero")
        cond_tanh = sem("cond_tanh")
        cond_ready = sem("cond_ready")
        sum_ready = sem("sum_ready")
        diag_ready = sem("diag_ready")
        x_new = sem("x_new")
        sq_ready = sem("sq_ready")
        sq_used = sem("sq_used")
        t_ready = sem("t_ready")
        hi_ready = sem("hi_ready")
        h_ready = sem("h_ready")
        p1_copied = sem("p1_copied")
        gmlp_in = sem("gmlp_in")
        gmlp_norm = sem("gmlp_norm")
        pool_x_free = sem("pool_x_free")
        pool_ready = sem("pool_ready")
        conv_in = sem("conv_in")
        conv_done = sem("conv_done")
        conv_norm = sem("conv_norm")
        conv_pre = sem("conv_pre")
        conv_silu = sem("conv_silu")
        qkv_ready = sem("qkv_ready")
        qkv_out = sem("qkv_out")
        q_part = sem("q_part")
        q_ready = sem("q_ready")
        k_ready = sem("k_ready")
        k2_ready = sem("k2_ready")
        v_ready = sem("v_ready")
        max_ready = sem("max_ready")
        exp_ready = sem("exp_ready")
        probs_ready = sem("probs_ready")
        pt_ready = sem("pt_ready")
        attn_ready = sem("attn_ready")
        br_part = sem("br_part")
        br_ready = sem("br_ready")
        gate_ready = sem("gate_ready")
        merge_sum = sem("merge_sum")
        mg_part = sem("mg_part")
        mg_ready = sem("mg_ready")
        up_copied = sem("up_copied")
        up_conv = sem("up_conv")
        up_tanh = sem("up_tanh")
        act_ready = sem("act_ready")
        a_part = sem("a_part")
        a_ready = sem("a_ready")
        pool_steps = sem("pool_steps")
        y_stored = sem("y_stored")

        def ring_round(L, phase, k):
            return L * RING_LAYER + (RING0[phase] + k)

        def set_use(L, phase, s, k):
            return L * SET_LAYER[s] + (SET_PRE[s] + SET0[phase][s] + k)

        def ada_use(L, slot, k):
            return L * ADA_LAYER[slot] + k

        def pre_tiles(i):
            t = range(i * ADA_MIX // ADA_LOADS, (i + 1) * ADA_MIX // ADA_LOADS)
            return t[0::2], t[1::2]

        def mods(L, k):
            return L * (2 * ADA) + (ADA_MIX + k)

        block = ctx.enter_context(nc.Block())

        @block.sync
        def _(sp):
            sp.dma_start(const[:, :], const_in).then_inc(const_in_place, 16)
            sp.dma_start(cond[:, :, :], cond_in).then_inc(const_in_place, 16)
            for c in range(DC):
                sp.dma_start(x[:, c, :], x_in[c]).then_inc(x_loaded, 16)

            def load_linear(L, phase, first_round, rounds):
                with sp.Fori(0, rounds) as r:
                    for s in range(SLOTS):
                        sp.wait_ge(raw_empty[s], ring_round(L, phase, first_round + 1) + r)
                        src = w_lin[bass.ds(L * LIN_BLOCKS + r * SLOTS + (LIN0[phase] + first_round * SLOTS + s), 1)]
                        sp.dma_start(w_raw[:, s, :], src.rearrange("a p n -> (a p) n")).then_inc(raw_loaded[s], 16)

            with sp.Fori(0, DEPTH) as L:
                load_linear(L, "p1", 0, 2)
                sp.wait_ge(layer_free, L + 1)
                sp.dma_start(par[:, :], params_in[bass.ds(L, 1)].rearrange("a p n -> (a p) n")).then_inc(par_loaded, 16)
                sp.dma_start(tables[:, :], tables_in[bass.ds(L, 1), :, 0:1024].rearrange("a p n -> (a p) n")).then_inc(par_loaded, 16)
                sp.wait_ge(h_ready, L * 2 * DC + DC)
                sp.dma_start(ckv[:, :, DEC_SEQ:KEYS], ctx_ckv[bass.ds(L, 1)].rearrange("a p c n -> (a p) c n")).then_inc(ctx_loaded, 16)
                for hd in range(2):
                    sp.dma_start(k_t[QK_NOPE:QK, hd, DEC_SEQ:KEYS], ctx_kpe[bass.ds(L, 1)].rearrange("a p n -> (a p) n")).then_inc(ctx_loaded, 16)
                sp.dma_start(ws_t[:, :], tables_in[bass.ds(L, 1), :, 1024:1536].rearrange("a p n -> (a p) n")).then_inc(ws_loaded, 16)
                load_linear(L, "p1", 2, P1_BLOCKS // SLOTS - 2)
                for p in range(N_PAIRS):
                    sp.wait_ge(pw_used, L * N_PAIRS + (p + 1))
                    sp.dma_start(pw[:, :], w_pair[bass.ds(L * N_PAIRS + p, 1)].rearrange("a p n -> (a p) n")).then_inc(pw_loaded, 16)
                with sp.Fori(0, DC) as d:
                    at = 0
                    for b, n in enumerate(MERGE_SIZES):
                        s, k = b % SLOTS, b // SLOTS
                        sp.wait_ge(raw_empty[s], ring_round(L, "merge", k + 1) + d * MERGE_ROUNDS)
                        src = w_merge[bass.ds(L * DC + d, 1), :, at * P:(at + n) * P]
                        sp.dma_start(w_raw[:, s, 0:n * P], src.rearrange("a p n -> (a p) n")).then_inc(raw_loaded[s], 16)
                        at += n
                load_linear(L, "out", 0, OUT_BLOCKS // SLOTS)
                load_linear(L, "up", 0, UP_BLOCKS // SLOTS)
                load_linear(L, "down", 0, DOWN_BLOCKS // SLOTS)
            for c in range(DC):
                sp.wait_ge(x_new, 2 * DC * DEPTH + c + 1)
                sp.dma_start(y_out[c], x[:, c, :]).then_inc(y_stored, 16)
            sp.wait_ge(y_stored, 16 * DC)

        @block.gpsimd
        def _(pool):
            for s in range(SLOTS):
                pool.sem_inc(raw_empty[s], 1)
            pool.sem_inc(pw_used, 1)

            def split(L, phase, r, nth, s, n):
                pool.wait_ge(raw_loaded[s], (ring_round(L, phase, nth + 1) + r) * 16)
                pool.wait_ge(w_used[s], ring_round(L, phase, nth + 1) + r)
                pool.sem_inc(pool_steps, 1)
                raw = w_raw[:, s, 0:n * P]
                pool.tensor_scalar(w_hi[:, s, 0:n * P], raw, 1.0, 0.0, ALU.mult, ALU.add)
                pool.drain()
                pool.tensor_tensor(w_lo[:, s, 0:n * P], raw, w_hi[:, s, 0:n * P], ALU.subtract).then_inc(w_split[s], 1)
                pool.wait_ge(w_split[s], ring_round(L, phase, nth + 1) + r)
                pool.sem_inc(raw_empty[s], 1)

            def split_linear(L, phase, rounds):
                with pool.Fori(0, rounds) as r:
                    for s in range(SLOTS):
                        split(L, phase, r, 0, s, TILES)

            for s in range(SLOTS):
                pool.sem_inc(w_used[s], 1)
            with pool.Fori(0, DEPTH) as L:
                pool.wait_ge(layer_free, L + 1)
                pool.sem_inc(pool_steps, 1)
                pool.memset(conv_x[:, :, :], 0.0).then_inc(halo_zero, 1)
                split_linear(L, "p1", P1_BLOCKS // SLOTS)
                pool.wait_ge(conv_in, 2 * L + 1)
                pool.sem_inc(pool_steps, 1)
                for k in range(CONV_K):
                    dst = conv_tmp[:, 0:CLEN] if k else conv_acc[:, 0, 0:CLEN]
                    pool.tensor_scalar(dst, conv_x[:, 0, k:k + CLEN], par[:, PCOL["conv_dw"] + k:PCOL["conv_dw"] + k + 1],
                                       0.0 if k else par[:, PCOL["conv_dw_b"]:PCOL["conv_dw_b"] + 1], ALU.mult, ALU.add)
                    pool.drain()
                    if k:
                        pool.tensor_tensor(conv_acc[:, 0, 0:CLEN], conv_acc[:, 0, 0:CLEN], dst, ALU.add)
                        pool.drain()
                pool.sem_inc(conv_done, 1)
                with pool.Fori(0, DC) as d:
                    for b, n in enumerate(MERGE_SIZES):
                        split(L, "merge", d * MERGE_ROUNDS, b // SLOTS, b % SLOTS, n)
                split_linear(L, "out", OUT_BLOCKS // SLOTS)
                split_linear(L, "up", UP_BLOCKS // SLOTS)
                split_linear(L, "down", DOWN_BLOCKS // SLOTS)

        @block.tensor
        def _(pe):
            def begin(L, phase, s, k):
                pe.wait_ge(set_empty[s], set_use(L, phase, s, k + 1))

            def product(L, phase, r, s, blocks, rhs, k_wait=None):
                total = sum(n for _, _, n in blocks)
                k = 0
                for b, (slot, nth, n) in enumerate(blocks):
                    pe.wait_ge(w_split[slot], ring_round(L, phase, nth + 1) + r)
                    for t in range(n):
                        if k_wait is not None:
                            k_wait(k)
                        hi, lo = rhs(k)
                        whi, wlo = w_hi[:, slot, t * P:(t + 1) * P], w_lo[:, slot, t * P:(t + 1) * P]
                        for i, (w, a) in enumerate(((whi, hi), (whi, lo), (wlo, hi))):
                            for j in range(2):
                                last = pe.matmul(ps[:, 2 * s + j, 0:HALF], w, a[:, j * HALF:(j + 1) * HALF],
                                                 start=(k == 0 and i == 0), stop=(k == total - 1 and i == 2))
                        k += 1
                    last.then_inc(set_full[s] if b == len(blocks) - 1 else w_used[slot], 1)

            def h_part(k):
                return h_hi[:, k, :], h_lo[:, k, :]

            def first_group(L, phase, rhs, k_wait):
                for k in range(DC):
                    pe.wait_ge(w_split[k % SLOTS], ring_round(L, phase, k // SLOTS + 1))
                    k_wait(k)
                    hi, lo = rhs(k)
                    for s in range(4):
                        whi, wlo = w_hi[:, k % SLOTS, s * P:(s + 1) * P], w_lo[:, k % SLOTS, s * P:(s + 1) * P]
                        for i, (w, a) in enumerate(((whi, hi), (whi, lo), (wlo, hi))):
                            for j in range(2):
                                last = pe.matmul(ps[:, 2 * s + j, 0:HALF], w, a[:, j * HALF:(j + 1) * HALF],
                                                 start=(k == 0 and i == 0), stop=(k == DC - 1 and i == 2))
                        if k == DC - 1:
                            last.then_inc(set_full[s], 1)
                    if k < DC - 1:
                        last.then_inc(w_used[k % SLOTS], 1)

            def ada(n, part, s, at=0):
                pe.wait_ge(ada_summed, n)
                for g in range(2):
                    pe.matmul(ps[:, 2 * s, HALF + at + g:HALF + at + g + 1], ada_part[:, part, g, :], ones[:, 0:1], start=True, stop=True)

            def two_blocks(j):
                return [((2 * j) % SLOTS, 2 * j // SLOTS, TILES), ((2 * j + 1) % SLOTS, (2 * j + 1) // SLOTS, TILES)]

            def sum_over_partitions(L, phase, s, k, n, src=sq_sum):
                begin(L, phase, s, k)
                pe.wait_ge(sum_ready, n)
                for b in range(NBLK):
                    last = pe.matmul(ps[:, 2 * s, b:b + 1], src[:, BLOCK_COL[b]:BLOCK_COL[b] + P], ones[:, 0:1],
                                     start=True, stop=True)
                last.then_inc(set_full[s], 1)

            def spread(L, phase, s, k, n, src=diag):
                begin(L, phase, s, k)
                pe.wait_ge(diag_ready, n)
                pe.matmul(ps[:, 2 * s, 0:P], ones, src[:, 0, :], start=True, stop=True)
                pe.matmul(ps[:, 2 * s + 1, :], ones, src[:, 1:NBLK, :].rearrange("p a b -> p (a b)"),
                          start=True, stop=True).then_inc(set_full[s], 1)

            def output_rms(L, phase, n_sum, n_diag):
                sum_over_partitions(L, phase, 1, 0, n_sum + 1)
                spread(L, phase, 2, 0, n_diag + 1)

            def x_rms(L, phase, k, n_diag, sq0):
                begin(L, phase, 3, 0)
                pe.matmul(ps[:, 6, 0:NBLK], ident, zeros, start=True, stop=False)
                for c in range(DC):
                    pe.wait_ge(sq_ready, L * SQ_LAYER + (sq0 + c + 1))
                    for b in range(NBLK):
                        last = pe.matmul(ps[:, 6, b:b + 1], sq[:, c % 2, BLOCK_COL[b]:BLOCK_COL[b] + P], ones[:, 0:1],
                                         start=False, stop=(c == DC - 1 and b == NBLK - 1))
                    last.then_inc(sq_used if c < DC - 1 else set_full[3], 1)
                spread(L, phase, 1, k, n_diag + 1)

            pe.wait_ge(const_in_place, 32)
            pe.wait_ge(cond_ready, 1)
            pe.wait_ge(set_empty[0], 1)
            for i in range(ADA_LOADS):
                pe.wait_ge(ada_pre_loaded[i], 16)
                for t in pre_tiles(i)[0]:
                    for k in range(DC):
                        last = pe.matmul(ps[:, 0, 2 * t:2 * t + 2], ada_pre[:, t, k * P:(k + 1) * P], cond[:, k, :],
                                         start=(k == 0), stop=(k == DC - 1))
            for i in range(ADA_LOADS):
                for t in pre_tiles(i)[1]:
                    n = t // 2
                    pe.wait_ge(ada_pre_summed, n + 1)
                    for g in range(2):
                        last = pe.matmul(ps[:, 0, 2 * t + g:2 * t + g + 1], ada_pre_part[:, n, g, :], ones[:, 0:1], start=True, stop=True)
            last.then_inc(set_full[0], 1)
            with pe.Fori(0, DEPTH) as L:
                x_rms(L, "head", 0, L * NDIAG, SQ_HEAD)

                uses = [0, 0, 0, 0]

                def p1_tile(t):
                    s = P1_SET[t]
                    begin(L, "p1", s, uses[s])
                    product(L, "p1", t // 2, s, [((2 * t) % SLOTS, 0, TILES), ((2 * t + 1) % SLOTS, 0, TILES)], h_part)
                    uses[s] += 1

                for s in range(4):
                    begin(L, "p1", s, uses[s])
                    uses[s] += 1
                first_group(L, "p1", h_part, lambda k: pe.wait_ge(h_ready, L * 2 * DC + k + 1))
                for t in range(4, 8):
                    p1_tile(t)
                sum_over_partitions(L, "p1", 0, uses[0], L * NSUM + 1)
                sum_over_partitions(L, "p1", 1, uses[1], L * NSUM + 2, sq_sum_kv)
                uses[0] += 1
                uses[1] += 1
                p1_tile(8)
                p1_tile(9)
                spread(L, "p1", 0, uses[0], L * NDIAG + 2)
                uses[0] += 1
                spread(L, "p1", 1, uses[1], L * NDIAG + 3, diag_kv)
                uses[1] += 1
                p1_tile(10)
                p1_tile(11)
                pe.wait_ge(gmlp_in, 2 * (L + 1))
                for b in range(NBLK):
                    s, bank = (0, b // 2) if b < 4 else (1, 0)
                    if b in (0, 4):
                        begin(L, "p1", s, uses[s])
                        uses[s] += 1
                    for c in range(2):
                        last = pe.transpose(ps[:, 2 * s + bank, (b % 2) * 256 + c * P:(b % 2) * 256 + (c + 1) * P],
                                            br[:, c, BLOCK_COL[b]:BLOCK_COL[b] + P], ident)
                    if b >= 3:
                        last.then_inc(set_full[s], 1)
                p1_tile(12)
                p1_tile(13)
                pe.wait_ge(ws_loaded, (L + 1) * 16)
                pe.wait_ge(gmlp_norm, L + 1)
                for c in range(2):
                    begin(L, "p1", c, uses[c])
                    uses[c] += 1
                    for b in range(NBLK):
                        for g in range(2):
                            out = ps[64 * g:64 * g + 64, 2 * c + min(b, 1), max(b - 1, 0) * P:max(b - 1, 0) * P + P]
                            last = pe.matmul(out, tok_major[:, b, c * P + 64 * g:c * P + 64 * g + 64],
                                             ws_t[:, (2 * c + g) * P:(2 * c + g + 1) * P], start=True, stop=True)
                    last.then_inc(set_full[c], 1)
                p1_tile(14)
                p1_tile(15)
                assert tuple(uses) == (6, 6, 6, 6), uses

                pe.wait_ge(qkv_ready, L + 1)
                pe.wait_ge(ctx_loaded, (L + 1) * 48)

                def expand_q(p, hd, use, k):
                    if hd == 0:
                        pe.wait_ge(pw_loaded, (L * N_PAIRS + p + 1) * 16)
                    pe.wait_ge(set_empty[hd], use(hd, k) + 1)
                    for g, (c0, n, _) in enumerate(REGIONS):
                        for c in range(QC):
                            last = pe.matmul(ps[:, 2 * hd + g, 0:n], pw[:, (3 * hd + c) * P:(3 * hd + c + 1) * P],
                                             qa[:, c, c0:c0 + n], start=(c == 0), stop=(c == QC - 1))
                    last.then_inc(set_full[hd], 1)

                def expand_k(use, k):
                    pe.wait_ge(set_empty[0], use(0, k) + 1)
                    for bank, (c0, n) in enumerate(((0, 512), (512, NKEY - 512))):
                        for c in range(KVC):
                            last = pe.matmul(ps[:, bank, 0:n], pw[:, (6 + c) * P:(7 + c) * P], ckv[:, c, c0:c0 + n],
                                             start=(c == 0), stop=(c == KVC - 1))
                    last.then_inc(set_full[0], 1)

                def expand_v(use, k1):
                    pe.wait_ge(set_empty[1], use(1, k1) + 1)
                    for b in range(6):
                        for k in range(KVC):
                            last = pe.matmul(ps[:, 2 + b // 4, (b % 4) * P:(b % 4 + 1) * P], ckv[:, k, b * P:(b + 1) * P],
                                             pw[:, (8 + k) * P:(9 + k) * P], start=(k == 0), stop=(k == KVC - 1))
                    last.then_inc(set_full[1], 1)

                def scores(p, i, use):
                    hd, j, s = i // 5, i % 5, i % 2
                    pe.wait_ge(set_empty[s], use(s, i // 2) + 1)
                    if j == 0:
                        pe.wait_ge(q_ready, (L * N_PAIRS + p) * 2 + (hd + 1))
                        pe.wait_ge((k_ready, k2_ready)[hd], L * N_PAIRS + p + 1)
                    if j < 4:
                        pe.matmul(ps[:, 2 * s, :], q_rot[0:QK, hd, j * P:(j + 1) * P], k_t[0:QK, hd, 0:DEC_SEQ],
                                  start=True, stop=True)
                        last = pe.matmul(ps[:, 2 * s + 1, 0:PAST], q_raw[0:QK, hd, SAMPLE0 + j * P:SAMPLE0 + (j + 1) * P],
                                         k_t[0:QK, hd, DEC_SEQ:KEYS], start=True, stop=True)
                    else:
                        last = pe.matmul(ps[:, 2 * s, 0:SEQ], q_raw[0:QK, hd, 0:SEQ], k_t[0:QK, hd, KEYS:NKEY],
                                         start=True, stop=True)
                    last.then_inc(set_full[s], 1)

                def transposes(p, i, use):
                    pe.wait_ge(set_empty[2], use(2, i) + 1)
                    pe.wait_ge(probs_ready, (L * N_PAIRS + p) * 10 + (i + 1))
                    for b in range(5 if i % 5 < 4 else 1):
                        last = pe.transpose(ps[:, 4 + b // 4, (b % 4) * P:(b % 4 + 1) * P], probs[:, i % 2, b * P:(b + 1) * P], ident)
                    last.then_inc(set_full[2], 1)

                def weighted(p, hd, use):
                    pe.wait_ge(set_empty[3], use(3, hd) + 1)
                    pe.wait_ge(pt_ready, (L * N_PAIRS + p) * 10 + 5 * (hd + 1))
                    if hd == 0:
                        pe.wait_ge(v_ready, L * N_PAIRS + p + 1)
                    vs = slice(hd * V_HEAD, (hd + 1) * V_HEAD)
                    for b in range(5):
                        pe.matmul(ps[0:V_HEAD, 7, :], v_pair[:, b, vs], probs_t[:, b, :], start=(b == 0), stop=(b == 4))
                    pe.matmul(ps[0:V_HEAD, 6, 0:SEQ], v_pair[:, 5, vs], probs_tp[:, :], start=True, stop=True).then_inc(set_full[3], 1)

                def pair(p, use, expand_next, between=None):
                    scores(p, 0, use)
                    scores(p, 1, use)
                    if between is not None:
                        between()
                    for i in range(10):
                        if i + 2 < 10:
                            scores(p, i + 2, use)
                        elif expand_next:
                            expand_q(p + 1, i - 8, use, 5)
                        transposes(p, i, use)
                        if i == 5:
                            weighted(p, 0, use)
                    if expand_next:
                        expand_k(use, 6)
                    weighted(p, 1, use)
                    if expand_next:
                        expand_v(use, 6)

                def first_use(s, k):
                    return set_use(L, "expand", s, k)

                for hd in range(2):
                    expand_q(0, hd, first_use, 0)
                expand_k(first_use, 1)
                expand_v(first_use, 1)
                for c in range(2):
                    begin(L, "expand", 2 + c, 0)
                    pe.wait_ge(pool_ready, L * 2 + (c + 1))
                    w = tables[:, 768 + c * P:768 + (c + 1) * P]
                    for j in range(2):
                        last = pe.matmul(ps[:, 2 * (2 + c) + j, 0:HALF], w, br[:, 8 + c, j * HALF:(j + 1) * HALF], start=True, stop=True)
                    last.then_inc(set_full[2 + c], 1)
                with pe.Fori(0, N_PAIRS - 1) as p:
                    pair(p, lambda s, k: set_use(L, "pair", s, k) + p * PAIR_USES[s], True)
                pe.wait_ge(conv_done, L + 1)
                pe.wait_ge(conv1_done, L + 1)

                def conv_to_tokens(k, blocks):
                    begin(L, "ln", 3, k)
                    for i, b in enumerate(blocks):
                        at = 0 if b == 0 else SEQ + HALO + (b - 1) * P
                        for c in range(2):
                            last = pe.transpose(ps[:, 6 + i // 2, (i % 2) * 256 + c * P:(i % 2) * 256 + (c + 1) * P],
                                                conv_acc[:, c, at:at + P], ident)
                    last.then_inc(set_full[3], 1)

                conv_to_tokens(0, (NBLK - 1,))
                pair(N_PAIRS - 1, lambda s, k: set_use(L, "lastpair", s, k), False, lambda: conv_to_tokens(1, range(NBLK - 1)))
                pe.wait_ge(conv_norm, L + 1)
                for c in range(2):
                    begin(L, "lnback", 2 + c, 0)
                    for b in range(NBLK):
                        last = pe.transpose(ps[:, 2 * (2 + c) + min(b, 1), max(b - 1, 0) * P:max(b - 1, 0) * P + P],
                                            conv_tok[:, b, c * P:(c + 1) * P], ident)
                    last.then_inc(set_full[2 + c], 1)

                with pe.Fori(0, DC) as d:
                    b0 = gate = 0
                    for s, half, branch in MERGE_PLAN:
                        n_blocks = 2 if branch is None else 1
                        blocks = [((b0 + i) % SLOTS, (b0 + i) // SLOTS, MERGE_SIZES[b0 + i]) for i in range(n_blocks)]
                        b0 += n_blocks
                        pe.wait_ge(set_empty[s], set_use(L, "merge", s, half + 1) + d * 2)
                        if branch is None:
                            rhs = h_part
                            if gate > 0:
                                ada(L * (2 * ADA) + gate + d * 3, gate - 1, s)
                            gate += 1
                        else:
                            first, n = BRANCH_CHUNKS[branch]
                            pe.wait_ge(br_ready, L * 10 + BRANCH_SPLIT[branch])
                            rhs = lambda k, first=first: (br_hi[:, first + k, :], br_lo[:, first + k, :])
                        product(L, "merge", d * MERGE_ROUNDS, s, blocks, rhs)

                def merged(k):
                    return mg_hi[:, k, :], mg_lo[:, k, :]

                for s in range(4):
                    begin(L, "out", s, 0)
                first_group(L, "out", merged, lambda k: pe.wait_ge(mg_ready, L * DC + k + 1))
                for s in range(4):
                    begin(L, "out", s, 1)
                    if s >= 2:
                        ada(L * (2 * ADA) + (ADA - 1 + s), s - 2, s)
                    product(L, "out", 2, s, two_blocks(s), merged)

                output_rms(L, "gap2", L * NSUM + 2, L * NDIAG + 3)
                x_rms(L, "gap2", 1, L * NDIAG + 4, SQ_GAP2)

                for s in range(4):
                    begin(L, "up", s, 0)
                first_group(L, "up", h_part, lambda k: pe.wait_ge(h_ready, L * 2 * DC + (DC + k + 1)))
                with pe.Fori(0, FFC // 2 - 1) as i:
                    for j in range(4):
                        pe.wait_ge(set_empty[j], set_use(L, "up", j, 2) + i)
                        if j == 3:
                            for t in range(2):
                                ada(L * (2 * ADA) + (ADA + 3 + t) + i * 2, t, j, 2 * t)
                        product(L, "up", i * 2 + 2, j, two_blocks(j), h_part)

                def down_chunk(pass_, chunk, nth, slot, par_, start, stop):
                    pe.wait_ge(w_split[slot], ring_round(L, "down", 1) + nth)
                    pe.wait_ge(a_ready, L * (2 * FFC) + chunk + 1)
                    for s in range(4):
                        if start:
                            begin(L, "down", s, pass_)
                            if pass_ == 1 and s < 2:
                                ada(L * (2 * ADA) + (2 * ADA - 1 + s), s, s)
                        hi, lo = a_hi[:, par_, :], a_lo[:, par_, :]
                        whi, wlo = w_hi[:, slot, s * P:(s + 1) * P], w_lo[:, slot, s * P:(s + 1) * P]
                        for i, (w, a) in enumerate(((whi, hi), (whi, lo), (wlo, hi))):
                            for j in range(2):
                                last = pe.matmul(ps[:, 2 * s + j, 0:HALF], w, a[:, j * HALF:(j + 1) * HALF],
                                                 start=(start and i == 0), stop=(stop and i == 2))
                        if stop:
                            last.then_inc(set_full[s], 1)
                    if not stop:
                        last.then_inc(w_used[slot], 1)

                for q in range(2):
                    c0 = q * FFC
                    for k in (0, 1):
                        down_chunk(q, c0 + k, (c0 + k) // SLOTS, (c0 + k) % SLOTS, k % 2, k == 0, False)
                    with pe.Fori(0, (FFC - 6) // SLOTS) as i:
                        for k in range(2, 6):
                            down_chunk(q, i * SLOTS + (c0 + k), i + (c0 + k) // SLOTS, (c0 + k) % SLOTS, k % 2, False, False)
                    for k in range(FFC - 4, FFC):
                        down_chunk(q, c0 + k, (c0 + k) // SLOTS, (c0 + k) % SLOTS, k % 2, False, k == FFC - 1)

                output_rms(L, "tail", L * NSUM + 3, L * NDIAG + 5)

        @block.scalar
        def _(ac):
            def full(L, phase, s, k):
                ac.wait_ge(set_full[s], set_use(L, phase, s, k + 1))

            def square(dst, src, L, n, first, i=0):
                ac.wait_ge(sq_used, L * SQ_LAYER + (n + (1 if first else 0)) + i)
                ac.activation(dst, src, ACT.Square).then_inc(sq_ready, 1)

            def release_after_square(s, L, n, i=0):
                ac.wait_ge(sq_ready, L * SQ_LAYER + (n + 1) + i)
                ac.sem_inc(set_empty[s], 1)

            def chunk(t, k):
                return t[:, bass.ds(k, 1), :].rearrange("p a b -> p (a b)")

            def keep_inv_rms(L, phase, s, k, n):
                full(L, phase, s, k)
                for c0, m, g in REGIONS:
                    last = ac.activation(inv_rms[:, c0:c0 + m], region(s, g), ACT.Copy)
                last.then_inc(inv_ready, 1)
                ac.wait_ge(inv_ready, n)
                ac.sem_inc(set_empty[s], 1)

            def next_h(L, phase, k, sq0, n, n_inv):
                for c in range(DC):
                    ac.wait_ge(x_new, n * DC + (c + 1))
                    square(sq[:, c % 2, :], x[:, c, :], L, sq0 + c, c == 0)
                keep_inv_rms(L, phase, 1, k, n_inv)
                for c in range(DC):
                    ac.wait_ge(t_ready, n * DC + (c + 1))
                    for c0, m, g in REGIONS:
                        last = ac.activation(h_hi[:, c, c0:c0 + m], hx[:, c % 2, c0:c0 + m], ACT.Identity, bias=mod_b[:, c, g:g + 1])
                    last.then_inc(hi_ready, 1)

            for s in range(4):
                ac.sem_inc(set_empty[s], 1)
            ac.wait_ge(const_in_place, 32)
            ac.activation(cond_t[:, :, :], cond[:, :, :], ACT.Tanh, scale=0.5).then_inc(cond_tanh, 1)

            def load_ada(slot, L, n, i=0):
                row = L * (2 * ADA) + (ADA_MIX + n) + i
                ac.dma_start(ada_raw[:, slot, :], w_ada[bass.ds(row, 1)].rearrange("a p n -> (a p) n")).then_inc(ada_loaded[slot], 16)

            def keep_ada(s, dst, at=0):
                ac.activation(dst, ps[:, 2 * s, HALF + at:HALF + at + 2], ACT.Copy).then_inc(mod_ready, 1)

            def column(t, k):
                return t[:, bass.ds(k, 1), :].rearrange("p a b -> p (a b)")

            for i in range(ADA_LOADS):
                part = slice(i * ADA_MIX // ADA_LOADS, (i + 1) * ADA_MIX // ADA_LOADS)
                ac.dma_start(ada_pre[:, part, :], w_ada[part].rearrange("a p n -> p a n")).then_inc(ada_pre_loaded[i], 16)
            full(0, "head", 0, -1)
            ac.activation(mod[:, 0:ADA_MIX, :].rearrange("p a b -> p (a b)"), ps[:, 0, 0:2 * ADA_MIX], ACT.Copy).then_inc(mod_ready, 1)
            ac.wait_ge(mod_ready, 1)
            ac.sem_inc(mod_ready, ADA_MIX - 1)
            ac.sem_inc(set_empty[0], 1)
            ac.sem_inc(layer_free, 1)
            with ac.Fori(0, DEPTH) as L:
                next_h(L, "head", 0, SQ_HEAD, L * 2, L * NINV + 1)

                uses = [0, 0, 0, 0]

                def tile_done(t):
                    s = P1_SET[t]
                    full(L, "p1", s, uses[s])
                    if t >= 3:
                        ac.sem_inc(w_used[(2 * t + 1) % SLOTS], 1)
                    uses[s] += 1
                    return s

                for t in range(QC + KVC):
                    s = tile_done(t)
                    dst = qa[:, t, :] if t < QC else kv_raw[:, t - QC, :]
                    ac.activation(two(dst), halves(s), ACT.Copy).then_inc(p1_copied, 1)
                    square(two(sq[:, t % 2, :]), halves(s), L, SQ_P1 + t, t == 0)
                    release_after_square(s, L, SQ_P1 + t)

                def copied(s):
                    ac.wait_ge(set_empty[s], set_use(L, "p1", s, uses[s] + 1))
                    ac.sem_inc(p1_copied, 1)

                s = tile_done(5)
                ac.activation(two(kpe_raw[64:P, :]), halves(s, 64, P), ACT.Copy).then_inc(set_empty[s], 1)
                copied(s)
                for c in range(2):
                    s = tile_done(6 + c)
                    ac.activation(two(br[:, c, :]), halves(s), ACT.Gelu).then_inc(set_empty[s], 1)
                    ac.wait_ge(set_empty[s], set_use(L, "p1", s, uses[s] + 1))
                    ac.sem_inc(gmlp_in, 1)
                uses[0] += 2
                uses[1] += 2
                for c in range(2):
                    s = tile_done(8 + c)
                    ac.activation(two(br[:, 6 + c, :]), halves(s), ACT.Gelu).then_inc(set_empty[s], 1)
                for c in range(2):
                    s = tile_done(10 + 3 * c)
                    ac.activation(two(br[:, 2 + c, :]), halves(s), ACT.Tanh, scale=0.5).then_inc(set_empty[s], 1)
                    s = tile_done(11 + 3 * c)
                    ac.activation(two(br[:, 4 + c, :]), halves(s), ACT.Copy).then_inc(set_empty[s], 1)
                    copied(s)
                    s = tile_done(12 + 3 * c)
                    ac.wait_ge(pool_x_free, L * 3 + (c + 1))
                    p0, in_first = 2 * EDGE + SEQ, HALF - SAMPLE0
                    ac.activation(pool_x[:, EDGE:EDGE + SEQ], ps[:, 2 * s, 0:SEQ], ACT.Copy)
                    ac.activation(pool_x[:, p0:p0 + in_first], ps[:, 2 * s, SAMPLE0:HALF], ACT.Copy)
                    ac.activation(pool_x[:, p0 + in_first:p0 + DEC_SEQ], ps[:, 2 * s + 1, 0:DEC_SEQ - in_first], ACT.Copy)\
                        .then_inc(set_empty[s], 1)
                    copied(s)
                assert uses == [4, 4, 6, 6], uses

                ac.wait_ge(qkv_ready, L + 1)
                ac.dma_start(ckv_out[bass.ds(L, 1)].rearrange("a p c n -> (a p) c n"), ckv[:, :, KEYS:NKEY]).then_inc(qkv_out, 16)
                ac.dma_start(kpe_out[bass.ds(L, 1)].rearrange("a p n -> (a p) n"), k_t[QK_NOPE:QK, 0, KEYS:NKEY]).then_inc(qkv_out, 16)
                def expanded_q(p, hd, use, k):
                    n = L * N_PAIRS + p
                    ac.wait_ge(set_full[hd], use(hd, k) + 1)
                    ac.activation(q_raw[:, hd, 0:SEQ], region(hd, 0), ACT.Copy, scale=SOFTMAX_SCALE)
                    ac.activation(q_raw[:, hd, SAMPLE0:SAMPLE0 + DEC_SEQ], region(hd, 1), ACT.Copy, scale=SOFTMAX_SCALE)
                    ac.activation(q_rot[0:QK_NOPE, hd, :], region(hd, 1, 0, QK_NOPE), ACT.Copy, scale=SOFTMAX_SCALE).then_inc(q_part, 1)
                    ac.wait_ge(q_part, n * 2 + (hd + 1))
                    ac.sem_inc(set_empty[hd], 1)

                def expanded_kv(p, use, k):
                    n = L * N_PAIRS + p
                    ac.wait_ge(set_full[0], use(0, k) + 1)
                    ac.activation(k_t[0:QK_NOPE, 0, :], line(0, NKEY, 0, QK_NOPE), ACT.Copy).then_inc(k_ready, 1)
                    ac.wait_ge(set_full[1], use(1, k) + 1)
                    ac.activation(v_pair[:, :, :].rearrange("p a b -> p (a b)"), line(1, NKEY), ACT.Copy).then_inc(v_ready, 1)
                    ac.wait_ge(v_ready, n + 1)
                    ac.sem_inc(set_empty[1], 1)
                    ac.sem_inc(pw_used, 1)

                def exp_item(p, i, use):
                    n, s, keys = (L * N_PAIRS + p) * 10 + (i + 1), i % 2, KEYS if i % 5 < 4 else SEQ
                    ac.wait_ge(max_ready, n)
                    ac.activation(probs[:, s, 0:keys], line(s, keys), ACT.Exp, bias=neg_max[:, s:s + 1],
                                  accum_out=exp_sum[:, s:s + 1]).then_inc(exp_ready, 1)
                    ac.wait_ge(exp_ready, n)
                    ac.sem_inc(set_empty[s], 1)

                def copy_item(p, i, use):
                    j = i % 5
                    ac.wait_ge(set_full[2], use(2, i) + 1)
                    if i == 0:
                        ac.wait_ge(attn_ready, (L * N_PAIRS + p) * 2 + 1)
                    if i == 5:
                        ac.wait_ge(set_full[3], use(3, 0) + 1)
                    if j < 4:
                        ac.activation(probs_t[:, :, j * P:(j + 1) * P], line(2, KEYS).rearrange("p (a b) -> p a b", a=5),
                                      ACT.Copy).then_inc(pt_ready, 1)
                    else:
                        ac.activation(probs_tp[:, :], line(2, SEQ), ACT.Copy).then_inc(pt_ready, 1)
                    ac.wait_ge(pt_ready, (L * N_PAIRS + p) * 10 + (i + 1))
                    ac.sem_inc(set_empty[2], 1)

                def pair(p, use, expand_next):
                    for i in range(11):
                        if i < 10:
                            exp_item(p, i, use)
                        if i >= 1:
                            copy_item(p, i - 1, use)
                        if i >= 9 and expand_next:
                            expanded_q(p + 1, i - 9, use, 5)
                    if expand_next:
                        expanded_kv(p + 1, use, 6)

                def first_use(s, k):
                    return set_use(L, "expand", s, k)

                for hd in range(2):
                    expanded_q(0, hd, first_use, 0)
                expanded_kv(0, first_use, 1)
                for c in range(2):
                    full(L, "expand", 2 + c, 0)
                    ac.activation(two(br[:, 8 + c, :]), halves(2 + c), ACT.Copy, scale=par[:, PCOL["pool_scale"] + c:PCOL["pool_scale"] + c + 1])\
                        .then_inc(set_empty[2 + c], 1)
                with ac.Fori(0, N_PAIRS - 1) as p:
                    pair(p, lambda s, k: set_use(L, "pair", s, k) + p * PAIR_USES[s], True)
                pair(N_PAIRS - 1, lambda s, k: set_use(L, "lastpair", s, k), False)

                def convolution_branch():
                    for c in range(2):
                        full(L, "lnback", 2 + c, 0)
                        for c0, m, g in REGIONS:
                            last = ac.activation(br[:, 4 + c, c0:c0 + m], region(2 + c, g), ACT.Identity,
                                                 scale=par[:, PCOL["conv_ln_g"] + c:PCOL["conv_ln_g"] + c + 1],
                                                 bias=par[:, PCOL["conv_ln_b"] + c:PCOL["conv_ln_b"] + c + 1])
                        last.then_inc(set_empty[2 + c], 1)
                        ac.wait_ge(set_empty[2 + c], set_use(L, "lnback", 2 + c, 2))
                        for c0, m, g in REGIONS:
                            last = ac.activation(hx[:, c, c0:c0 + m], br[:, 4 + c, c0:c0 + m], ACT.Tanh, scale=0.5)
                        last.then_inc(conv_pre, 1)

                ac.wait_ge(attn_ready, (L + 1) * HEADS + 1)
                ac.wait_ge(qkv_out, (L + 1) * 32)
                for s in range(ADA_SLOTS):
                    load_ada(s, L, s)
                for n, c in enumerate(SPLIT_ORDER):
                    if n == BRANCH_SPLIT[2]:
                        convolution_branch()
                        ac.wait_ge(conv_silu, (L + 1) * 2)
                    ac.activation(br_hi[:, c, :], br[:, c, :], ACT.Copy).then_inc(br_part, 1)

                ac.wait_ge(br_ready, (L + 1) * 10)
                with ac.Fori(0, DC) as d:
                    for b, (s, k) in enumerate((s, k) for s, k, branch in MERGE_PLAN if branch is None):
                        ac.wait_ge(set_full[s], set_use(L, "merge", s, k + 1) + d * 2)
                        ac.sem_inc(w_used[GATE_LAST_SLOT[b]], 1)
                        if b > 0:
                            load_ada((0, 1, 0)[b - 1], L, (2, 4, 3)[b - 1], d * 3)
                            keep_ada(s, column(mod, d * 3 + (ADA + b - 1)))
                        if b == 0:
                            ac.wait_ge(merge_sum, (L * DC + d) + 1)
                        ac.activation(two(gate_t[:, b, :]), halves(s), ACT.Tanh, scale=0.5, bias=half_gate[:, bass.ds(d + BRANCHES[b] * DC, 1)])\
                            .then_inc(gate_ready, 1)
                        ac.wait_ge(gate_ready, (L * DC + d) * 4 + (b + 1))
                        ac.sem_inc(set_empty[s], 1)
                    ac.wait_ge(merge_sum, (L * DC + d) + 2)
                    ac.activation(chunk(mg_hi, d), macc[:, :], ACT.Copy, scale=0.5).then_inc(mg_part, 1)

                ac.wait_ge(mg_ready, (L + 1) * DC)
                for i in range(2):
                    for j in range(4):
                        full(L, "out", j, i)
                        if i or j == 3:
                            ac.sem_inc(w_used[(2 * j + 1) % SLOTS], 1)
                        if i == 1 and j >= 2:
                            load_ada(j - 2, L, ADA + j)
                            keep_ada(j, mod[:, FFC + j - 2, :])
                        square(two(sq[:, j % 2, :]), halves(j), L, SQ_OUT + 4 * i + j, False)
                        ac.activation(two(yb[:, i * 4 + j, :]), halves(j), ACT.Copy).then_inc(set_empty[j], 1)

                keep_inv_rms(L, "gap2", 2, 0, L * NINV + 2)
                next_h(L, "gap2", 1, SQ_GAP2, L * 2 + 1, L * NINV + 3)

                def up_step(i, first=False, last=False):
                    for j in range(4):
                        q = j // 2
                        if last and j == 3:
                            hi_part(0, 0)
                            hi_part(1, 1)
                        ac.wait_ge(set_full[j], set_use(L, "up", j, 1) + i)
                        if not first or j == 3:
                            ac.sem_inc(w_used[(2 * j + 1) % SLOTS], 1)
                        if j == 3 and not first:
                            for t in range(2):
                                load_ada(t, L, ADA + 2 + t, i * 2)
                                keep_ada(j, column(mod, i * 2 + t), 2 * t)
                        if j % 2 == 0:
                            ac.wait_ge(up_conv, L * FFC + (q + 1) + i * 2)
                        ac.activation(two(up_x[:, j, 2:2 + TOK]), halves(j), ACT.Copy).then_inc(up_copied, 1)
                        ac.wait_ge(up_copied, L * (2 * FFC) + (j + 1) + i * 4)
                        ac.sem_inc(set_empty[j], 1)
                        if j % 2 == 1:
                            if last and j == 3:
                                hi_part(2, 2)
                            ac.wait_ge(up_conv, L * FFC + (q + 3) + i * 2)
                            ac.activation(up_t[:, q, :], up_y[:, 2 * q, :], ACT.Tanh, scale=0.5).then_inc(up_tanh, 1)

                def hi_part(n, k, i=0):
                    if n >= 2:
                        ac.wait_ge(w_used[(n - 2) % SLOTS], ring_round(L, "down", (n - 2) // SLOTS + 2) + i)
                    if n < FFC:
                        ac.wait_ge(act_ready, L * FFC + (n + 1) + i * SLOTS)
                    src = act[:, k, :] if isinstance(k, int) else chunk(act, k)
                    ac.activation(a_hi[:, n % 2, :], src, ACT.Copy).then_inc(a_part, 1)

                up_step(0, first=True)
                with ac.Fori(1, FFC // 2 - 1) as i:
                    up_step(i)
                up_step(FFC // 2 - 1, last=True)

                def outputs(q):
                    for s in range(4):
                        full(L, "down", s, q)
                        if s == 3:
                            ac.sem_inc(w_used[((q + 1) * FFC - 1) % SLOTS], 1)
                        if q == 1 and s < 2:
                            keep_ada(s, mod[:, s, :])
                        square(two(sq[:, s % 2, :]), halves(s), L, SQ_DOWN + 4 * q + s, q == 0 and s == 0)
                        ac.activation(two(yb[:, 4 * q + s, :]), halves(s), ACT.Copy).then_inc(set_empty[s], 1)

                for q in range(2):
                    n0 = q * FFC
                    if q == 1:
                        hi_part(n0, 0)
                        outputs(0)
                        hi_part(n0 + 1, 1)
                    for k in range(2 if q else 3, 2 + SLOTS):
                        hi_part(n0 + k, k)
                    with ac.Fori(1, (FFC - 2) // SLOTS) as i:
                        for k in range(2, 2 + SLOTS):
                            hi_part(n0 + k, i * SLOTS + k, i)
                outputs(1)
                ac.sem_inc(layer_free, 1)
                keep_inv_rms(L, "tail", 2, 0, L * NINV + 4)

        @block.vector
        def _(dv):
            def full(L, phase, s, k):
                dv.wait_ge(set_full[s], set_use(L, phase, s, k + 1))

            def chunk(t, k):
                return t[:, bass.ds(k, 1), :].rearrange("p a b -> p (a b)")

            def add_square(sums, b, L, n, i=0):
                dv.wait_ge(sq_ready, L * SQ_LAYER + (n + 1) + i)
                dv.tensor_tensor(sums[:, :], sums[:, :], sq[:, b, :], ALU.add).then_inc(sq_used, 1)
                dv.drain()

            def inverse_root(src, scale):
                dv.tensor_scalar(var_e, src, scale, EPS, ALU.mult, ALU.add)
                dv.drain()
                dv.tensor_scalar(rstd.bitcast(I32), var_e.bitcast(I32), -0.5, 1597463007.0, ALU.mult, ALU.add)
                dv.drain()
                for _ in range(3):
                    dv.tensor_tensor(nw_a, rstd, rstd, ALU.mult)
                    dv.drain()
                    dv.scalar_tensor_tensor(out=nw_b, in0=nw_a, scalar=-0.5, in1=var_e, op0=ALU.mult, op1=ALU.mult)
                    dv.drain()
                    dv.scalar_tensor_tensor(out=rstd, in0=nw_b, scalar=1.5, in1=rstd, op0=ALU.add, op1=ALU.mult)
                    dv.drain()

            def diagonals(dst):
                dv.tensor_tensor(dst[:, :, :], ident[:, None, :].broadcast_to([P, NBLK, P]),
                                 rstd[:, :, None].broadcast_to([P, NBLK, P]), ALU.mult).then_inc(diag_ready, 1)

            def rms(L, phase, s, k, width, dst):
                full(L, phase, s, k)
                inverse_root(ps[:, 2 * s, 0:NBLK], 1.0 / width)
                dv.sem_inc(set_empty[s], 1)
                diagonals(dst)

            def sum_tiles(tiles, signal, chunks=(0, DC)):
                for k in range(*chunks):
                    for w, acc in tiles:
                        for g in range(2):
                            if k == 0:
                                last = dv.tensor_scalar(acc[:, g, :], w[:, k * P:(k + 1) * P], cond[:, k, g:g + 1], None, ALU.mult)
                            else:
                                last = dv.scalar_tensor_tensor(out=acc[:, g, :], in0=w[:, k * P:(k + 1) * P], scalar=cond[:, k, g:g + 1],
                                                               in1=acc[:, g, :], op0=ALU.mult, op1=ALU.add)
                        if k == DC - 1:
                            last.then_inc(signal, 1)
                    if k < DC - 1:
                        dv.drain()

            def ada(slot, use, part, chunks=(0, DC)):
                if chunks[0] == 0:
                    dv.wait_ge(ada_loaded[slot], use * 16)
                sum_tiles([(ada_raw[:, slot, :], ada_part[:, part, :, :])], ada_summed, chunks)

            def both_slots(use):
                for slot in range(2):
                    dv.wait_ge(ada_loaded[slot], use(slot) * 16)
                sum_tiles([(ada_raw[:, slot, :], ada_part[:, slot, :, :]) for slot in range(2)], ada_summed)

            def output_gain(tile, ada_tile, post_g):
                bias = par[:, PCOL["ada_b"] + ada_tile:PCOL["ada_b"] + ada_tile + ADA_G, None].broadcast_to([P, ADA_G, 2])
                dv.tensor_tensor(mod[:, tile:tile + ADA_G, :], mod[:, tile:tile + ADA_G, :], bias, ALU.add)
                dv.drain()
                g = par[:, PCOL[post_g]:PCOL[post_g] + DC, None].broadcast_to([P, DC, 2])
                dv.tensor_tensor(mod_g[:, :, :], mod[:, tile:tile + ADA_G, :], g, ALU.mult)
                dv.drain()

            def update_x(L, phase, n_inv):
                rms(L, phase, 1, 0, D_MODEL, diag)
                dv.wait_ge(inv_ready, n_inv)
                for c in range(DC + 1):
                    if c < DC:
                        for c0, m, g in REGIONS:
                            dv.scalar_tensor_tensor(out=yb[:, c, c0:c0 + m], in0=yb[:, c, c0:c0 + m], scalar=mod_g[:, c, g:g + 1],
                                                    in1=inv_rms[:, c0:c0 + m], op0=ALU.mult, op1=ALU.mult)
                    if 1 <= c <= DC:
                        for c0, m, g in REGIONS:
                            last = dv.tensor_tensor(x[:, c - 1, c0:c0 + m], x[:, c - 1, c0:c0 + m], yb[:, c - 1, c0:c0 + m], ALU.add)
                        last.then_inc(x_new, 1)
                    dv.drain()

            def next_h(L, phase, n, n_inv, n_mod, tile, ada_tile, pre_g):
                if phase == "head":
                    dv.wait_ge(par_loaded, (L + 1) * 32)
                    dv.tensor_scalar(half_gate[:, :], par[:, PCOL["b_gate"]:PCOL["b_gate"] + 4 * DC], 0.5, None, ALU.mult)
                dv.wait_ge(mod_ready, n_mod)
                m = mod[:, tile:tile + ADA_MIX, :]
                bias = par[:, PCOL["ada_b"] + ada_tile:PCOL["ada_b"] + ada_tile + ADA_MIX, None].broadcast_to([P, ADA_MIX, 2])
                dv.tensor_tensor(m, m, bias, ALU.add)
                dv.drain()
                g = par[:, PCOL[pre_g]:PCOL[pre_g] + DC, None].broadcast_to([P, DC, 2])
                dv.scalar_tensor_tensor(out=mod_a[:, :, :], in0=mod[:, tile + DC:tile + 2 * DC, :], scalar=1.0, in1=g, op0=ALU.add, op1=ALU.mult)
                dv.tensor_copy(mod_b[:, :, :], mod[:, tile:tile + DC, :])
                dv.drain()
                full(L, phase, 3, 0)
                dv.sem_inc(sq_used, 1)
                rms(L, phase, 3, 0, D_MODEL, diag)
                dv.wait_ge(inv_ready, n_inv)
                for c in range(DC + 1):
                    if c < DC:
                        for c0, m, g in REGIONS:
                            last = dv.scalar_tensor_tensor(out=hx[:, c % 2, c0:c0 + m], in0=x[:, c, c0:c0 + m], scalar=mod_a[:, c, g:g + 1],
                                                           in1=inv_rms[:, c0:c0 + m], op0=ALU.mult, op1=ALU.mult)
                        last.then_inc(t_ready, 1)
                    if c >= 1:
                        dv.wait_ge(hi_ready, n * DC + c)
                        for c0, m, g in REGIONS:
                            last = dv.scalar_tensor_tensor(out=h_lo[:, c - 1, c0:c0 + m], in0=hx[:, (c - 1) % 2, c0:c0 + m],
                                                           scalar=mod_b[:, c - 1, g:g + 1], in1=h_hi[:, c - 1, c0:c0 + m],
                                                           op0=ALU.add, op1=ALU.subtract)
                        last.then_inc(h_ready, 1)
                    dv.drain()

            def block_src(s, b):
                return ps[:, 2 * s + b // 2, (b % 2) * 256:(b % 2) * 256 + 256]

            def statistics(src):
                for b in range(NBLK):
                    dv.bn_stats(bn[:, b, :], src(b))
                dv.drain()

            def moments():
                for b in range(NBLK):
                    dv.bn_aggr(mean_var[:, b, :], bn[:, b, :])
                dv.drain()
                inverse_root(mean_var[:, :, 1], 1.0)

            def standardise(dst, src):
                for b in range(NBLK):
                    dv.tensor_scalar(dst[:, b, :], src(b), mean_var[:, b, 0:1], rstd[:, b:b + 1], ALU.subtract, ALU.mult)
                dv.drain()

            def rotate(dst, pe_rows, swapped_rows):
                dv.scalar_tensor_tensor(out=hx[64:96, 0, 0:DEC_SEQ], in0=pe_rows, scalar=1.0, in1=rope[64:96, :], op0=ALU.mult, op1=ALU.mult)
                dv.scalar_tensor_tensor(out=hx[64:96, 1, 0:DEC_SEQ], in0=swapped_rows, scalar=1.0, in1=rope[96:P, :], op0=ALU.mult, op1=ALU.mult)
                dv.drain()
                return dv.tensor_tensor(dst, hx[64:96, 0, 0:DEC_SEQ], hx[64:96, 1, 0:DEC_SEQ], ALU.add)

            dv.sem_inc(sq_used, 1)
            dv.sem_inc(attn_ready, 1)
            dv.sem_inc(merge_sum, 1)
            dv.sem_inc(up_conv, 2)
            for c in (SEQ, TOK - 2):
                dv.memset(h_hi[:, :, c:c + 2].bitcast(F32), 0.0)
                dv.memset(h_lo[:, :, c:c + 2].bitcast(F32), 0.0)
            dv.wait_ge(cond_tanh, 1)
            dv.tensor_scalar(cond_t[:, :, :], cond_t[:, :, :], 0.5, 0.5, ALU.mult, ALU.add)
            dv.drain()
            dv.tensor_tensor(cond[:, :, :], cond[:, :, :], cond_t[:, :, :], ALU.mult).then_inc(cond_ready, 1)
            dv.drain()
            for i in range(ADA_LOADS):
                dv.wait_ge(ada_pre_loaded[i], 16)
                sum_tiles([(ada_pre[:, t, :], ada_pre_part[:, t // 2, :, :]) for t in pre_tiles(i)[1]], ada_pre_summed)
            dv.wait_ge(x_loaded, 16 * DC)
            dv.sem_inc(x_new, DC)

            with dv.Fori(0, DEPTH) as L:
                next_h(L, "head", L * 2, L * NINV + 1, mods(L, 0), MOD_MIX, 0, "pre_mix_g")

                dv.memset(sq_sum[:, :], 0.0)
                dv.memset(sq_sum_kv[:, :], 0.0)
                dv.memset(pool_x[:, :], 0.0)
                dv.drain()
                dv.sem_inc(pool_x_free, 1)
                for c in range(QC):
                    add_square(sq_sum, c % 2, L, SQ_P1 + c)
                dv.sem_inc(sum_ready, 1)
                for c in range(KVC):
                    add_square(sq_sum_kv, (QC + c) % 2, L, SQ_P1 + QC + c)
                dv.sem_inc(sum_ready, 1)
                dv.wait_ge(p1_copied, L * 10 + 6)
                rotate(k_t[64:96, 0, 0:DEC_SEQ], kpe_raw[64:96, SAMPLE0:SAMPLE0 + DEC_SEQ], kpe_raw[96:P, SAMPLE0:SAMPLE0 + DEC_SEQ])
                for hd in range(2):
                    dv.tensor_copy(k_t[64:96, hd, KEYS:NKEY], kpe_raw[64:96, 0:SEQ])
                dv.drain()
                dv.tensor_copy(k_t[64:96, 1, 0:DEC_SEQ], k_t[64:96, 0, 0:DEC_SEQ])
                rms(L, "p1", 0, 2, Q_LORA, diag)
                dv.drain()
                rms(L, "p1", 1, 2, KV_LORA, diag_kv)
                full(L, "p1", 0, 3)
                for c in range(QC):
                    for c0, m, g in REGIONS:
                        dv.scalar_tensor_tensor(out=qa[:, c, c0:c0 + m], in0=qa[:, c, c0:c0 + m], scalar=par[:, PCOL["q_norm_g"] + c:PCOL["q_norm_g"] + c + 1],
                                                in1=region(0, g), op0=ALU.mult, op1=ALU.mult)
                dv.drain()
                dv.sem_inc(set_empty[0], 1)
                full(L, "p1", 1, 3)
                for c in range(KVC):
                    for c0, m, g in REGIONS:
                        to = 0 if g else KEYS
                        dv.scalar_tensor_tensor(out=ckv[:, c, to:to + m], in0=kv_raw[:, c, c0:c0 + m], scalar=par[:, PCOL["kv_norm_g"] + c:PCOL["kv_norm_g"] + c + 1],
                                                in1=region(1, g), op0=ALU.mult, op1=ALU.mult)
                dv.drain()
                dv.sem_inc(set_empty[1], 1)
                dv.sem_inc(qkv_ready, 1)

                dv.wait_ge(halo_zero, L + 1)

                def gated_input(c):
                    dv.wait_ge(p1_copied, L * 10 + (7 + 2 * c))
                    dv.tensor_scalar(br[:, 2 + c, :], br[:, 2 + c, :], 0.5, 0.5, ALU.mult, ALU.add)
                    dv.drain()
                    for c0, m, g in REGIONS:
                        to = HALO + (SEQ + HALO) * g
                        last = dv.tensor_tensor(conv_x[:, c, to:to + m], br[:, 2 + c, c0:c0 + m], br[:, 4 + c, c0:c0 + m], ALU.mult)
                    last.then_inc(conv_in, 1)

                def pool(c):
                    dv.wait_ge(p1_copied, L * 10 + (8 + 2 * c))
                    n = PPAD
                    dv.tensor_tensor(sum_a[:, 1:n], pool_x[:, 0:n - 1], pool_x[:, 1:n], ALU.add)
                    dv.drain()
                    dv.tensor_tensor(sum_b[:, 2:n - 1], sum_a[:, 1:n - 2], sum_a[:, 3:n], ALU.add)
                    dv.drain()
                    if c == 1:
                        dv.tensor_tensor(sum_a[:, 4:n - 3], sum_b[:, 2:n - 5], sum_b[:, 6:n - 1], ALU.add)
                        dv.drain()
                        dv.tensor_tensor(sum_b[:, 8:n - 7], sum_a[:, 4:n - 11], sum_a[:, 12:n - 3], ALU.add)
                        dv.drain()
                    dv.tensor_copy(sum_a[64:P, 8:n - 8], sum_b[64:P, 8:n - 8])
                    dv.drain()
                    for g, m in enumerate((SEQ, DEC_SEQ)):
                        p0 = EDGE + (SEQ + EDGE) * g
                        for side in range(2):
                            at = p0 + side * (m - EDGE)
                            dv.tensor_tensor(sum_a[:, at:at + EDGE], sum_a[:, at:at + EDGE], edge[:, c, side, :], ALU.mult)
                    dv.drain()
                    for c0, m, g in REGIONS:
                        p0 = EDGE + (SEQ + EDGE) * g
                        dv.scalar_tensor_tensor(out=br[:, 8 + c, c0:c0 + m], in0=sum_a[:, p0:p0 + m], scalar=inv_window[:, c:c + 1],
                                                in1=pool_x[:, p0:p0 + m], op0=ALU.mult, op1=ALU.subtract)
                        dv.memset(br[:, 8 + c, c0 + m:c0 + m + 2], 0.0)
                    dv.drain()
                    dv.sem_inc(pool_ready, 1)
                    dv.sem_inc(pool_x_free, 1)

                gated_input(0)
                def v_src(b):
                    return block_src(0, b) if b < 4 else block_src(1, 0)

                full(L, "p1", 0, 4)
                full(L, "p1", 1, 4)
                statistics(v_src)
                moments()
                standardise(tok_major, v_src)
                dv.sem_inc(set_empty[0], 1)
                dv.sem_inc(set_empty[1], 1)
                for i, op in enumerate((ALU.mult, ALU.add)):
                    t = tables[:, None, i * GMLP_W:(i + 1) * GMLP_W].broadcast_to([P, NBLK, GMLP_W])
                    dv.tensor_tensor(tok_major[:, :, :], tok_major[:, :, :], t, op)
                    dv.drain()
                dv.sem_inc(gmlp_norm, 1)
                pool(0)
                for c in range(2):
                    full(L, "p1", c, 5)
                    t = tables[:, 512 + c * P:512 + (c + 1) * P]
                    dv.tensor_tensor(hx[:, c, 0:SEQ], region(c, 0), t, ALU.add)
                    dv.tensor_tensor(hx[:, c, SAMPLE0:SAMPLE0 + DEC_SEQ].rearrange("p (a b) -> p a b", a=4),
                                     region(c, 1).rearrange("p (a b) -> p a b", a=4), t[:, None, :].broadcast_to([P, 4, P]), ALU.add)
                    dv.drain()
                    dv.sem_inc(set_empty[c], 1)
                    for c0, m, g in REGIONS:
                        dv.tensor_tensor(br[:, 6 + c, c0:c0 + m], br[:, 6 + c, c0:c0 + m], hx[:, c, c0:c0 + m], ALU.mult)
                gated_input(1)
                dv.drain()
                tap1 = PCOL["conv_dw"] + CONV_K
                dv.tensor_scalar(conv_acc[:, 1, 0:CLEN], conv_x[:, 1, 0:CLEN], par[:, tap1:tap1 + 1],
                                 par[:, PCOL["conv_dw_b"] + 1:PCOL["conv_dw_b"] + 2], ALU.mult, ALU.add)
                pool(1)
                for c in (SEQ, TOK - 2):
                    dv.memset(br[:, 0:4, c:c + 2], 0.0)
                dv.drain()

                def expand(p, use, k):
                    n = L * N_PAIRS + p
                    for hd in range(2):
                        dv.wait_ge(q_part, n * 2 + (hd + 1))
                        sample = slice(SAMPLE0, SAMPLE0 + DEC_SEQ)
                        rotate(q_rot[64:96, hd, :], q_raw[64:96, hd, sample], q_raw[96:P, hd, sample])
                        dv.drain()
                        dv.sem_inc(q_ready, 1)
                    dv.wait_ge(set_full[0], use(0, k + 1) + 1)
                    dv.tensor_copy(k_t[0:QK_NOPE, 1, :], line(0, NKEY, 64, P)).then_inc(k2_ready, 1)
                    dv.wait_ge(k2_ready, n + 1)
                    dv.wait_ge(k_ready, n + 1)
                    dv.sem_inc(set_empty[0], 1)

                def max_item(p, i, use):
                    s, keys = i % 2, KEYS if i % 5 < 4 else SEQ
                    dv.wait_ge(set_full[s], use(s, i // 2) + 1)
                    dv.tensor_reduce(neg_max[:, s:s + 1], line(s, keys), AX.X, ALU.max, negate=True).then_inc(max_ready, 1)

                def normalise_item(p, i):
                    s, keys = i % 2, KEYS if i % 5 < 4 else SEQ
                    dv.wait_ge(exp_ready, (L * N_PAIRS + p) * 10 + (i + 1))
                    dv.reciprocal(inv_sum[:, s:s + 1], exp_sum[:, s:s + 1])
                    dv.drain()
                    dv.tensor_scalar(probs[:, s, 0:keys], probs[:, s, 0:keys], inv_sum[:, s:s + 1], None, ALU.mult).then_inc(probs_ready, 1)

                def head_out(p, hd, use):
                    dv.wait_ge(set_full[3], use(3, hd) + 1)
                    rows = slice(64 * hd, 64 * hd + 64)
                    for c0, m, g in REGIONS:
                        dst = br[rows, p, c0:c0 + m] if isinstance(p, int) else br[rows, bass.ds(p, 1), c0:c0 + m].rearrange("p a b -> p (a b)")
                        dv.tensor_copy(dst, region(3, g, 0, V_HEAD))
                    dv.drain()
                    dv.sem_inc(set_empty[3], 1)
                    dv.sem_inc(attn_ready, 1)

                def tap(k):
                    dv.scalar_tensor_tensor(out=conv_acc[:, 1, 0:CLEN], in0=conv_x[:, 1, bass.ds(k, CLEN)],
                                            scalar=par[:, bass.ds(k + tap1, 1)], in1=conv_acc[:, 1, 0:CLEN], op0=ALU.mult, op1=ALU.add)

                def pair(p, use, expand_next, between=None):
                    max_item(p, 0, use)
                    for i in range(10):
                        if i + 1 < 10:
                            max_item(p, i + 1, use)
                        normalise_item(p, i)
                        if expand_next:
                            tap(p * 10 + (i + 1))
                        if between is not None:
                            between(i)
                        if i == 6:
                            head_out(p, 0, use)
                    if expand_next:
                        expand(p + 1, use, 5)
                    head_out(p, 1, use)

                expand(0, lambda s, k: set_use(L, "expand", s, k), 0)
                with dv.Fori(0, N_PAIRS - 1) as p:
                    pair(p, lambda s, k: set_use(L, "pair", s, k) + p * PAIR_USES[s], True)
                assert (N_PAIRS - 1) * 10 + 1 == CONV_K
                dv.drain()
                dv.sem_inc(conv1_done, 1)

                def conv_src(b):
                    return block_src(3, b) if b < NBLK - 1 else conv_tok[:, b, :]

                def conv_layernorm(i):
                    if i == 0:
                        full(L, "ln", 3, 1)
                        statistics(conv_src)
                    elif i == 1:
                        moments()
                    elif i == 2:
                        standardise(conv_tok, conv_src)
                        dv.sem_inc(set_empty[3], 1)
                        dv.sem_inc(conv_norm, 1)

                full(L, "ln", 3, 0)
                dv.tensor_copy(conv_tok[:, NBLK - 1, :], block_src(3, 0))
                dv.drain()
                dv.sem_inc(set_empty[3], 1)
                pair(N_PAIRS - 1, lambda s, k: set_use(L, "lastpair", s, k), False, conv_layernorm)

                for n, c in enumerate(SPLIT_ORDER):
                    if n == BRANCH_SPLIT[2]:
                        ada(0, ada_use(L, 0, 1), 0)
                        for b in range(2):
                            dv.wait_ge(conv_pre, L * 2 + (b + 1))
                            for c0, m, g in REGIONS:
                                dv.tensor_scalar(hx[:, b, c0:c0 + m], hx[:, b, c0:c0 + m], 0.5, 0.5, ALU.mult, ALU.add)
                            dv.drain()
                            for c0, m, g in REGIONS:
                                last = dv.tensor_tensor(br[:, 4 + b, c0:c0 + m], br[:, 4 + b, c0:c0 + m], hx[:, b, c0:c0 + m], ALU.mult)
                            last.then_inc(conv_silu, 1)
                        dv.drain()
                    dv.wait_ge(br_part, L * 10 + (n + 1))
                    dv.tensor_tensor(br_lo[:, c, :], br[:, c, :], br_hi[:, c, :], ALU.subtract).then_inc(br_ready, 1)

                def merge_step(d, last_step=False):
                    for b, (s, k) in enumerate((s, k) for s, k, branch in MERGE_PLAN if branch is not None):
                        if b == 1:
                            ada(1, ada_use(L, 1, 1) + d, 1)
                        elif b == 2:
                            ada(0, ada_use(L, 0, 2) + d * 2, 2)
                        dv.wait_ge(set_full[s], set_use(L, "merge", s, k + 1) + d * 2)
                        dv.sem_inc(w_used[BRANCH_LAST_SLOT[b]], 1)
                        dv.wait_ge(gate_ready, (L * DC + d) * 4 + (b + 1))
                        dst = macc if b == 0 else mtmp
                        dv.scalar_tensor_tensor(out=two(dst[:, :]), in0=two(gate_t[:, b, :]), scalar=1.0, in1=halves(s),
                                                op0=ALU.add, op1=ALU.mult).then_inc(set_empty[s], 1)
                        dv.drain()
                        if b:
                            last = dv.tensor_tensor(macc[:, :], macc[:, :], mtmp[:, :], ALU.add)
                            if b == 3:
                                last.then_inc(merge_sum, 1)
                            dv.drain()
                    dv.wait_ge(mg_part, L * DC + d + 1)
                    dv.scalar_tensor_tensor(out=chunk(mg_lo, d), in0=macc[:, :], scalar=0.5, in1=chunk(mg_hi, d),
                                            op0=ALU.mult, op1=ALU.subtract).then_inc(mg_ready, 1)
                    dv.drain()
                    if not last_step:
                        ada(0, ada_use(L, 0, 3) + d * 2, 0)

                with dv.Fori(0, DC - 1) as d:
                    merge_step(d)
                merge_step(DC - 1, last_step=True)

                dv.memset(sq_sum[:, :], 0.0)
                dv.drain()
                for i in range(2):
                    for j in range(4):
                        add_square(sq_sum, j % 2, L, SQ_OUT + 4 * i + j)
                    if i == 0:
                        both_slots(lambda slot: ada_use(L, slot, (2 * DC, DC)[slot] + 1))
                dv.sem_inc(sum_ready, 1)

                dv.wait_ge(mod_ready, mods(L, ADA))
                output_gain(MOD_MIX_G, ADA_MIX, "post_mix_g")
                update_x(L, "gap2", L * NINV + 2)
                next_h(L, "gap2", L * 2 + 1, L * NINV + 3, mods(L, ADA), MOD_FFN, ADA, "pre_ffn_g")

                for j in range(4):
                    dv.memset(up_x[:, j, 0:2], 0.0)
                    dv.memset(up_x[:, j, 2 + TOK:4 + TOK], 0.0)
                dv.drain()
                def up_step(i, last_step=False):
                    if not (isinstance(i, int) and i == 0):
                        both_slots(lambda slot: ada_use(L, slot, (2 * DC, DC)[slot] + 1) + i)
                    for q in range(2):
                        def col(name, v, tap=0):
                            at = PCOL[name] + tap * 2 * FFC + 2 * q + v
                            return par[:, i * 4 + at:i * 4 + at + 1] if isinstance(i, int) else par[:, bass.ds(i * 4 + at, 1)]
                        if last_step and q == 1:
                            lo_part(0, 0)
                            lo_part(1, 1)
                        dv.wait_ge(up_copied, L * (2 * FFC) + (2 * q + 2) + i * 4)
                        for v in range(2):
                            j = 2 * q + v
                            dv.tensor_scalar(up_y[:, j, :], up_x[:, j, 2:2 + TOK], col("ffn_dw", v, 1), col("ffn_dw_b", v), ALU.mult, ALU.add)
                        for tap in (0, 2):
                            dv.drain()
                            for v in range(2):
                                j = 2 * q + v
                                last = dv.scalar_tensor_tensor(out=up_y[:, j, :], in0=up_x[:, j, 1 + tap:1 + tap + TOK], scalar=col("ffn_dw", v, tap),
                                                               in1=up_y[:, j, :], op0=ALU.mult, op1=ALU.add)
                        last.then_inc(up_conv, 1)
                        dv.drain()
                        if last_step and q == 1:
                            lo_part(2, 2)
                        dv.wait_ge(up_tanh, L * FFC + (q + 1) + i * 2)
                        dv.scalar_tensor_tensor(out=up_t[:, q, :], in0=up_t[:, q, :], scalar=1.0, in1=up_y[:, 2 * q, :], op0=ALU.add, op1=ALU.mult)
                        dv.drain()
                        dst = act[:, 2 * i + q, :] if isinstance(i, int) else chunk(act, i * 2 + q)
                        dv.scalar_tensor_tensor(out=dst, in0=up_t[:, q, :], scalar=0.5, in1=up_y[:, 2 * q + 1, :],
                                                op0=ALU.mult, op1=ALU.mult).then_inc(act_ready, 1)

                def lo_part(n, k, i=0):
                    dv.wait_ge(a_part, L * 2 * FFC + (n + 1) + i * SLOTS)
                    src = act[:, k, :] if isinstance(k, int) else chunk(act, k)
                    dv.tensor_tensor(a_lo[:, n % 2, :], src, a_hi[:, n % 2, :], ALU.subtract).then_inc(a_ready, 1)

                up_step(0)
                with dv.Fori(1, FFC // 2 - 1) as i:
                    up_step(i)
                up_step(FFC // 2 - 1, last_step=True)

                for q in range(2):
                    n0 = q * FFC
                    if q == 1:
                        lo_part(n0, 0)
                        for s in range(4):
                            add_square(sq_sum, s % 2, L, SQ_DOWN + s)
                        lo_part(n0 + 1, 1)
                    steps = (FFC - 2) // SLOTS
                    for k in range(2 if q else 3, 2 + SLOTS):
                        lo_part(n0 + k, k)
                    with dv.Fori(1, steps - 1) as i:
                        for k in range(2, 2 + SLOTS):
                            lo_part(n0 + k, i * SLOTS + k, i)
                    if q == 0:
                        dv.memset(sq_sum[:, :], 0.0)
                        dv.drain()

                        dv.wait_ge(mod_ready, mods(L, 2 * ADA - 2))
                        output_gain(MOD_FFN_G, 2 * ADA - ADA_G, "post_ffn_g")
                    for n in range(SLOTS):
                        if q == 0:
                            slot, half = n // 2, n % 2
                            ada(slot, ada_use(L, slot, ADA_LAYER[slot]), slot, (half * DC // 2, (half + 1) * DC // 2))
                        lo_part(n0 + FFC - SLOTS + n, FFC - SLOTS + n)
                for s in range(4):
                    add_square(sq_sum, s % 2, L, SQ_DOWN + 4 + s)
                dv.sem_inc(sum_ready, 1)

                update_x(L, "tail", L * NINV + 4)


def _tiles(w, cols):
    n_l, k, _ = w.shape
    t = np.stack([w[:, :, c:c + P] for c in cols], 1)
    return t.reshape(n_l, len(cols), k // P, P, P).transpose(0, 1, 3, 2, 4)


def _blocks(t):
    n_l, n, _, k, _ = t.shape
    return t.reshape(n_l, n, P, k // TILES, WBLK).transpose(0, 1, 3, 2, 4).reshape(n_l, -1, P, WBLK)


def _first_group(b, first):
    n_l = b.shape[0]
    g = b[:, first:first + 8].reshape(n_l, 4, 2, P, TILES, P).transpose(0, 2, 4, 3, 1, 5).reshape(n_l, 8, P, WBLK)
    return np.concatenate([b[:, :first], g, b[:, first + 8:]], 1)


def _columns(v):
    return v.reshape(v.shape[0], -1, P).transpose(0, 2, 1)


_SWAP = np.concatenate([np.arange(8, 16), np.arange(0, 8), np.arange(24, 32), np.arange(16, 24)])


def _const():
    c = np.zeros((P, N_CONST), np.float32)
    c[:, 0:P] = np.eye(P)
    c[:, P:2 * P] = 1.0
    t = np.arange(DEC_SEQ)
    half = QK_ROPE // 4
    inv = (np.float32(ROPE_BASE) ** (-np.arange(half, dtype=np.float32) / np.float32(half))).astype(np.float32)
    for i in range(QK_ROPE):
        pos = (t // GRID_W if i < QK_ROPE // 2 else t % GRID_W).astype(np.float32)
        ang = pos * inv[i % half]
        c[64 + i, 2 * P:2 * P + DEC_SEQ] = np.cos(ang)
        c[96 + i, 2 * P:2 * P + DEC_SEQ] = np.sin(ang) * (-1.0 if (i // half) % 2 == 0 else 1.0)
    for p in range(P):
        for k in range(2):
            w = POOL_WINDOWS[2 * k + p // 64]
            lo, hi = w // 2, w - w // 2 - 1
            for e in range(EDGE):
                base = 2 * P + DEC_SEQ + 2 * k * EDGE
                c[p, base + e] = w / (min(e, lo) + hi + 1)
                c[p, base + EDGE + e] = w / (lo + min(EDGE - 1 - e, hi) + 1)
            c[p, 2 * P + DEC_SEQ + 4 * EDGE + k] = 1.0 / w
    return c


def kernel(**inputs):
    import concourse.bacc as _bacc
    from concourse import mybir as _mybir
    from concourse.bass_utils import run_bass_kernel_spmd as _run

    a = {k: np.asarray(v) for k, v in inputs.items()}
    f = np.float32
    ld = DEPTH
    x_in = np.zeros((DC, P, TOK), f)
    x_in[:, :, 0:SEQ] = a["x_prompt"][0].T.reshape(DC, P, SEQ)
    x_in[:, :, SAMPLE0:SAMPLE0 + DEC_SEQ] = a["x_sample"][0].T.reshape(DC, P, DEC_SEQ)
    cond_in = np.stack([a["c_ctx"].reshape(DC, P).T, a["c"][0].reshape(DC, P).T], 2)

    w_in = a["w_in"]
    kpe = w_in[:, :, OFF_KPE:OFF_CONV]
    zeros = np.zeros((ld, D_MODEL, 64), f)
    kpe_tile = np.concatenate([zeros, kpe, kpe[:, :, _SWAP]], 2)
    def t(*cols):
        return _tiles(w_in, cols)
    v0, u0, x1, x2, pl = OFF_GMLP + GMLP_W, OFF_GMLP, OFF_CONV, OFF_CONV + CONV_W, OFF_POOL
    p1 = np.concatenate([t(0, P, 2 * P, OFF_KV, OFF_KV + P), _tiles(kpe_tile, [0]), t(v0, v0 + P, u0, u0 + P),
                         t(x2, x1, pl, x2 + P, x1 + P, pl + P)], 1)
    ada = _tiles(a["ada_w"], range(0, 6 * D_MODEL, P))
    up = _tiles(a["ffn_up"], [o + c * P for c in range(FFC) for o in (0, D_FF)])
    down = a["ffn_down"].reshape(ld, FFC, P, 2, 4 * P).transpose(0, 3, 1, 2, 4).reshape(ld, 2 * FFC, P, WBLK)
    w_lin = np.concatenate([_first_group(_blocks(p1), 0), _first_group(_blocks(_tiles(a["w_out"], range(0, D_MODEL, P))), 0),
                            _first_group(_blocks(up), 0), down], 1).reshape(ld * LIN_BLOCKS, P, WBLK)
    ada = ada.reshape(ld, 2 * ADA, P, D_MODEL)
    parts = [ada[0, :ADA_MIX]]
    for n in range(ld):
        after = ada[n + 1, :ADA_MIX] if n + 1 < ld else np.zeros_like(ada[0, :ADA_MIX])
        late = np.concatenate([after, ada[n, 2 * ADA - ADA_G:]], 0)
        parts += [ada[n, ADA:ADA + ADA_MIX], ada[n, ADA_MIX:ADA], late[[FFC, FFC + 1] + list(range(2, FFC)) + [0, 1]]]
    w_ada = np.concatenate(parts, 0)
    gates = [_tiles(w_in, [OFF_GATE + b * D_MODEL + d * P for d in range(DC)]) for b in range(4)]
    outs = [_tiles(a[n], range(0, D_MODEL, P)) for n in ("w_o_mla", "w_conv_out", "w_gmlp_out", "w_pool_out")]
    w_merge = np.concatenate([w for b in BRANCHES for w in (gates[b], outs[b])], 3)
    w_merge = w_merge.reshape(ld * DC, P, MERGE_TILES * P)
    wq = a["w_q_b"].reshape(ld, QC, P, HEADS, QK)
    wq = np.concatenate([wq, wq[..., QK_NOPE:][..., _SWAP]], 4).transpose(0, 3, 2, 1, 4)
    wq = wq.reshape(ld, N_PAIRS, 2, P, QC * P).transpose(0, 1, 3, 2, 4).reshape(ld, N_PAIRS, P, 2 * QC * P)
    wkv = a["w_kv_b"].reshape(ld, KVC, P, N_PAIRS, 2, 2, 64).transpose(0, 3, 2, 5, 1, 4, 6)
    w_pair = np.concatenate([wq, wkv.reshape(ld, N_PAIRS, P, 4 * P)], 3).reshape(ld * N_PAIRS, P, 10 * P)

    def taps(w, order):
        return w.reshape(ld, w.shape[1], -1, P).transpose(order).reshape(ld, P, -1)

    def interleaved(v):
        return v.reshape(ld, v.shape[1], 2, FFC, P).transpose(0, 4, 1, 3, 2).reshape(ld, P, -1)

    parts = {n: _columns(a[n]) for n in ("pre_mix_g", "post_mix_g", "pre_ffn_g", "post_ffn_g", "q_norm_g", "kv_norm_g", "b_gate",
                                         "conv_dw_b", "conv_ln_g", "conv_ln_b", "pool_scale", "ada_b")}
    parts["conv_dw"] = taps(a["conv_dw"], (0, 3, 2, 1))
    parts["ffn_dw"] = interleaved(a["ffn_dw"])
    parts["ffn_dw_b"] = interleaved(a["ffn_dw_b"][:, None, :])
    params_in = np.concatenate([parts[n] for n, _ in PARAMS], 2)

    rows = np.broadcast_to(np.concatenate([a["gmlp_ln_g"], a["gmlp_ln_b"]], 1)[:, None, :], (ld, P, 2 * GMLP_W))
    bs = np.repeat(a["gmlp_bs"], 64, axis=1).reshape(ld, 2, P, P).transpose(0, 2, 1, 3).reshape(ld, P, 2 * P)
    pool_w = np.zeros((ld, P, 2, P), f)
    for g in range(4):
        o = 64 * (g % 2)
        pool_w[:, o:o + 64, g // 2, o:o + 64] = a["pool_w"][:, g]
    ws = a["gmlp_ws"].transpose(0, 3, 1, 2).reshape(ld, P, 4 * P)
    tables_in = np.concatenate([rows, bs, pool_w.reshape(ld, P, 2 * P), ws], 2)
    ctx_ckv = a["cache_ckv"][0].reshape(ld, PAST, KVC, P).transpose(0, 3, 2, 1)
    ctx_kpe = a["cache_kpe"][0].transpose(0, 2, 1)

    nc = _bacc.Bacc("TRN2", target_bir_lowering=False, num_devices=1)
    arrays, args = {}, []
    for name, v in (("x", x_in), ("cond", cond_in), ("w_ada", w_ada), ("w_lin", w_lin), ("w_merge", w_merge), ("w_pair", w_pair), ("params", params_in),
                    ("tables", tables_in), ("ctx_ckv", ctx_ckv), ("ctx_kpe", ctx_kpe), ("const", _const())):
        v = np.ascontiguousarray(v)
        arrays[f"in_{name}_dram"] = v
        args.append(nc.dram_tensor(f"in_{name}_dram", v.shape, _mybir.dt.from_np(v.dtype), kind="ExternalInput").ap())
    for name, shape in (("y", (DC, P, TOK)), ("ckv", (ld, P, KVC, SEQ)), ("kpe", (ld, QK_ROPE, SEQ))):
        args.append(nc.dram_tensor(f"out_{name}_dram", shape, F32, kind="ExternalOutput").ap())
    trunk_kernel(nc, *args)
    r = _run(nc, [arrays], core_ids=[0]).results[0]
    y = r["out_y_dram"].reshape(D_MODEL, TOK)
    y_prompt = np.ascontiguousarray(y[:, 0:SEQ].T)[None]
    y_sample = np.ascontiguousarray(y[:, SAMPLE0:SAMPLE0 + DEC_SEQ].T)[None]
    new_ckv = np.ascontiguousarray(r["out_ckv_dram"].transpose(0, 3, 2, 1).reshape(ld, SEQ, KV_LORA))[None]
    new_kpe = np.ascontiguousarray(r["out_kpe_dram"].transpose(0, 2, 1))[None]
    return y_prompt, y_sample, new_ckv, new_kpe
```
